# Optimizing a Trainium2 kernel written in Bass

```python
import math
import numpy as np
import jax, jax.numpy as jnp
from jax import lax

D_MODEL = 1024
BATCH = 1
SEQ = 256
DEPTH = 1

HEAD_DIM = 64
ROT_DIM = HEAD_DIM // 4
ROPE_THETA = 500000.0
NORM_EPS = 1e-6
NEG_INF = -1e30
BIG = 1e30

A_HEADS = 8
A_BLOCK = 256
A_TOPK = 3
A_QBLOCK = 64

B_HEADS = 8
B_KV_HEADS = 2
B_GROUP = B_HEADS // B_KV_HEADS
CMP_LEN = 32
CMP_STRIDE = 16
CMP_HIDDEN = 256
SLC_BLOCK = 64
SLC_TOPN = 16
WINDOW = 512
B_QBLOCK = 64

PEER_HEADS = 8
PEER_NKEYS = 128
PEER_N = PEER_NKEYS * PEER_NKEYS
PEER_QDIM = 256
PEER_HALF = PEER_QDIM // 2
PEER_TOPK = 16
PEER_CHUNK = 128

A_WIDTH = A_HEADS * HEAD_DIM
B_WIDTH = B_HEADS * HEAD_DIM
B_KV_WIDTH = B_KV_HEADS * HEAD_DIM
N_BRANCH = 2
IN_COLS = 3 * A_WIDTH + B_WIDTH + 6 * B_KV_WIDTH + 3 * B_HEADS + N_BRANCH * D_MODEL


def rmsnorm(x, g):
    xf = x.astype(jnp.float32)
    y = xf * lax.rsqrt(jnp.mean(xf * xf, axis=-1, keepdims=True) + NORM_EPS)
    return (y * g.astype(jnp.float32)).astype(x.dtype)

def rope_tables(S):
    inv = ROPE_THETA ** (-jnp.arange(0, ROT_DIM, 2, dtype=jnp.float32) / ROT_DIM)
    ang = jnp.arange(S, dtype=jnp.float32)[:, None] * inv[None, :]
    return jnp.cos(ang), jnp.sin(ang)

def partial_rope(x, cos, sin):
    c = cos[None, :, None, :].astype(x.dtype)
    s = sin[None, :, None, :].astype(x.dtype)
    x1 = x[..., :ROT_DIM // 2]
    x2 = x[..., ROT_DIM // 2:ROT_DIM]
    return jnp.concatenate([x1 * c - x2 * s, x2 * c + x1 * s, x[..., ROT_DIM:]], axis=-1)

def masked_softmax(s, mask):
    p = jax.nn.softmax(jnp.where(mask, s.astype(jnp.float32), NEG_INF), axis=-1)
    return p * jnp.any(mask, axis=-1, keepdims=True)

def split_columns(t):
    sizes = (A_WIDTH, A_WIDTH, A_WIDTH, B_WIDTH, B_KV_WIDTH, B_KV_WIDTH, B_KV_WIDTH,
             B_KV_WIDTH, B_KV_WIDTH, B_KV_WIDTH, 3 * B_HEADS, N_BRANCH * D_MODEL)
    points, acc = [], 0
    for s in sizes[:-1]:
        acc += s
        points.append(acc)
    return jnp.split(t, points, axis=-1)

def moba_attention(q, k, v):
    B, S, H, D = q.shape
    n_blk = -(-S // A_BLOCK)
    pad = n_blk * A_BLOCK - S
    topk = min(A_TOPK, n_blk)
    nc = S // A_QBLOCK
    Q = A_QBLOCK
    L = A_BLOCK
    scale = HEAD_DIM ** -0.5

    def to_blocks(t):
        t = jnp.pad(t, ((0, 0), (0, pad), (0, 0), (0, 0)))
        return t.reshape(B, n_blk, L, H, D).transpose(0, 3, 1, 2, 4)

    kb, vb = to_blocks(k), to_blocks(v)
    qh = q.transpose(0, 2, 1, 3)
    k_mean = jnp.mean(kb.astype(jnp.float32), axis=3)
    gate = jnp.einsum('bhsd,bhnd->bhsn', qh.astype(jnp.float32), k_mean)
    own = jnp.arange(S) // A_BLOCK
    past = jnp.arange(n_blk)[None, :] < own[:, None]
    gate = jnp.where(past, gate, NEG_INF)
    top_v, sel = lax.top_k(gate, topk)
    valid = top_v > 0.5 * NEG_INF

    def per_batch(args):
        q_b, kb_b, vb_b, sel_b, valid_b = args

        def per_chunk(c):
            start = c * Q
            pos = start + jnp.arange(Q)
            qc = lax.dynamic_slice_in_dim(q_b, start, Q, axis=1)
            sc = lax.dynamic_slice_in_dim(sel_b, start, Q, axis=1)
            vc = lax.dynamic_slice_in_dim(valid_b, start, Q, axis=1)
            kg = jax.vmap(lambda kbh, ih: kbh[ih])(kb_b, sc)
            vg = jax.vmap(lambda vbh, ih: vbh[ih])(vb_b, sc)
            blk = start // A_BLOCK
            k_own = lax.dynamic_index_in_dim(kb_b, blk, axis=1, keepdims=False)
            v_own = lax.dynamic_index_in_dim(vb_b, blk, axis=1, keepdims=False)
            s_sel = jnp.einsum('hqd,hqkld->hqkl', qc, kg).reshape(H, Q, topk * L)
            s_own = jnp.einsum('hqd,hld->hql', qc, k_own)
            m_sel = jnp.broadcast_to(vc[..., None], (H, Q, topk, L)).reshape(H, Q, topk * L)
            kpos = blk * A_BLOCK + jnp.arange(L)
            m_own = jnp.broadcast_to(kpos[None, None, :] <= pos[None, :, None], (H, Q, L))
            s = jnp.concatenate([s_sel, s_own], axis=-1).astype(jnp.float32) * scale
            p = masked_softmax(s, jnp.concatenate([m_sel, m_own], axis=-1)).astype(v.dtype)
            o = jnp.einsum('hqkl,hqkld->hqd', p[..., :topk * L].reshape(H, Q, topk, L), vg)
            return o + jnp.einsum('hql,hld->hqd', p[..., topk * L:], v_own)

        outs = lax.map(per_chunk, jnp.arange(nc))
        return outs.transpose(0, 2, 1, 3).reshape(S, H, D)

    return lax.map(per_batch, (qh, kb, vb, sel, valid))

def compress(t, pos_emb, w1, b1, w2, b2):
    B, S, G, D = t.shape
    n_cmp = (S - CMP_LEN) // CMP_STRIDE + 1
    idx = np.arange(n_cmp)[:, None] * CMP_STRIDE + np.arange(CMP_LEN)[None, :]
    blocks = t[:, idx] + pos_emb[None, None, :, None, :]
    flat = blocks.transpose(0, 3, 1, 2, 4).reshape(B, G, n_cmp, CMP_LEN * D)
    return jax.nn.gelu(flat @ w1 + b1) @ w2 + b2

def nsa_attention(q, kc, vc, ks, vs, kw, vw, gates):
    B, S, H, D = q.shape
    G, R, Q = B_KV_HEADS, B_GROUP, B_QBLOCK
    n_cmp = kc.shape[2]
    n_slc = S // SLC_BLOCK
    topn = min(SLC_TOPN, n_slc)
    nc = S // Q
    scale = HEAD_DIM ** -0.5
    cmp_end = jnp.arange(n_cmp) * CMP_STRIDE + (CMP_LEN - 1)
    ci = np.arange(n_cmp)[:, None]
    sj = np.arange(n_slc)[None, :]
    overlap = jnp.asarray(((ci * CMP_STRIDE < (sj + 1) * SLC_BLOCK) &
                           (ci * CMP_STRIDE + CMP_LEN > sj * SLC_BLOCK)).astype(np.float32))

    qg = q.reshape(B, S, G, R, D).transpose(0, 2, 3, 1, 4)
    ksb = ks.transpose(0, 2, 1, 3).reshape(B, G, n_slc, SLC_BLOCK, D)
    vsb = vs.transpose(0, 2, 1, 3).reshape(B, G, n_slc, SLC_BLOCK, D)
    kwp = jnp.pad(kw.transpose(0, 2, 1, 3), ((0, 0), (0, 0), (WINDOW, 0), (0, 0)))
    vwp = jnp.pad(vw.transpose(0, 2, 1, 3), ((0, 0), (0, 0), (WINDOW, 0), (0, 0)))
    gg = gates.reshape(B, S, G, R, 3).transpose(0, 2, 3, 1, 4)

    def per_batch(args):
        q_b, kc_b, vc_b, ks_b, vs_b, kw_b, vw_b, g_b = args

        def per_chunk(c):
            start = c * Q
            pos = start + jnp.arange(Q)
            qc = lax.dynamic_slice_in_dim(q_b, start, Q, axis=2)
            gc = lax.dynamic_slice_in_dim(g_b, start, Q, axis=2)
            s = jnp.einsum('grqd,gnd->grqn', qc, kc_b).astype(jnp.float32) * scale
            p_cmp = masked_softmax(s, cmp_end[None, :] <= pos[:, None])
            o_cmp = jnp.einsum('grqn,gnd->grqd', p_cmp.astype(vc_b.dtype), vc_b)
            imp = jnp.einsum('grqn,nj->gqj', p_cmp, overlap)
            own = pos // SLC_BLOCK
            blk = jnp.arange(n_slc)[None, :]
            forced = (blk == 0) | (blk == own[:, None]) | (blk == own[:, None] - 1)
            imp = jnp.where(forced, BIG, imp)
            imp = jnp.where(blk <= own[:, None], imp, NEG_INF)
            top_v, sel = lax.top_k(imp, topn)
            valid = top_v > 0.5 * NEG_INF
            kg = jax.vmap(lambda kbg, ig: kbg[ig])(ks_b, sel)
            vg = jax.vmap(lambda vbg, ig: vbg[ig])(vs_b, sel)
            s = jnp.einsum('grqd,gqnld->grqnl', qc, kg).astype(jnp.float32) * scale
            kpos = sel[..., None] * SLC_BLOCK + jnp.arange(SLC_BLOCK)
            m = valid[..., None] & (kpos <= pos[None, :, None, None])
            p = masked_softmax(s.reshape(G, R, Q, topn * SLC_BLOCK),
                               m.reshape(G, 1, Q, topn * SLC_BLOCK))
            o_slc = jnp.einsum('grqnl,gqnld->grqd',
                               p.reshape(G, R, Q, topn, SLC_BLOCK).astype(vs_b.dtype), vg)
            kwc = lax.dynamic_slice_in_dim(kw_b, start, WINDOW + Q, axis=1)
            vwc = lax.dynamic_slice_in_dim(vw_b, start, WINDOW + Q, axis=1)
            kpos_w = start - WINDOW + jnp.arange(WINDOW + Q)
            m_w = ((kpos_w[None, :] <= pos[:, None]) & (kpos_w[None, :] > pos[:, None] - WINDOW)
                   & (kpos_w[None, :] >= 0))
            s = jnp.einsum('grqd,gkd->grqk', qc, kwc).astype(jnp.float32) * scale
            p = masked_softmax(s, m_w)
            o_win = jnp.einsum('grqk,gkd->grqd', p.astype(vwc.dtype), vwc)
            return gc[..., 0:1] * o_cmp + gc[..., 1:2] * o_slc + gc[..., 2:3] * o_win

        outs = lax.map(per_chunk, jnp.arange(nc))
        return outs.transpose(0, 3, 1, 2, 4).reshape(S, H, D)

    return lax.map(per_batch, (qg, kc, vc, ksb, vsb, kwp, vwp, gg))

def peer_ffn(h, w_q, sub_k1, sub_k2, expert_u, expert_v):
    B, S, Dm = h.shape
    T = B * S
    ht = h.reshape(T, Dm)
    q = (ht @ w_q).reshape(T, PEER_HEADS, PEER_QDIM)
    s1 = jnp.einsum('thd,nd->thn', q[..., :PEER_HALF], sub_k1).astype(jnp.float32)
    s2 = jnp.einsum('thd,nd->thn', q[..., PEER_HALF:], sub_k2).astype(jnp.float32)
    v1, i1 = lax.top_k(s1, PEER_TOPK)
    v2, i2 = lax.top_k(s2, PEER_TOPK)
    cand = (v1[..., :, None] + v2[..., None, :]).reshape(T, PEER_HEADS, PEER_TOPK * PEER_TOPK)
    cand_idx = (i1[..., :, None] * PEER_NKEYS + i2[..., None, :]).reshape(T, PEER_HEADS, PEER_TOPK * PEER_TOPK)
    vals, pos = lax.top_k(cand, PEER_TOPK)
    experts = jnp.take_along_axis(cand_idx, pos, axis=-1)
    gates = jax.nn.softmax(vals, axis=-1)

    def per_chunk(args):
        xc, ec, gc = args
        u = expert_u[ec]
        a = jnp.einsum('cd,chkd->chk', xc, u).astype(jnp.float32)
        w = (jax.nn.gelu(a) * gc).astype(xc.dtype)
        return jnp.einsum('chk,chkd->cd', w, expert_v[ec])

    nc = T // PEER_CHUNK
    out = lax.map(per_chunk, (ht.reshape(nc, PEER_CHUNK, Dm),
                              experts.reshape(nc, PEER_CHUNK, PEER_HEADS, PEER_TOPK),
                              gates.reshape(nc, PEER_CHUNK, PEER_HEADS, PEER_TOPK)))
    return out.reshape(B, S, Dm)

def hybrid_layer(x, cos, sin, norm1_g, w_in, b_merge, a_q_g, a_k_g, b_q_g, b_kc_g, b_ks_g, b_kw_g,
                 cmp_pos_k, cmp_k_w1, cmp_k_b1, cmp_k_w2, cmp_k_b2,
                 cmp_pos_v, cmp_v_w1, cmp_v_b1, cmp_v_w2, cmp_v_b2,
                 w_up_a, w_up_b, w_out, norm2_g, peer_wq, peer_k1, peer_k2, peer_u, peer_v):
    B, S, _ = x.shape
    h = rmsnorm(x, norm1_g)
    (aq, ak, av, bq, bkc, bvc, bks, bvs, bkw, bvw, bgate, mgate) = split_columns(h @ w_in)

    def heads(t, n):
        return t.reshape(B, S, n, HEAD_DIM)

    qa = partial_rope(rmsnorm(heads(aq, A_HEADS), a_q_g), cos, sin)
    ka = partial_rope(rmsnorm(heads(ak, A_HEADS), a_k_g), cos, sin)
    ya = moba_attention(qa, ka, heads(av, A_HEADS)).reshape(B, S, A_WIDTH)

    qb = partial_rope(rmsnorm(heads(bq, B_HEADS), b_q_g), cos, sin)
    kc = rmsnorm(compress(heads(bkc, B_KV_HEADS), cmp_pos_k, cmp_k_w1, cmp_k_b1, cmp_k_w2, cmp_k_b2), b_kc_g)
    vc = compress(heads(bvc, B_KV_HEADS), cmp_pos_v, cmp_v_w1, cmp_v_b1, cmp_v_w2, cmp_v_b2)
    ks = partial_rope(rmsnorm(heads(bks, B_KV_HEADS), b_ks_g), cos, sin)
    kw = partial_rope(rmsnorm(heads(bkw, B_KV_HEADS), b_kw_g), cos, sin)
    gb = jax.nn.sigmoid(bgate.astype(jnp.float32)).astype(x.dtype).reshape(B, S, B_HEADS, 3)
    yb = nsa_attention(qb, kc, vc, ks, heads(bvs, B_KV_HEADS), kw, heads(bvw, B_KV_HEADS), gb)
    yb = yb.reshape(B, S, B_WIDTH)

    g = jax.nn.sigmoid((mgate.reshape(B, S, N_BRANCH, D_MODEL) + b_merge).astype(jnp.float32)).astype(x.dtype)
    merged = g[:, :, 0] * (ya @ w_up_a) + g[:, :, 1] * (yb @ w_up_b)
    x = x + merged @ w_out

    return x + peer_ffn(rmsnorm(x, norm2_g), peer_wq, peer_k1, peer_k2, peer_u, peer_v)

def first_inputs(seed: int = 0) -> dict:
    key = jax.random.key(seed)
    ks = jax.random.split(key, 32)
    L = DEPTH
    f32 = jnp.float32

    def nrm(k, shape, scale):
        return jax.random.normal(k, shape, f32) * scale

    def gain(k, shape):
        return 1.0 + 0.05 * jax.random.normal(k, shape, f32)

    return {
        "x": nrm(ks[0], (BATCH, SEQ, D_MODEL), 1.0),
        "norm1_g": gain(ks[1], (L, D_MODEL)),
        "w_in": nrm(ks[2], (L, D_MODEL, IN_COLS), D_MODEL ** -0.5),
        "b_merge": nrm(ks[3], (L, N_BRANCH, D_MODEL), 0.1),
        "a_q_g": gain(ks[4], (L, HEAD_DIM)),
        "a_k_g": gain(ks[5], (L, HEAD_DIM)),
        "b_q_g": gain(ks[6], (L, HEAD_DIM)),
        "b_kc_g": gain(ks[7], (L, HEAD_DIM)),
        "b_ks_g": gain(ks[8], (L, HEAD_DIM)),
        "b_kw_g": gain(ks[9], (L, HEAD_DIM)),
        "cmp_pos_k": nrm(ks[10], (L, CMP_LEN, HEAD_DIM), 0.1),
        "cmp_k_w1": nrm(ks[11], (L, CMP_LEN * HEAD_DIM, CMP_HIDDEN), (CMP_LEN * HEAD_DIM) ** -0.5),
        "cmp_k_b1": nrm(ks[12], (L, CMP_HIDDEN), 0.02),
        "cmp_k_w2": nrm(ks[13], (L, CMP_HIDDEN, HEAD_DIM), CMP_HIDDEN ** -0.5),
        "cmp_k_b2": nrm(ks[14], (L, HEAD_DIM), 0.02),
        "cmp_pos_v": nrm(ks[15], (L, CMP_LEN, HEAD_DIM), 0.1),
        "cmp_v_w1": nrm(ks[16], (L, CMP_LEN * HEAD_DIM, CMP_HIDDEN), (CMP_LEN * HEAD_DIM) ** -0.5),
        "cmp_v_b1": nrm(ks[17], (L, CMP_HIDDEN), 0.02),
        "cmp_v_w2": nrm(ks[18], (L, CMP_HIDDEN, HEAD_DIM), CMP_HIDDEN ** -0.5),
        "cmp_v_b2": nrm(ks[19], (L, HEAD_DIM), 0.02),
        "w_up_a": nrm(ks[20], (L, A_WIDTH, D_MODEL), A_WIDTH ** -0.5),
        "w_up_b": nrm(ks[21], (L, B_WIDTH, D_MODEL), B_WIDTH ** -0.5),
        "w_out": nrm(ks[22], (L, D_MODEL, D_MODEL), D_MODEL ** -0.5),
        "norm2_g": gain(ks[23], (L, D_MODEL)),
        "peer_wq": nrm(ks[24], (L, D_MODEL, PEER_HEADS * PEER_QDIM), D_MODEL ** -0.5),
        "peer_k1": nrm(ks[25], (L, PEER_NKEYS, PEER_HALF), PEER_HALF ** -0.5),
        "peer_k2": nrm(ks[26], (L, PEER_NKEYS, PEER_HALF), PEER_HALF ** -0.5),
        "peer_u": nrm(ks[27], (L, PEER_N, D_MODEL), D_MODEL ** -0.5),
        "peer_v": nrm(ks[28], (L, PEER_N, D_MODEL), 0.3),
    }

def first_block(x, norm1_g, w_in, b_merge, a_q_g, a_k_g, b_q_g, b_kc_g, b_ks_g, b_kw_g,
              cmp_pos_k, cmp_k_w1, cmp_k_b1, cmp_k_w2, cmp_k_b2,
              cmp_pos_v, cmp_v_w1, cmp_v_b1, cmp_v_w2, cmp_v_b2,
              w_up_a, w_up_b, w_out, norm2_g, peer_wq, peer_k1, peer_k2, peer_u, peer_v):
    cos, sin = rope_tables(x.shape[1])
    for l in range(DEPTH):
        x = hybrid_layer(x, cos, sin, norm1_g[l], w_in[l], b_merge[l], a_q_g[l], a_k_g[l],
                         b_q_g[l], b_kc_g[l], b_ks_g[l], b_kw_g[l],
                         cmp_pos_k[l], cmp_k_w1[l], cmp_k_b1[l], cmp_k_w2[l], cmp_k_b2[l],
                         cmp_pos_v[l], cmp_v_w1[l], cmp_v_b1[l], cmp_v_w2[l], cmp_v_b2[l],
                         w_up_a[l], w_up_b[l], w_out[l], norm2_g[l],
                         peer_wq[l], peer_k1[l], peer_k2[l], peer_u[l], peer_v[l])
    return x


DEPTH_2 = 2

N_MIXERS = 2
N_ATTN_LAYERS = (DEPTH_2 + 1) // 2
N_POOL_LAYERS = DEPTH_2 // 2
GRID_W = 64
EPS = 1e-6

N_HEADS = D_MODEL // HEAD_DIM
N_KV_HEADS = 4
GQA_GROUP = N_HEADS // N_KV_HEADS
Q_BLOCK = 128
ROPE_THETA_2 = 10000.0
ROPE_PAIRS = HEAD_DIM // 4
QKV_DIM = (N_HEADS + 2 * N_KV_HEADS) * HEAD_DIM

POOL_WINDOWS = (2, 4, 8, 16)
N_POOL_GROUPS = len(POOL_WINDOWS)
POOL_GROUP_W = D_MODEL // N_POOL_GROUPS

MEM_LEN = 256
X_HEADS = 4
X_HEAD_DIM = D_MODEL // X_HEADS

D_FF = 2816
CONV_W = 3


def rmsnorm_2(x, gain):
    x32 = x.astype(jnp.float32)
    y = x32 * lax.rsqrt(jnp.mean(x32 * x32, axis=-1, keepdims=True) + EPS)
    return (y * gain.astype(jnp.float32)).astype(x.dtype)

def axial_rope_tables(seq_len):
    n_rows = seq_len // GRID_W
    row = jnp.repeat(jnp.arange(n_rows, dtype=jnp.float32), GRID_W)
    col = jnp.tile(jnp.arange(GRID_W, dtype=jnp.float32), n_rows)
    inv_freq = ROPE_THETA_2 ** (-jnp.arange(ROPE_PAIRS, dtype=jnp.float32) / ROPE_PAIRS)
    ang = jnp.stack([row[:, None] * inv_freq, col[:, None] * inv_freq], axis=1)
    return jnp.cos(ang), jnp.sin(ang)

def apply_axial_rope(x, cos, sin):
    b, s, h, d = x.shape
    xs = x.astype(jnp.float32).reshape(b, s, h, 2, 2, ROPE_PAIRS)
    x1, x2 = xs[..., 0, :], xs[..., 1, :]
    c = cos[None, :, None]
    sn = sin[None, :, None]
    out = jnp.stack([x1 * c - x2 * sn, x2 * c + x1 * sn], axis=-2)
    return out.reshape(b, s, h, d).astype(x.dtype)

def axial_gqa_attention(h, w_qkv, q_gain, k_gain, w_o):
    b, s, _ = h.shape
    qkv = h @ w_qkv
    q_end = N_HEADS * HEAD_DIM
    k_end = q_end + N_KV_HEADS * HEAD_DIM
    q = qkv[..., :q_end].reshape(b, s, N_HEADS, HEAD_DIM)
    k = qkv[..., q_end:k_end].reshape(b, s, N_KV_HEADS, HEAD_DIM)
    v = qkv[..., k_end:].reshape(b, s, N_KV_HEADS, HEAD_DIM)
    q = rmsnorm_2(q, q_gain)
    k = rmsnorm_2(k, k_gain)
    cos, sin = axial_rope_tables(s)
    q = apply_axial_rope(q, cos, sin) * (HEAD_DIM ** -0.5)
    k = apply_axial_rope(k, cos, sin)
    n_blk = s // Q_BLOCK
    qb = q.reshape(b, n_blk, Q_BLOCK, N_KV_HEADS, GQA_GROUP, HEAD_DIM).transpose(1, 0, 3, 4, 2, 5)
    kt = k.transpose(0, 2, 1, 3)
    vt = v.transpose(0, 2, 1, 3)

    def attend_block(q_blk):
        scores = jnp.einsum('bkgqd,bksd->bkgqs', q_blk, kt).astype(jnp.float32)
        p = jax.nn.softmax(scores, axis=-1).astype(vt.dtype)
        return jnp.einsum('bkgqs,bksd->bkgqd', p, vt)

    o = lax.map(attend_block, qb)
    o = o.transpose(1, 0, 4, 2, 3, 5).reshape(b, s, N_HEADS * HEAD_DIM)
    return o @ w_o

def multiscale_pool_mixer(h, w_grp, scale):
    b, s, d = h.shape
    hg = h.astype(jnp.float32).reshape(b, s, N_POOL_GROUPS, POOL_GROUP_W)
    csum = jnp.concatenate(
        [jnp.zeros((b, 1, N_POOL_GROUPS, POOL_GROUP_W), jnp.float32), jnp.cumsum(hg, axis=1)], axis=1)
    t = jnp.arange(s)[:, None]
    win = jnp.array(POOL_WINDOWS, dtype=jnp.int32)[None, :]
    lo = jnp.clip(t - win // 2, 0, s)
    hi = jnp.clip(t + win - win // 2, 0, s)
    s_hi = jnp.take_along_axis(csum, hi[None, :, :, None], axis=1)
    s_lo = jnp.take_along_axis(csum, lo[None, :, :, None], axis=1)
    count = (hi - lo).astype(jnp.float32)[None, :, :, None]
    mixed = (s_hi - s_lo) / count - hg
    y = jnp.einsum('bsgc,gcd->bsgd', mixed, w_grp.astype(jnp.float32)).reshape(b, s, d)
    return (y * scale.astype(jnp.float32)).astype(h.dtype)

def memory_cross_attention(h, mem_n, w_q, w_kv, w_o):
    b, s, _ = h.shape
    m = mem_n.shape[1]
    q = (h @ w_q).reshape(b, s, X_HEADS, X_HEAD_DIM) * (X_HEAD_DIM ** -0.5)
    kv = mem_n @ w_kv
    k = kv[..., :D_MODEL].reshape(b, m, X_HEADS, X_HEAD_DIM)
    v = kv[..., D_MODEL:].reshape(b, m, X_HEADS, X_HEAD_DIM)
    scores = jnp.einsum('bshd,bmhd->bhsm', q, k).astype(jnp.float32)
    p = jax.nn.softmax(scores, axis=-1).astype(v.dtype)
    o = jnp.einsum('bhsm,bmhd->bshd', p, v).reshape(b, s, D_MODEL)
    return o @ w_o

def conv_gated_ffn(h, w_up, conv_w, conv_b, w_down):
    u = h @ w_up
    up = jnp.pad(u, ((0, 0), (1, 1), (0, 0)))
    u = up[:, :-2] * conv_w[0] + up[:, 1:-1] * conv_w[1] + up[:, 2:] * conv_w[2] + conv_b
    gate, val = u[..., :D_FF], u[..., D_FF:]
    return (jax.nn.silu(gate) * val) @ w_down

def second_inputs(seed: int = 0) -> dict:
    key = jax.random.key(seed)
    ks = jax.random.split(key, 24)
    f32 = jnp.float32

    def nrm(k, shape, scale):
        return jax.random.normal(k, shape, f32) * scale

    def gain(k, shape):
        return 1.0 + 0.05 * jax.random.normal(k, shape, f32)

    na, nb = N_ATTN_LAYERS, N_POOL_LAYERS
    return {
        "x": nrm(ks[0], (BATCH, SEQ, D_MODEL), 1.0),
        "mem": nrm(ks[1], (BATCH, MEM_LEN, D_MODEL), 1.0),
        "attn_norm": gain(ks[2], (na, D_MODEL)),
        "attn_w_qkv": nrm(ks[3], (na, D_MODEL, QKV_DIM), D_MODEL ** -0.5),
        "attn_q_gain": gain(ks[4], (na, HEAD_DIM)),
        "attn_k_gain": gain(ks[5], (na, HEAD_DIM)),
        "attn_w_o": nrm(ks[6], (na, N_HEADS * HEAD_DIM, D_MODEL), (N_HEADS * HEAD_DIM) ** -0.5),
        "pool_norm": gain(ks[7], (nb, D_MODEL)),
        "pool_w": nrm(ks[8], (nb, N_POOL_GROUPS, POOL_GROUP_W, POOL_GROUP_W), POOL_GROUP_W ** -0.5),
        "pool_scale": gain(ks[9], (nb, D_MODEL)),
        "xattn_norm": gain(ks[10], (DEPTH_2, D_MODEL)),
        "mem_norm": gain(ks[11], (DEPTH_2, D_MODEL)),
        "xattn_w_q": nrm(ks[12], (DEPTH_2, D_MODEL, D_MODEL), D_MODEL ** -0.5),
        "xattn_w_kv": nrm(ks[13], (DEPTH_2, D_MODEL, 2 * D_MODEL), D_MODEL ** -0.5),
        "xattn_w_o": nrm(ks[14], (DEPTH_2, D_MODEL, D_MODEL), D_MODEL ** -0.5),
        "ffn_norm": gain(ks[15], (DEPTH_2, D_MODEL)),
        "ffn_w_up": nrm(ks[16], (DEPTH_2, D_MODEL, 2 * D_FF), D_MODEL ** -0.5),
        "ffn_conv_w": nrm(ks[17], (DEPTH_2, CONV_W, 2 * D_FF), CONV_W ** -0.5),
        "ffn_conv_b": nrm(ks[18], (DEPTH_2, 2 * D_FF), 0.02),
        "ffn_w_down": nrm(ks[19], (DEPTH_2, D_FF, D_MODEL), D_FF ** -0.5),
        "final_norm": gain(ks[20], (D_MODEL,)),
    }

def second_block(x, mem, attn_norm, attn_w_qkv, attn_q_gain, attn_k_gain, attn_w_o,
              pool_norm, pool_w, pool_scale,
              xattn_norm, mem_norm, xattn_w_q, xattn_w_kv, xattn_w_o,
              ffn_norm, ffn_w_up, ffn_conv_w, ffn_conv_b, ffn_w_down,
              final_norm):
    ia = 0
    ib = 0
    for i in range(DEPTH_2):
        if i % N_MIXERS == 0:
            x = x + axial_gqa_attention(rmsnorm_2(x, attn_norm[ia]), attn_w_qkv[ia],
                                        attn_q_gain[ia], attn_k_gain[ia], attn_w_o[ia])
            ia += 1
        else:
            x = x + multiscale_pool_mixer(rmsnorm_2(x, pool_norm[ib]), pool_w[ib], pool_scale[ib])
            ib += 1
        x = x + memory_cross_attention(rmsnorm_2(x, xattn_norm[i]), rmsnorm_2(mem, mem_norm[i]),
                                       xattn_w_q[i], xattn_w_kv[i], xattn_w_o[i])
        x = x + conv_gated_ffn(rmsnorm_2(x, ffn_norm[i]), ffn_w_up[i], ffn_conv_w[i],
                               ffn_conv_b[i], ffn_w_down[i])
    return rmsnorm_2(x, final_norm)


def setup_inputs(seed=0):
    out = dict(first_inputs(seed))
    for name, value in second_inputs(seed + 1).items():
        if name != "x":
            out[name + "_2"] = value
    return out


def reference(
    x, norm1_g, w_in, b_merge, a_q_g, a_k_g, b_q_g, b_kc_g, b_ks_g, b_kw_g, cmp_pos_k, cmp_k_w1,
    cmp_k_b1, cmp_k_w2, cmp_k_b2, cmp_pos_v, cmp_v_w1, cmp_v_b1, cmp_v_w2, cmp_v_b2, w_up_a,
    w_up_b, w_out, norm2_g, peer_wq, peer_k1, peer_k2, peer_u, peer_v, mem_2, attn_norm_2,
    attn_w_qkv_2, attn_q_gain_2, attn_k_gain_2, attn_w_o_2, pool_norm_2, pool_w_2, pool_scale_2,
    xattn_norm_2, mem_norm_2, xattn_w_q_2, xattn_w_kv_2, xattn_w_o_2, ffn_norm_2, ffn_w_up_2,
    ffn_conv_w_2, ffn_conv_b_2, ffn_w_down_2, final_norm_2,
):
    x = first_block(
        x, norm1_g, w_in, b_merge, a_q_g, a_k_g, b_q_g, b_kc_g, b_ks_g, b_kw_g, cmp_pos_k,
        cmp_k_w1, cmp_k_b1, cmp_k_w2, cmp_k_b2, cmp_pos_v, cmp_v_w1, cmp_v_b1, cmp_v_w2,
        cmp_v_b2, w_up_a, w_up_b, w_out, norm2_g, peer_wq, peer_k1, peer_k2, peer_u, peer_v,
    )
    return second_block(
        x, mem_2, attn_norm_2, attn_w_qkv_2, attn_q_gain_2, attn_k_gain_2, attn_w_o_2,
        pool_norm_2, pool_w_2, pool_scale_2, xattn_norm_2, mem_norm_2, xattn_w_q_2,
        xattn_w_kv_2, xattn_w_o_2, ffn_norm_2, ffn_w_up_2, ffn_conv_w_2, ffn_conv_b_2,
        ffn_w_down_2, final_norm_2,
    )


_drawn_inputs = setup_inputs


def setup_inputs(seed=0):
    import zlib

    import numpy as np

    out = dict(_drawn_inputs(seed))
    spreads = {}
    factors = {'b_merge': 2.994,
     'a_q_g': 4.592,
     'a_k_g': 3.921,
     'b_q_g': 3.898,
     'b_kc_g': 6.066,
     'b_ks_g': 5.519,
     'b_kw_g': 5.397,
     'cmp_pos_k': 4.72,
     'cmp_k_b1': 8.0,
     'cmp_k_b2': 8.0,
     'cmp_v_b1': 5.614,
     'cmp_v_b2': 3.386,
     'attn_norm_2': 4.946,
     'attn_q_gain_2': 8.0,
     'attn_k_gain_2': 7.574,
     'xattn_norm_2': 7.773,
     'mem_norm_2': 5.405,
     'ffn_conv_b_2': 3.004}
    for name, (base, spread) in spreads.items():
        noise = np.random.default_rng([zlib.crc32(name.encode()), seed]).standard_normal(out[name].shape)
        drawn = base * np.exp(spread * noise) if base else spread * noise
        out[name] = __import__('jax').numpy.asarray(drawn.astype(out[name].dtype))
    for name, factor in factors.items():
        out[name] = (out[name] * factor).astype(out[name].dtype)
    return out
```

```python
from contextlib import ExitStack

import numpy as np
import concourse.bass as bass
from concourse import mybir

F32 = mybir.dt.float32
U32 = mybir.dt.uint32
ALU = mybir.AluOpType
ACT = mybir.ActivationFunctionType
AXX = mybir.AxisListType.X

P = 128
S = 256
T = S // P
D = 1024
KD = D // P
HD = 64
NEG = -1e30
LOW = -3.0e38
EPS = 1e-6

A_HEADS = B_HEADS = 8
KV_HEADS = 2
N_NORMED = 28
NORMED = N_NORMED * HD
AV, VS, VW, KC, VC, BG = NORMED, NORMED + 512, NORMED + 640, NORMED + 768, NORMED + 896, NORMED + 1024
PROJ = BG + 3 * B_HEADS
N_WIN = -(-PROJ // 512)
CMP_LEN, CMP_STRIDE, CMP_HID = 32, 16, 256
N_CMP = (S - CMP_LEN) // CMP_STRIDE + 1
PEER_HEADS, NKEYS, TOPK = 8, 128, 16

DEPTH2 = 2
N_HEADS, N_KV = 16, 4
QKV = (N_HEADS + 2 * N_KV) * HD
X_HEADS, X_HD = 4, 256
D_FF = 2816
NF = D_FF // P
POOL_WINDOWS = (2, 4, 8, 16)
GRID_W = 64

BLK = 4096
SLOTS = 3


def weight_blocks():
    out = [("win", n) for n in range(N_WIN)] + [("mg", 0), ("mg", 1), ("cmp", 0), ("cmp", 1), ("mg", 2), ("mg", 3)]
    out += [("up", 0), ("up", 1), ("out", 0), ("out", 1)] + [("wq", n) for n in range(4)]
    out += [("qkv", n) for n in range(3)]
    for i in range(DEPTH2):
        out += [("xk", i, n) for n in range(2)] + [("xv", i, n) for n in range(2)]
        out += [("wo", n) for n in range(2)] if i == 0 else [("pool", 0)]
        out += [("xq", i, n) for n in range(2)] + [("xo", i, n) for n in range(2)]
        out += [("ffu", i, n) for n in range(NF // 2)] + [("ffd", i, n) for n in range(-(-NF // 4))]
    return out


BLOCKS = weight_blocks()
BLOCK = {name: n for n, name in enumerate(BLOCKS)}
FIRST2 = BLOCK[("qkv", 0)]


def bank_groups():
    out = [(("win", n, t), "da"[t]) for n in range(N_WIN) for t in range(T)]
    out += [(("win2", kv), "d") for kv in range(2)]
    out += [(("mg", g), "a") for g in range(4)]
    out += [(("hid", kv), "d") for kv in range(2)] + [(("mg", 4), "a")]
    out += [(("hidT", kv), "d") for kv in range(2)] + [(("mg", 5), "a")]
    out += [(("c2", kv), "d") for kv in range(2)] + [(("mg", 6), "a")]
    out += [(("kcT",), "d"), (("mg", 7), "a")]
    out += [(("qkt", m), "a") for m in range(7)]
    out += [(("scmp", g), "d") for g in range(KV_HEADS)] + [(("pct", m), "a") for m in range(4)]
    out += [(("ya", p), "d") for p in range(4)] + [(("yb", r), "d") for r in range(4)]
    out += [(("up", f), "d") for f in range(KD)]
    out += [(("pq", g), "a") for g in range(8)] + [(("sc", m), "a") for m in range(8)]
    out += [(("et", m), "a") for m in range(3)]
    out += [(("qkv", n, t), "da"[t]) for n in range(3) for t in range(T)]
    for i in range(DEPTH2):
        out += [(("xk", i, g), "a") for g in range(4)]
        if i == 0:
            out += [(("qkt2", m), "a") for m in range(5)] + [(("y2", p), "d") for p in range(8)]
        else:
            out += [(("pm", g), "a") for g in range(4)] + [(("py", t, g), "d") for t in range(T) for g in range(2)]
        out += [(("xq", i, g), "a") for g in range(4)] + [(("yx", i, h), "d") for h in range(X_HEADS)]
        out += [(("ffu", i, f), "d") for f in range(NF)]
    return out


GROUPS = bank_groups()
GROUP = {name: q for q, (name, _) in enumerate(GROUPS)}
RING = 4


def freed(q):
    who = GROUPS[q][1]
    return who, sum(1 for _, w in GROUPS[:q + 1] if w == who)


NORMS = ["norm1", "norm2", "attn", "mem0", "x0", "ffn0", "mem1", "pool", "x1", "ffn1", "final"]
TURNED = [n for n in NORMS if n not in ("pool", "final")]
WIDE = ["out", "peer", "xv0", "wo", "xo0", "ffd0", "xv1", "xo1", "ffd1"]
JOBS = {"a": 0, "b": 8, "self": 24, "x0": 40, "x1": 44}
PAIR_JOBS = 8


class Columns:

    def __init__(self, at=0):
        self.at = at

    def take(self, n):
        self.at += n
        return slice(self.at - n, self.at)


SM = Columns()
IDENT, IOTA, GAINS = SM.take(P), SM.take(NKEYS), SM.take((len(NORMS) - 1) * KD)
CONV, BMERGE, PKEYS = SM.take(DEPTH2 * 2 * NF * 4), SM.take(2 * KD), SM.take(2 * NKEYS)
EPSC, ROPE1, ROPE2 = SM.take(1), SM.take(2 * T * 8), SM.take(2 * T * 2 * 16)
HG1, HG2 = SM.take(5 * HD), SM.take(2 * HD)
L1 = Columns()
MASK, CMASK, CANY, CPOS = L1.take(T * S), L1.take(T * N_CMP), L1.take(T), L1.take(2 * 16)
CB1, CB2, CW2, KCG = L1.take(2 * CMP_HID), L1.take(2 * HD), L1.take(2 * 2 * HD), L1.take(HD)


def block_stack(nc: bass.Bass, x, mem, weights, expert_u, expert_v, small, layer1, band, wide_gains, out):
    with ExitStack() as ctx:
        def sb(name, shape, dt=F32):
            return ctx.enter_context(nc.sbuf_tensor(name, shape, dt))

        def sem(name):
            return ctx.enter_context(nc.semaphore(name))

        X = sb("X", [P, T, D])
        HT = sb("HT", [P, KD, S])
        wring = sb("wring", [P, SLOTS, BLK])
        smalls = sb("smalls", [P, SM.at])
        stat = sb("stat", [P, 4 * T])
        arena = sb("arena", [P, NKEYS * S])
        att = sb("att", [P, 4, 4, T])
        PS = [ctx.enter_context(nc.psum_tensor(f"bank{b}", [P, 512], F32)) for b in range(8)]

        ident = smalls[:, IDENT]
        iota = smalls[:, IOTA]
        eps = smalls[:, EPSC]
        gains = smalls[:, GAINS].rearrange("p (n k) -> p n k", k=KD)
        conv = smalls[:, CONV].rearrange("p (i f c) -> p i f c", i=DEPTH2, c=4)
        pkeys = smalls[:, PKEYS].rearrange("p (h n) -> p h n", h=2)
        rope1 = smalls[:, ROPE1].rearrange("p (c t j) -> p c t j", c=2, t=T)
        rope2 = smalls[:, ROPE2].rearrange("p (c t a j) -> p c t a j", c=2, t=T, a=2)

        def area(cols, *dims, dt=None):
            n = int(np.prod(dims))
            v = arena[:, cols.take(n)]
            if dt is not None:
                v = v.bitcast(dt)
            names = " ".join(f"d{i}" for i in range(len(dims)))
            sizes = {f"d{i}": d for i, d in enumerate(dims)}
            return v.rearrange(f"p ({names}) -> p {names}", **sizes) if len(dims) > 1 else v

        c1 = Columns()
        H = area(c1, T, D)
        proj = area(c1, T, PROJ)
        qkT = area(c1, 14, S)
        mgate = area(c1, KD, 2, S)
        yT = area(c1, 2, 4, S)
        merged = area(c1, KD, S)
        SMx = area(c1, 2, T, S)
        Pr = area(c1, 3, T, S)
        PT = area(c1, 2, T, S)
        consts1 = area(c1, L1.at)
        gate3 = area(c1, T, 3 * B_HEADS)
        merged_at = 2048 + T * PROJ + 14 * S + 2 * KD * S + 2 * 4 * S
        sq1 = arena[:, merged_at:merged_at + T * NORMED].rearrange("p (t n) -> p t n", t=T)
        hstat1 = area(c1, 3, T, N_NORMED)
        rtmp1 = area(c1, 4, T, N_NORMED, 8)
        blocksT = area(c1, 2, 16, 2, N_CMP)
        hid = area(c1, 2, CMP_HID)
        hidT = area(c1, 2, 2, 2 * N_CMP)
        kvc = area(c1, 2, KV_HEADS, HD)
        ctmp = area(c1, 2, KV_HEADS, HD)
        cst = area(c1, 3, KV_HEADS)
        kcT = area(c1, 16)
        scmp = area(c1, 16, 16)
        cred = area(c1, 3, 16)
        pcT = area(c1, B_HEADS, S)
        assert c1.at <= NKEYS * S
        mask = consts1[:, MASK].rearrange("p (t n) -> p t n", t=T)
        cmask = consts1[:, CMASK].rearrange("p (t n) -> p t n", t=T)
        cany = consts1[:, CANY]
        cpos = consts1[:, CPOS].rearrange("p (v k) -> p v k", v=2)
        cb1 = consts1[:, CB1].rearrange("p (v n) -> p v n", v=2)
        cb2 = consts1[:, CB2].rearrange("p (v n) -> p v n", v=2)
        cw2 = consts1[:, CW2].rearrange("p (v k n) -> p v k n", v=2, k=2)
        kcg = consts1[:, KCG]

        cp = Columns()
        cp.take(2048)
        pq = area(cp, 16, S)
        sc = area(cp, T, PEER_HEADS, 2, NKEYS)
        srep = area(cp, 2, NKEYS)
        v16 = area(cp, T, PEER_HEADS, 2, TOPK)
        i16 = area(cp, T, PEER_HEADS, 2, TOPK, dt=U32)
        i16f = area(cp, T, PEER_HEADS, 2, TOPK)
        cand = area(cp, 2, TOPK, TOPK)
        tv = area(cp, T, PEER_HEADS, TOPK)
        ti = area(cp, T, PEER_HEADS * TOPK, dt=U32)
        tab = area(cp, 2, T, PEER_HEADS * TOPK, dt=U32)
        tabf = area(cp, 2, T, PEER_HEADS * TOPK)
        onehot16 = area(cp, PEER_HEADS * TOPK, TOPK)
        ex = area(cp, 2, T, PEER_HEADS * TOPK)
        gsum = area(cp, 2, T, PEER_HEADS)
        gates = arena[:, :].rearrange("p (i t) -> p i t", i=NKEYS)
        scratch = wring[:, 2, :]
        eT = scratch[:, 0:3 * S].rearrange("p (k t) -> p k t", k=3)
        hots = scratch[:, 768:2816].rearrange("p (b j w n) -> p b j w n", b=2, j=4, w=2)
        act_a = scratch[:, 2816:3328].rearrange("p (b t) -> p b t", b=2)
        wexp = scratch[:, 3328:3840].rearrange("p (b t) -> p b t", b=2)
        u_ring = wring[:, 0, :].rearrange("p (s k e) -> p s k e", s=4, k=KD)
        v_ring = wring[:, 1, :].rearrange("p (s n) -> p s n", s=4)

        c2 = Columns()
        c2.take(2048)
        qkv = area(c2, T, QKV)
        ff = area(c2, NF, S)
        qkT2 = area(c2, 10, S)
        oT = area(c2, KD, S)
        memory = area(c2, T, D)
        memT = area(c2, KD, S)
        kxT = area(c2, KD, S)
        vx = area(c2, T, D)
        cv = area(c2, 2, 2, S)
        SM2 = area(c2, 2, T, S)
        Pr2 = area(c2, 3, T, S)
        PT2 = area(c2, 2, T, S)
        wideg = area(c2, 2, D)
        hstat2 = area(c2, 3, T, 20)
        assert c2.at <= NKEYS * S
        qxT = arena[:, 2048:2048 + KD * S].rearrange("p (k t) -> p k t", k=KD)
        ff0 = 2048 + T * QKV
        sq2 = arena[:, ff0:ff0 + T * 1280].rearrange("p (t n) -> p t n", t=T)
        rtmp2 = arena[:, ff0 + 2560:ff0 + 2560 + 2560].rearrange("p (c h a j) -> p c h a j", c=4, h=20, a=2)
        poolT = arena[:, ff0 + NF * S:ff0 + NF * S + KD * S].rearrange("p (k t) -> p k t", k=KD)
        bandm = ff[:, 0:8, :]

        in_x, in_small, in_layer1 = sem("in_x"), sem("in_small"), sem("in_layer1")
        in_mem, in_band, in_wide = sem("in_mem"), sem("in_band"), sem("in_wide")
        w_landed = [sem(f"w_landed{s}") for s in range(SLOTS)]
        w_freed = sem("w_freed")
        u_landed = [sem(f"u_landed{s}") for s in range(4)]
        v_landed = [sem(f"v_landed{s}") for s in range(4)]
        bank_full = sem("bank_full")
        bank_freed = {"a": sem("bank_freed_by_scalar"), "d": sem("bank_freed_by_vector")}
        norm_sq, norm_root, norm_h, norm_t = sem("norm_sq"), sem("norm_root"), sem("norm_h"), sem("norm_t")
        norm_a, norm_d = sem("norm_out_by_scalar"), sem("norm_out_by_vector")
        wide_done, wide_out = sem("wide_done"), sem("wide_out")
        head_sq, head_sum, head_root, head_done = sem("head_sq"), sem("head_sum"), sem("head_root"), sem("head_done")
        gate3_done, merged_done = sem("gate3_done"), sem("merged_done")
        cmp_gelu, cmp_sum, cmp_root = sem("cmp_gelu"), sem("cmp_sum"), sem("cmp_root")
        cmp_key, cmp_less, cmp_exp, cmp_prob = sem("cmp_key"), sem("cmp_less"), sem("cmp_exp"), sem("cmp_prob")
        s_full, s_max, s_exp, s_prob = sem("scores_full"), sem("scores_max"), sem("scores_exp"), sem("scores_prob")
        t_full, t_out, y_full = sem("probsT_full"), sem("probsT_out"), sem("y_full")
        gate_less, gate_exp, ex_done = sem("gate_less"), sem("gate_exp"), sem("experts_done")
        hot_made, hot_full, hot_out = sem("hot_made"), sem("hot_full"), sem("hot_out")
        a_full, a_gelu, a_w, a_v = sem("a_full"), sem("a_gelu"), sem("a_weighted"), sem("a_times_v")
        conv_a, conv_d, conv_s, conv_m = sem("conv_mid"), sem("conv_sum"), sem("conv_silu"), sem("conv_mul")
        pool_done, final_h = sem("pool_done"), sem("final_h")
        chain = sem("vector_chain")
        stored = sem("stored")

        def bank(name):
            return PS[4 + GROUP[name] % RING]

        def wait_full(eng, name):
            eng.wait_ge(bank_full, sum(1 for n, _ in GROUPS[:GROUP[name] + 1] if n[0] not in ("ya", "yb", "y2", "yx")))

        def wait_freed(eng, name):
            who, count = freed(GROUP[name])
            eng.wait_ge(bank_freed[who], count)

        def wait_normed(eng, name):
            i = TURNED.index(name) + 1
            eng.wait_ge(norm_a, 4 * i)
            eng.wait_ge(norm_d, 4 * i)

        def wait_wide(eng, name):
            eng.wait_ge(wide_out, 4 * (WIDE.index(name) + 1))

        def tok(t):
            return slice(t * P, (t + 1) * P)

        def a_jobs():
            for h in range(A_HEADS):
                b = slice(HD * (h % 2), HD * (h % 2) + HD)
                yield dict(
                    q=lambda t, h=h, b=b: [qkT[b, h // 2, tok(t)]], k=[qkT[b, 8 + h // 2, :]], masked=True, gate=None,
                    v=lambda kt, h=h: [proj[:, kt, AV + h * HD:AV + (h + 1) * HD]], rows=b, cmp=None,
                    y=("ya", h // 2), first=True, last=h % 2 == 1, dest=(yT[:, 0, h // 2, :],))

        def b_jobs():
            for r in range(4):
                for g in range(KV_HEADS):
                    b, h = slice(HD * g, HD * g + HD), 4 * g + r
                    for j, (slot, vat) in enumerate(((12, VS), (13, VW))):
                        yield dict(
                            q=lambda t, r=r, b=b: [qkT[b, 4 + r, tok(t)]], k=[qkT[b, slot, :]], masked=True,
                            gate=lambda t, h=h, j=j: gate3[:, t, 3 * h + 1 + j:3 * h + 2 + j],
                            v=lambda kt, g=g, vat=vat: [proj[:, kt, vat + g * HD:vat + (g + 1) * HD]], rows=b,
                            cmp=(g, h) if j == 0 else None, y=("yb", r), first=j == 0, last=(g, j) == (1, 1),
                            dest=(yT[:, 1, r, :],))

        def self_jobs():
            for p in range(8):
                for i in range(2):
                    b, kv = slice(HD * i, HD * i + HD), 2 * (p // 4) + i
                    vat = (N_HEADS + N_KV + kv) * HD
                    yield dict(
                        q=lambda t, p=p, b=b: [qkT2[b, p, tok(t)]], k=[qkT2[b, 8 + p // 4, :]], masked=False, gate=None,
                        v=lambda kt, vat=vat: [qkv[:, kt, vat:vat + HD]], rows=b, cmp=None,
                        y=("y2", p), first=True, last=i == 1, dest=(oT[:, p, :],))

        def cross_jobs(i):
            for h in range(X_HEADS):
                yield dict(
                    q=lambda t, h=h: [qxT[:, 2 * h + d, tok(t)] for d in range(2)],
                    k=[kxT[:, 2 * h + d, :] for d in range(2)], masked=False, gate=None,
                    v=lambda kt, h=h: [vx[:, kt, (2 * h + d) * P:(2 * h + d + 1) * P] for d in range(2)],
                    rows=slice(0, P), cmp=None, y=("yx", i, h), first=True, last=True,
                    dest=(oT[:, 2 * h, :], oT[:, 2 * h + 1, :]))

        USES = {
            "a": (list(a_jobs()), SMx, Pr, PT, HD ** -0.5), "b": (list(b_jobs()), SMx, Pr, PT, HD ** -0.5),
            "self": (list(self_jobs()), None, Pr2, PT2, HD ** -0.5),
            "x0": (list(cross_jobs(0)), None, Pr2, PT2, X_HD ** -0.5),
            "x1": (list(cross_jobs(1)), None, Pr2, PT2, X_HD ** -0.5),
        }

        block = ctx.enter_context(nc.Block())

        @block.sync
        def _(sp):
            def load_static(n):
                if n >= SLOTS:
                    sp.wait_ge(w_freed, n - SLOTS + 1)
                sp.dma_start(wring[:, n % SLOTS, :], weights[n]).then_inc(w_landed[n % SLOTS], 16)

            def load_many(n0, n1):
                while n0 < n1 and (n0 % SLOTS or n0 < SLOTS):
                    load_static(n0)
                    n0 += 1
                turns = (n1 - n0) // SLOTS
                if turns > 0:
                    with sp.Fori(n0 // SLOTS, n0 // SLOTS + turns) as i:
                        for s in range(SLOTS):
                            sp.wait_ge(w_freed, i * SLOTS + (s - SLOTS + 1))
                            sp.dma_start(wring[:, s, :], weights[i * SLOTS + s]).then_inc(w_landed[s], 16)
                for n in range(n0 + turns * SLOTS, n1):
                    load_static(n)

            sp.dma_start(X[:, :, :], x.rearrange("b (t p) d -> p (b t) d", p=P)).then_inc(in_x, 16)
            sp.dma_start(smalls[:, :], small).then_inc(in_small, 16)
            load_static(0)
            sp.dma_start(consts1[:, :], layer1).then_inc(in_layer1, 16)
            load_many(1, FIRST2)
            sp.wait_ge(w_freed, FIRST2)

            def load_experts(e, s):
                sp.dma_start(u_ring[:, s, :, :].rearrange("p k e -> p (k e)"), expert_u[e]).then_inc(u_landed[s], 16)
                sp.dma_start(v_ring[:, s, :], expert_v[e]).then_inc(v_landed[s], 16)

            for s in range(4):
                load_experts(s, s)
            with sp.Fori(1, NKEYS // 4) as i:
                for s in range(4):
                    sp.wait_ge(a_v, i * 4 + (s - 2))
                    load_experts(i * 4 + s, s)
            wait_wide(sp, "peer")
            sp.dma_start(memory[:, :, :], mem.rearrange("b (t p) d -> p (b t) d", p=P)).then_inc(in_mem, 16)
            load_many(FIRST2, FIRST2 + 2)
            sp.dma_start(wideg[:, :, :], wide_gains).then_inc(in_wide, 16)
            load_many(FIRST2 + 2, len(BLOCKS))
            sp.wait_ge(final_h, 2)
            sp.dma_start(out.rearrange("b (t p) d -> p (b t) d", p=P), H[:, :, :]).then_inc(stored, 16)
            sp.wait_ge(stored, 16)

        @block.tensor
        def _(pe):
            state = {"frees": 0}

            def mm(out, lhsT, rhs, start, stop):
                ins = pe.matmul(out, lhsT, rhs, start=start, stop=stop)
                if state["frees"]:
                    ins.then_inc(w_freed, state["frees"])
                    state["frees"] = 0
                return ins

            def weights_of(name, frees=1):
                n = BLOCK[name]
                pe.wait_ge(w_landed[n % SLOTS], 16 * (n // SLOTS + 1))
                state["frees"] = frees if n not in (0, FIRST2) else 0
                return wring[:, n % SLOTS, :]

            def open_bank(name):
                q = GROUP[name]
                if q >= RING:
                    wait_freed(pe, GROUPS[q - RING][0])
                return PS[4 + q % RING]

            def norm(name):
                pe.wait_ge(norm_h, 2 * (NORMS.index(name) + 1))
                for b in range(4):
                    for k in range(2):
                        for t in range(T):
                            c = 2 * b + k
                            ins = pe.transpose(PS[b][:, (k * T + t) * P:(k * T + t + 1) * P],
                                               H[:, t, c * P:(c + 1) * P], ident)
                    ins.then_inc(norm_t, 1)

            def feature_major(names, blocks, src, tiles_per_block, kd=KD):
                tiles = 2 * len(names)
                for c in range(tiles):
                    if c % tiles_per_block == 0:
                        w = weights_of(blocks[c // tiles_per_block]).rearrange("p (k n) -> p k n", k=kd)
                    if c % 2 == 0:
                        b = open_bank(names[c // 2])
                    at = (c % tiles_per_block) * P
                    for k in range(kd):
                        ins = mm(b[:, (c % 2) * S:(c % 2 + 1) * S], w[:, k, at:at + P], src[:, k, :], k == 0, k == kd - 1)
                    if c % 2:
                        ins.then_inc(bank_full, 1)

            def token_major(names, blocks, src):
                for n, blk in enumerate(blocks):
                    w = weights_of(blk).rearrange("p (k n) -> p k n", k=KD)
                    for t in range(T):
                        b = open_bank(names[n * T + t])
                        for k in range(KD):
                            ins = mm(b[:, :], src[:, k, tok(t)], w[:, k, :], k == 0, k == KD - 1)
                        ins.then_inc(bank_full, 1)

            def wide(name, blocks, src, kt):
                if WIDE.index(name):
                    wait_wide(pe, WIDE[WIDE.index(name) - 1])
                for k in range(kt):
                    if k % 4 == 0:
                        w = weights_of(blocks[k // 4]).rearrange("p (k n) -> p k n", k=4)
                    for t in range(T):
                        for h in range(2):
                            ins = mm(PS[2 * t + h][:, :], src(k, t), w[:, k % 4, h * 512:(h + 1) * 512],
                                     k == 0, k == kt - 1)
                ins.then_inc(wide_done, 1)

            def attention(use):
                jobs, _, Pb, Tb, _ = USES[use]
                j0, n = JOBS[use], len(jobs)
                for step in range(n + 2):
                    if step < n:
                        job, j = jobs[step], j0 + step
                        if step >= 2:
                            pe.wait_ge(s_exp, j - 1)
                        for t in range(T):
                            qs = job["q"](t)
                            for d, q in enumerate(qs):
                                ins = mm(PS[j % 2][:, t * S:(t + 1) * S], q, job["k"][d], d == 0, d == len(qs) - 1)
                        ins.then_inc(s_full, 1)
                    if 1 <= step <= n:
                        j = j0 + step - 1
                        pe.wait_ge(s_prob, j + 1)
                        if step >= 3:
                            pe.wait_ge(t_out, j - 1)
                        for kt in range(T):
                            for t in range(T):
                                ins = pe.transpose(PS[2 + j % 2][:, kt * S + t * P:kt * S + (t + 1) * P],
                                                   Pb[:, j % 3, t, kt * P:(kt + 1) * P], ident)
                        ins.then_inc(t_full, 1)
                    if step >= 2:
                        job, j = jobs[step - 2], j0 + step - 2
                        if step == 2 or jobs[step - 3]["y"] != job["y"]:
                            b = open_bank(job["y"])
                        if job["cmp"] is not None:
                            g, h = job["cmp"]
                            wait_freed(pe, ("pct", h // 2))
                            mm(b[job["rows"], 0:S], kvc[0:N_CMP, 1, g, :], pcT[0:N_CMP, h, :], True, False)
                        pe.wait_ge(t_out, j + 1)
                        dn = len(job["dest"])
                        for d in range(dn):
                            for kt in range(T):
                                first = job["first"] and job["cmp"] is None
                                more = job["y"][0] == "yb" and not (job["cmp"] is None)
                                ins = mm(b[job["rows"], d * S:(d + 1) * S], job["v"](kt)[d], Tb[:, j % 2, kt, :],
                                         first and kt == 0, kt == T - 1 and not more)
                        ins.then_inc(y_full, 1)

            pe.wait_ge(in_small, 16)
            norm("norm1")
            wait_normed(pe, "norm1")
            token_major([("win", n, t) for n in range(N_WIN) for t in range(T)], [("win", n) for n in range(N_WIN)], HT)
            for kv, at in enumerate((KC, VC)):
                b = open_bank(("win2", kv))
                wait_freed(pe, ("win", N_WIN - 1, 0))
                wait_freed(pe, ("win", N_WIN - 1, 1))
                for g in range(KV_HEADS):
                    for par in range(2):
                        for t in range(T):
                            ins = mm(b[HD * par:HD * par + HD, g * P + t * HD:g * P + (t + 1) * HD],
                                     proj[:, t, at + g * HD:at + (g + 1) * HD], ident[:, par::2], True, True)
                ins.then_inc(bank_full, 1)

            def merge_gates(gs):
                for g in gs:
                    if g % 2 == 0:
                        state["mg"] = weights_of(("mg", g // 2)).rearrange("p (k n) -> p k n", k=KD)
                    w, b = state["mg"], open_bank(("mg", g))
                    for c in range(2):
                        at = (2 * (g % 2) + c) * P
                        for k in range(KD):
                            ins = mm(b[:, c * S:(c + 1) * S], w[:, k, at:at + P], HT[:, k, :], k == 0, k == KD - 1)
                    ins.then_inc(bank_full, 1)

            merge_gates(range(4))
            for kv in range(2):
                w = weights_of(("cmp", kv)).rearrange("p (k n) -> p k n", k=16)
                b = open_bank(("hid", kv))
                wait_freed(pe, ("win2", kv))
                for k in range(16):
                    ins = mm(b[0:2 * N_CMP, 0:CMP_HID], blocksT[:, kv, k, :, :].rearrange("p g n -> p (g n)"), w[:, k, :],
                             k == 0, k == 15)
                ins.then_inc(bank_full, 1)
            merge_gates([4])
            pe.wait_ge(in_layer1, 16)
            for kv in range(2):
                b = open_bank(("hidT", kv))
                pe.wait_ge(cmp_gelu, kv + 1)
                for k in range(2):
                    ins = pe.transpose(b[:, k * 32:k * 32 + 2 * N_CMP], hid[0:2 * N_CMP, kv, k * P:(k + 1) * P],
                                       ident[0:2 * N_CMP, 0:2 * N_CMP])
                ins.then_inc(bank_full, 1)
            merge_gates([5])
            for kv in range(2):
                b = open_bank(("c2", kv))
                wait_freed(pe, ("hidT", kv))
                for g in range(KV_HEADS):
                    for k in range(2):
                        ins = mm(b[0:N_CMP, g * HD:(g + 1) * HD], hidT[:, kv, k, g * N_CMP:(g + 1) * N_CMP],
                                 cw2[:, kv, k, :], k == 0, k == 1)
                ins.then_inc(bank_full, 1)
            merge_gates([6])
            b = open_bank(("kcT",))
            pe.wait_ge(cmp_key, 1)
            for g in range(KV_HEADS):
                ins = mm(b[HD * g:HD * g + HD, 0:N_CMP], kvc[0:N_CMP, 0, g, :], ident[0:N_CMP, 0:N_CMP], True, True)
            ins.then_inc(bank_full, 1)
            merge_gates([7])
            pe.wait_ge(head_done, 1)
            for m in range(7):
                b = open_bank(("qkt", m))
                for s in range(2):
                    for t in range(T):
                        ins = pe.transpose(b[:, s * S + t * P:s * S + (t + 1) * P],
                                           proj[:, t, (2 * m + s) * P:(2 * m + s + 1) * P], ident)
                ins.then_inc(bank_full, 1)
            wait_freed(pe, ("qkt", 3))
            wait_freed(pe, ("kcT",))
            for h in range(B_HEADS):
                g, r = h // 4, h % 4
                if r == 0:
                    b = open_bank(("scmp", g))
                for t in range(T):
                    ins = mm(b[:, (2 * r + t) * 16:(2 * r + t) * 16 + N_CMP], qkT[HD * g:HD * g + HD, 4 + r, tok(t)],
                             kcT[HD * g:HD * g + HD, 0:N_CMP], True, True)
                if r == 3:
                    ins.then_inc(bank_full, 1)
            wait_freed(pe, ("qkt", 6))
            pe.wait_ge(cmp_prob, 1)
            for m in range(4):
                b = open_bank(("pct", m))
                for s in range(2):
                    for t in range(T):
                        ins = pe.transpose(b[0:N_CMP, s * S + t * P:s * S + (t + 1) * P],
                                           scmp[:, (2 * m + s) * T + t, 0:N_CMP], ident)
                ins.then_inc(bank_full, 1)
            attention("a")
            attention("b")
            wa = weights_of(("up", 0)).rearrange("p (k n) -> p k n", k=4)
            frees = state["frees"]
            wb = weights_of(("up", 1), 0).rearrange("p (k n) -> p k n", k=4)
            state["frees"] = frees
            wait_freed(pe, ("yb", 3))
            for f in range(KD):
                b = open_bank(("up", f))
                for br, w in enumerate((wa, wb)):
                    for k in range(4):
                        ins = mm(b[:, br * S:(br + 1) * S], w[:, k, f * P:(f + 1) * P], yT[:, br, k, :], k == 0, k == 3)
                ins.then_inc(bank_full, 1)
            pe.wait_ge(merged_done, KD)
            w_out_frees = 2
            for k in range(KD):
                if k % 4 == 0:
                    w = weights_of(("out", k // 4), w_out_frees).rearrange("p (k n) -> p k n", k=4)
                    w_out_frees = 1
                for t in range(T):
                    for h in range(2):
                        ins = mm(PS[2 * t + h][:, :], merged[:, k, tok(t)], w[:, k % 4, h * 512:(h + 1) * 512],
                                 k == 0, k == KD - 1)
            ins.then_inc(wide_done, 1)

            norm("norm2")
            wait_normed(pe, "norm2")
            feature_major([("pq", g) for g in range(8)], [("wq", n) for n in range(4)], HT, 4)
            state["frees"] = 1
            for m in range(8):
                t, hp = m // 4, m % 4
                b = open_bank(("sc", m))
                wait_freed(pe, ("pq", 2 * hp + 1))
                for s in range(4):
                    ins = mm(b[:, s * P:(s + 1) * P], pq[:, 4 * hp + s, tok(t)], pkeys[:, s % 2, :], True, True)
                ins.then_inc(bank_full, 1)
            pe.wait_ge(ex_done, 1)
            for m in range(3):
                b = open_bank(("et", m))
                for t in range(T):
                    src = ex[:, m, t, :] if m < 2 else tv[:, t, :, :].rearrange("p h k -> p (h k)")
                    ins = pe.transpose(b[:, tok(t)], src, ident)
                ins.then_inc(bank_full, 1)
            pe.sem_inc(hot_full, 1)
            with pe.Fori(0, S // 8) as i:
                for half in range(2):
                    pe.wait_ge(hot_made, i * 2 + (half + 1))
                    pe.wait_ge(hot_out, i * 2 + half)
                    for j in range(4):
                        ins = pe.matmul(PS[half][:, j * P:(j + 1) * P], hots[:, half, j, 0, :], hots[:, half, j, 1, :],
                                        start=True, stop=True)
                    ins.then_inc(hot_full, 1)
            pe.wait_ge(hot_out, 1 + S // 4)

            def times_u(e, s, turn):
                pe.wait_ge(u_landed[s], turn)
                pe.wait_ge(a_gelu, e)
                for k in range(KD):
                    ins = pe.matmul(PS[s % 2][:, 0:S], u_ring[:, s, k, :], HT[:, k, :], start=k == 0, stop=k == KD - 1)
                ins.then_inc(a_full, 1)

            def times_v(e, s, turn, stop=False):
                pe.wait_ge(v_landed[s], turn)
                pe.wait_ge(a_w, e + 2)
                for t in range(T):
                    for h in range(2):
                        ins = pe.matmul(PS[4 + 2 * t + h][:, :], wexp[:, s % 2, tok(t)], v_ring[:, s, h * 512:(h + 1) * 512],
                                        start=False, stop=stop, skip_group_check=True)
                ins.then_inc(a_v, 1)

            pe.wait_ge(a_w, 1)
            for b in range(4):
                ins = pe.matmul(PS[4 + b][:, :], wexp[:, 0, 0:P], hots[:, 0, 0:2, :, :].rearrange("p j w n -> p (j w n)"),
                                start=True, stop=False, skip_group_check=True)
            ins.then_inc(a_v, 1)
            turns = NKEYS // 4
            times_u(0, 0, 16)
            with pe.Fori(0, turns - 1) as i:
                for s in range(4):
                    nxt = (s + 1) % 4
                    times_u(i * 4 + s, nxt, i * 16 + (16 if s < 3 else 32))
                    times_v(i * 4 + s, s, i * 16 + 16)
            for s in range(4):
                e = NKEYS - 4 + s
                if s < 3:
                    times_u(e, s + 1, 16 * turns)
                times_v(e, s, 16 * turns, stop=True)

            wait_wide(pe, "peer")
            norm("attn")
            wait_normed(pe, "attn")
            token_major([("qkv", n, t) for n in range(3) for t in range(T)], [("qkv", n) for n in range(3)], HT)
            norm("mem0")
            for i in range(DEPTH2):
                wait_normed(pe, f"mem{i}")
                feature_major([("xk", i, g) for g in range(4)], [("xk", i, n) for n in range(2)], memT, 4)
                wide(f"xv{i}", [("xv", i, n) for n in range(2)], lambda k, t: memT[:, k, tok(t)], KD)
                if i == 0:
                    pe.wait_ge(head_done, 2)
                    for m in range(5):
                        b = open_bank(("qkt2", m))
                        for s in range(2):
                            for t in range(T):
                                ins = pe.transpose(b[:, s * S + t * P:s * S + (t + 1) * P],
                                                   qkv[:, t, (2 * m + s) * P:(2 * m + s + 1) * P], ident)
                        ins.then_inc(bank_full, 1)
                    wait_freed(pe, ("qkt2", 4))
                    wait_wide(pe, "xv0")
                    attention("self")
                    wait_freed(pe, ("y2", 7))
                    wide("wo", [("wo", n) for n in range(2)], lambda k, t: oT[:, k, tok(t)], KD)
                else:
                    pe.wait_ge(norm_h, 2 * (NORMS.index("pool") + 1))
                    pe.wait_ge(in_band, 16)
                    for g in range(4):
                        b = open_bank(("pm", g))
                        for c in range(2):
                            for s in range(T):
                                at = (2 * g + c) * P
                                ins = mm(b[:, c * S:(c + 1) * S], H[:, s, at:at + P], bandm[:, 2 * g + s, :], s == 0, s == 1)
                        ins.then_inc(bank_full, 1)
                    w = weights_of(("pool", 0))[:, 0:4 * 2 * S].rearrange("p (g c n) -> p g c n", g=4, c=2)
                    wait_freed(pe, ("pm", 3))
                    for t in range(T):
                        for g2 in range(2):
                            b = open_bank(("py", t, g2))
                            for u in range(2):
                                for c in range(2):
                                    gg = 2 * g2 + u
                                    ins = mm(b[:, u * S:(u + 1) * S], poolT[:, 2 * gg + c, tok(t)], w[:, gg, c, :], c == 0, c == 1)
                            ins.then_inc(bank_full, 1)
                norm(f"x{i}")
                wait_normed(pe, f"x{i}")
                feature_major([("xq", i, g) for g in range(4)], [("xq", i, n) for n in range(2)], HT, 4)
                wait_freed(pe, ("xq", i, 3))
                wait_wide(pe, f"xv{i}")
                attention(f"x{i}")
                wait_freed(pe, ("yx", i, 3))
                wide(f"xo{i}", [("xo", i, n) for n in range(2)], lambda k, t: oT[:, k, tok(t)], KD)
                norm(f"ffn{i}")
                wait_normed(pe, f"ffn{i}")
                if i == 0:
                    norm("mem1")
                for f in range(NF):
                    if f % 2 == 0:
                        w = weights_of(("ffu", i, f // 2)).rearrange("p (k c n) -> p k c n", k=KD, c=4)
                    b = open_bank(("ffu", i, f))
                    for c in range(2):
                        for k in range(KD):
                            ins = mm(b[:, c * S:(c + 1) * S], w[:, k, 2 * (f % 2) + c, :], HT[:, k, :], k == 0, k == KD - 1)
                    ins.then_inc(bank_full, 1)
                if i == 0:
                    wait_normed(pe, "mem1")
                pe.wait_ge(conv_m, NF * (i + 1))
                wide(f"ffd{i}", [("ffd", i, n) for n in range(-(-NF // 4))], lambda k, t: ff[:, k, tok(t)], NF)

        @block.scalar
        def _(act):
            def norm_sums(name, src):
                i = NORMS.index(name)
                if i:
                    before = [n for n in NORMS[:i] if n in TURNED]
                    act.wait_ge(norm_t, 4 * len(before))
                for t in range(T):
                    act.activation(H[:, t, :], src[:, t, :], ACT.Square, accum_out=stat[:, t:t + 1]).then_inc(norm_sq, 1)
                act.wait_ge(norm_sq, 2 * i + 2)
                act.activation(stat[:, 2:4], stat[:, 0:2], ACT.Sqrt, bias=eps, scale=1.0 / D).then_inc(norm_root, 1)

            def norm_out(name, dst):
                i, n = TURNED.index(name), NORMS.index(name)
                for b in (1, 3):
                    act.wait_ge(norm_t, 4 * i + b + 1)
                    for c in (2 * b, 2 * b + 1):
                        act.activation(dst[:, c, :], PS[b][:, (c % 2) * S:(c % 2 + 1) * S], ACT.Copy,
                                       scale=gains[:, n, c:c + 1]).then_inc(norm_a, 1)

            def copy_bank(name, dst, width=512, rows=P):
                wait_full(act, name)
                src = bank(name)[0:rows, 0:width]
                if len(dst.shape) == 3:
                    src = src.rearrange("p (a b) -> p a b", a=dst.shape[1])
                act.activation(dst, src, ACT.Copy).then_inc(bank_freed["a"], 1)

            def attention(use):
                jobs, Sb, Pb, Tb, scale = USES[use]
                j0, n = JOBS[use], len(jobs)
                for step in range(n + 1):
                    if step < n:
                        j = j0 + step
                        act.wait_ge(s_max, j + 1)
                        if step >= 3:
                            act.wait_ge(t_full, j - 2)
                        for t in range(T):
                            src = Sb[:, j % 2, t, :] if Sb is not None else PS[j % 2][:, t * S:(t + 1) * S]
                            ins = act.activation(Pb[:, j % 3, t, :], src, ACT.Exp, bias=att[:, 1, j % 4, t:t + 1], scale=scale,
                                                 accum_out=att[:, 2, j % 4, t:t + 1])
                        ins.then_inc(s_exp, 1)
                    if step >= 1:
                        j = j0 + step - 1
                        act.wait_ge(t_full, j + 1)
                        if step >= 3:
                            act.wait_ge(y_full, j - 1)
                        act.activation(Tb[:, j % 2, :, :], PS[2 + j % 2][:, :].rearrange("p (a b) -> p a b", a=T),
                                       ACT.Copy).then_inc(t_out, 1)

            act.wait_ge(in_x, 16)
            act.wait_ge(in_small, 16)
            norm_sums("norm1", X)
            norm_out("norm1", HT)
            for n in range(N_WIN):
                width = min(512, PROJ - 512 * n)
                copy_bank(("win", n, 1), proj[:, 1, 512 * n:512 * n + width], width)
                if n == NORMED // 512:
                    wait_freed(act, ("win", n, 0))
                    wait_freed(act, ("win", n, 1))
                    act.activation(sq1, proj[:, :, 0:NORMED], ACT.Square).then_inc(head_sq, 1)
            wait_freed(act, ("win", N_WIN - 1, 0))
            wait_freed(act, ("win", N_WIN - 1, 1))
            act.wait_ge(head_sum, 1)
            act.activation(hstat1[:, 1, :, :], hstat1[:, 0, :, :], ACT.Sqrt, bias=eps, scale=1.0 / HD).then_inc(head_root, 1)
            act.activation(gate3[:, :, :], proj[:, :, BG:PROJ], ACT.Sigmoid).then_inc(gate3_done, 1)

            def merge_gates(gs):
                for g in gs:
                    wait_full(act, ("mg", g))
                    for c in range(2):
                        n = 2 * g + c
                        ins = act.activation(mgate[:, n % KD, n // KD, :], bank(("mg", g))[:, c * S:(c + 1) * S],
                                             ACT.Sigmoid, bias=smalls[:, BMERGE][:, n:n + 1])
                    ins.then_inc(bank_freed["a"], 1)

            merge_gates(range(4))
            merge_gates([4])
            for kv in range(2):
                wait_freed(act, ("hid", kv))
                act.activation(hid[0:2 * N_CMP, kv, :], hid[0:2 * N_CMP, kv, :], ACT.Gelu_apprx_tanh).then_inc(cmp_gelu, 1)
            merge_gates([5])
            merge_gates([6])
            act.wait_ge(cmp_sum, 1)
            act.activation(cst[0:N_CMP, 1, :], cst[0:N_CMP, 0, :], ACT.Sqrt, bias=eps[0:N_CMP], scale=1.0 / HD).then_inc(cmp_root, 1)
            merge_gates([7])
            for m in range(7):
                copy_bank(("qkt", m), qkT[:, 2 * m:2 * m + 2, :])
            act.wait_ge(cmp_less, 1)
            act.activation(scmp[:, :, 0:N_CMP], scmp[:, :, 0:N_CMP], ACT.Exp, scale=HD ** -0.5).then_inc(cmp_exp, 1)
            for m in range(4):
                copy_bank(("pct", m), pcT[0:N_CMP, 2 * m:2 * m + 2, :], rows=N_CMP)
            attention("a")
            attention("b")

            wait_wide(act, "out")
            norm_sums("norm2", X)
            norm_out("norm2", HT)
            for g in range(8):
                copy_bank(("pq", g), pq[:, 2 * g:2 * g + 2, :])
            for m in range(8):
                t, hp = m // 4, m % 4
                copy_bank(("sc", m), sc[:, t, 2 * hp:2 * hp + 2, :, :].rearrange("p h s n -> p (h s n)"))
            act.wait_ge(gate_less, 1)
            act.activation(tv[:, :, :, :], tv[:, :, :, :], ACT.Exp).then_inc(gate_exp, 1)
            for m in range(3):
                copy_bank(("et", m), eT[:, m, :], S)
            act.sem_inc(hot_out, 1)
            with act.Fori(0, S // 8) as i:
                for half in range(2):
                    act.wait_ge(hot_full, i * 2 + (half + 2))
                    act.activation(gates[:, :, bass.ds(i * 8 + 4 * half, 4)].rearrange("p i t -> p t i"),
                                   PS[half][:, :].rearrange("p (t i) -> p t i", t=4), ACT.Copy).then_inc(hot_out, 1)
            act.wait_ge(hot_out, 1 + S // 4)
            with act.Fori(0, NKEYS // 4) as i:
                for s in range(4):
                    act.wait_ge(a_full, i * 4 + (s + 1))
                    act.wait_ge(a_w, i * 4 + s)
                    act.activation(act_a[:, s % 2, :], PS[s % 2][:, 0:S], ACT.Gelu_apprx_tanh).then_inc(a_gelu, 1)

            wait_wide(act, "peer")
            norm_sums("attn", X)
            norm_out("attn", HT)
            act.wait_ge(in_mem, 16)
            norm_sums("mem0", memory)
            for n in range(3):
                copy_bank(("qkv", n, 1), qkv[:, 1, 512 * n:512 * (n + 1)])
            norm_out("mem0", memT)
            for i in range(DEPTH2):
                if i == 0:
                    wait_freed(act, ("qkv", 2, 0))
                    wait_freed(act, ("qkv", 2, 1))
                    act.activation(sq2, qkv[:, :, 0:1280], ACT.Square).then_inc(head_sq, 1)
                else:
                    wait_wide(act, "ffd0")
                    act.dma_start(bandm, band).then_inc(in_band, 16)
                    norm_sums("pool", X)
                for g in range(4):
                    copy_bank(("xk", i, g), kxT[:, 2 * g:2 * g + 2, :])
                    if i == 0 and g == 0:
                        act.wait_ge(head_sum, 2)
                        act.activation(hstat2[:, 1, :, :], hstat2[:, 0, :, :], ACT.Sqrt, bias=eps,
                                       scale=1.0 / HD).then_inc(head_root, 1)
                if i == 0:
                    for m in range(5):
                        copy_bank(("qkt2", m), qkT2[:, 2 * m:2 * m + 2, :])
                    attention("self")
                    wait_wide(act, "wo")
                else:
                    for g in range(4):
                        wait_full(act, ("pm", g))
                        for c in range(2):
                            ct = 2 * g + c
                            ins = act.activation(poolT[:, ct, :], bank(("pm", g))[:, c * S:(c + 1) * S], ACT.Copy,
                                                 scale=gains[:, NORMS.index("pool"), ct:ct + 1])
                        ins.then_inc(bank_freed["a"], 1)
                    act.wait_ge(pool_done, 4)
                norm_sums(f"x{i}", X)
                norm_out(f"x{i}", HT)
                for g in range(4):
                    copy_bank(("xq", i, g), qxT[:, 2 * g:2 * g + 2, :])
                attention(f"x{i}")
                wait_wide(act, f"xo{i}")
                norm_sums(f"ffn{i}", X)
                norm_out(f"ffn{i}", HT)
                if i == 0:
                    norm_sums("mem1", memory)
                    norm_out("mem1", memT)
                for f in range(NF + 1):
                    if f < NF:
                        wait_full(act, ("ffu", i, f))
                        if f >= 2:
                            act.wait_ge(conv_m, NF * i + f - 1)
                        for c in range(2):
                            w = conv[:, i, c * NF + f, :]
                            ins = act.activation(cv[:, f % 2, c, :], bank(("ffu", i, f))[:, c * S:(c + 1) * S], ACT.Identity,
                                                 bias=w[:, 3:4], scale=w[:, 1:2])
                        ins.then_inc(conv_a, 1)
                    if f:
                        act.wait_ge(conv_d, NF * i + f)
                        g = (f - 1) % 2
                        act.activation(cv[:, g, 0, :], cv[:, g, 0, :], ACT.Silu).then_inc(conv_s, 1)
            wait_wide(act, "ffd1")
            norm_sums("final", X)

        @block.vector
        def _(dve):
            links = [0]

            def link(ins):
                ins.then_inc(chain, 1)
                links[0] += 1
                dve.wait_ge(chain, links[0])

            def norm_scale(name, src):
                i = NORMS.index(name)
                dve.wait_ge(norm_root, i + 1)
                link(dve.reciprocal(stat[:, 4:6], stat[:, 2:4]))
                for t in range(T):
                    dve.tensor_scalar(H[:, t, :], src[:, t, :], stat[:, 4 + t:5 + t], None, ALU.mult).then_inc(norm_h, 1)

            def norm_out(name, dst):
                i, n = TURNED.index(name), NORMS.index(name)
                for b in (0, 2):
                    dve.wait_ge(norm_t, 4 * i + b + 1)
                    for c in (2 * b, 2 * b + 1):
                        dve.tensor_scalar(dst[:, c, :], PS[b][:, (c % 2) * S:(c % 2 + 1) * S], gains[:, n, c:c + 1], None,
                                          ALU.mult).then_inc(norm_d, 1)

            def copy_bank(name, dst, src):
                wait_full(dve, name)
                dve.tensor_copy(dst, src).then_inc(bank_freed["d"], 1)

            def wide_read(name, dst, add):
                dve.wait_ge(wide_done, sum(1 for n in WIDE[:WIDE.index(name) + 1] if n != "peer"))
                for t in range(T):
                    for h in range(2):
                        o = dst[:, t, h * 512:(h + 1) * 512]
                        b = PS[2 * t + h][:, :]
                        ins = dve.tensor_tensor(o, o, b, ALU.add) if add else dve.tensor_copy(o, b)
                        ins.then_inc(wide_out, 1)

            def head_norm(k, heads, st, kinds, rope):
                sq, hd = heads
                n = hd.shape[2] // HD
                hv = hd.rearrange("p t (h d) -> p t h d", d=HD)
                dve.wait_ge(head_sq, k + 1)
                dve.tensor_reduce(st[:, 0, :, :], sq.rearrange("p t (h d) -> p t h d", d=HD), AXX, ALU.add).then_inc(head_sum, 1)
                dve.wait_ge(head_root, k + 1)
                link(dve.reciprocal(st[:, 2, :, :], st[:, 1, :, :]))
                link(dve.tensor_tensor(hv, hv, st[:, 2, :, :].unsqueeze(3).to_broadcast([P, T, n, HD]), ALU.mult))
                at = 0
                for m, gain in kinds:
                    v = hv[:, :, at:at + m, :]
                    ins = dve.tensor_tensor(v, v, gain.unsqueeze(1).unsqueeze(1).to_broadcast([P, T, m, HD]), ALU.mult)
                    at += m
                link(ins)
                rope(hv)

            def rotate(x1, x2, c, s, tmp):
                dve.tensor_tensor(tmp[0], x1, c, ALU.mult)
                dve.tensor_tensor(tmp[1], x2, s, ALU.mult)
                dve.tensor_tensor(tmp[2], x2, c, ALU.mult)
                link(dve.tensor_tensor(tmp[3], x1, s, ALU.mult))
                dve.tensor_tensor(x1, tmp[0], tmp[1], ALU.subtract)
                return dve.tensor_tensor(x2, tmp[2], tmp[3], ALU.add)

            def rope_first(hv):
                c, s = (rope1[:, w, :, :].unsqueeze(2).to_broadcast([P, T, N_NORMED, 8]) for w in range(2))
                rotate(hv[:, :, :, 0:8], hv[:, :, :, 8:16], c, s, [rtmp1[:, w] for w in range(4)]).then_inc(head_done, 1)

            def rope_axial(hv):
                for t in range(T):
                    h2 = hv[:, t, :, :].rearrange("p h (a x j) -> p h a x j", a=2, x=2)
                    c, s = (rope2[:, w, t, :, :].unsqueeze(1).to_broadcast([P, 20, 2, 16]) for w in range(2))
                    ins = rotate(h2[:, :, :, 0, :], h2[:, :, :, 1, :], c, s, [rtmp2[:, w] for w in range(4)])
                    if t == T - 1:
                        ins.then_inc(head_done, 1)
                    else:
                        link(ins)

            def attention(use):
                jobs, Sb, Pb, Tb, scale = USES[use]
                j0, n = JOBS[use], len(jobs)
                for step in range(n + 3):
                    if step < n:
                        j = j0 + step
                        dve.wait_ge(s_full, j + 1)
                        if step >= 2:
                            dve.wait_ge(s_exp, j - 1)
                        mx = att[:, 0, j % 4, :]
                        b = PS[j % 2][:, :].rearrange("p (t n) -> p t n", t=T)
                        if Sb is not None:
                            for t in range(T):
                                ins = dve.tensor_tensor_reduce(Sb[:, j % 2, t, :], b[:, t, :], mask[:, t, :], 1.0, LOW, ALU.add,
                                                               ALU.max, mx[:, t:t + 1])
                            link(ins)
                        else:
                            link(dve.tensor_reduce(mx, b, AXX, ALU.max))
                        dve.tensor_scalar(att[:, 1, j % 4, :], mx, -scale, None, ALU.mult).then_inc(s_max, 1)
                    if 1 <= step <= n:
                        job, j = jobs[step - 1], j0 + step - 1
                        dve.wait_ge(s_exp, j + 1)
                        link(dve.reciprocal(att[:, 3, j % 4, :], att[:, 2, j % 4, :]))
                        for t in range(T):
                            r, p = att[:, 3, j % 4, t:t + 1], Pb[:, j % 3, t, :]
                            if job["gate"] is None:
                                ins = dve.tensor_scalar(p, p, r, None, ALU.mult)
                            else:
                                ins = dve.tensor_scalar(p, p, r, job["gate"](t), ALU.mult, ALU.mult)
                        ins.then_inc(s_prob, 1)
                    if step >= 3 and jobs[step - 3]["last"]:
                        job, j = jobs[step - 3], j0 + step - 3
                        dve.wait_ge(y_full, j + 1)
                        for d, dest in enumerate(job["dest"]):
                            ins = dve.tensor_copy(dest, bank(job["y"])[:, d * S:(d + 1) * S])
                        ins.then_inc(bank_freed["d"], 1)

            dve.wait_ge(in_x, 16)
            dve.wait_ge(in_small, 16)
            norm_scale("norm1", X)
            norm_out("norm1", HT)
            for n in range(N_WIN):
                width = min(512, PROJ - 512 * n)
                copy_bank(("win", n, 0), proj[:, 0, 512 * n:512 * n + width], bank(("win", n, 0))[:, 0:width])
            dve.wait_ge(in_layer1, 16)
            for kv in range(2):
                wait_full(dve, ("win2", kv))
                for g in range(KV_HEADS):
                    for kh in range(2):
                        src = bank(("win2", kv))[:, g * P + 8 * kh:g * P + 8 * kh + 8 * N_CMP]
                        pos = cpos[:, kv, 8 * kh:8 * kh + 8].unsqueeze(2).to_broadcast([P, 8, N_CMP])
                        ins = dve.tensor_tensor(blocksT[:, kv, 8 * kh:8 * kh + 8, g, :],
                                                src.rearrange("p (n k) -> p k n", k=8), pos, ALU.add)
                ins.then_inc(bank_freed["d"], 1)
            hg = smalls[:, HG1].rearrange("p (n d) -> p n d", n=5)
            head_norm(0, (sq1, proj[:, :, 0:NORMED]), hstat1, list(zip((8, 8, 8, 2, 2), [hg[:, m, :] for m in range(5)])),
                      rope_first)
            for kv in range(2):
                wait_full(dve, ("hid", kv))
                dve.tensor_tensor(hid[0:2 * N_CMP, kv, :], bank(("hid", kv))[0:2 * N_CMP, 0:CMP_HID],
                                  cb1[0:2 * N_CMP, kv, :], ALU.add).then_inc(bank_freed["d"], 1)
            for kv in range(2):
                copy_bank(("hidT", kv), hidT[:, kv, :, :],
                          bank(("hidT", kv))[:, 0:64].rearrange("p (k n) -> p k n", k=2)[:, :, 0:2 * N_CMP])
            w = slice(0, N_CMP)
            for kv in range(2):
                wait_full(dve, ("c2", kv))
                dve.tensor_tensor(kvc[w, kv, :, :], bank(("c2", kv))[w, 0:2 * HD].rearrange("p (g d) -> p g d", g=2),
                                  cb2[w, kv, :].unsqueeze(1).to_broadcast([N_CMP, 2, HD]), ALU.add).then_inc(bank_freed["d"], 1)
            wait_freed(dve, ("c2", 0))
            link(dve.tensor_tensor(ctmp[w, 0, :, :], kvc[w, 0, :, :], kvc[w, 0, :, :], ALU.mult))
            dve.tensor_reduce(cst[w, 0, :], ctmp[w, 0, :, :], AXX, ALU.add).then_inc(cmp_sum, 1)
            dve.wait_ge(cmp_root, 1)
            link(dve.reciprocal(cst[w, 2, :], cst[w, 1, :]))
            link(dve.tensor_tensor(kvc[w, 0, :, :], kvc[w, 0, :, :], cst[w, 2, :].unsqueeze(2).to_broadcast([N_CMP, 2, HD]),
                                   ALU.mult))
            dve.tensor_tensor(kvc[w, 0, :, :], kvc[w, 0, :, :], kcg[w].unsqueeze(1).to_broadcast([N_CMP, 2, HD]),
                              ALU.mult).then_inc(cmp_key, 1)
            copy_bank(("kcT",), kcT[:, 0:N_CMP], bank(("kcT",))[:, 0:N_CMP])
            sc4 = scmp[:, :, :].rearrange("p (h t) n -> p h t n", t=T)[:, :, :, w]
            sc3 = scmp[:, :, w]
            for g in range(KV_HEADS):
                wait_full(dve, ("scmp", g))
                src = bank(("scmp", g))[:, 0:4 * T * 16].rearrange("p (r t n) -> p r t n", r=4, t=T)[:, :, :, w]
                dve.tensor_tensor(sc4[:, 4 * g:4 * g + 4], src, cmask.unsqueeze(1).to_broadcast([P, 4, T, N_CMP]),
                                  ALU.add).then_inc(bank_freed["d"], 1)
            wait_freed(dve, ("scmp", 1))
            link(dve.tensor_reduce(cred[:, 0, :], sc3, AXX, ALU.max))
            dve.tensor_tensor(sc3, sc3, cred[:, 0, :].unsqueeze(2).to_broadcast([P, 16, N_CMP]), ALU.subtract)\
               .then_inc(cmp_less, 1)
            dve.wait_ge(cmp_exp, 1)
            link(dve.tensor_reduce(cred[:, 1, :], sc3, AXX, ALU.add))
            link(dve.reciprocal(cred[:, 2, :], cred[:, 1, :]))
            r2 = cred[:, 2, :].rearrange("p (h t) -> p h t", t=T)
            link(dve.tensor_tensor(r2, r2, cany.unsqueeze(1).to_broadcast([P, 8, T]), ALU.mult))
            dve.wait_ge(gate3_done, 1)
            link(dve.tensor_tensor(r2, r2, gate3[:, :, :].rearrange("p t (h b) -> p h t b", b=3)[:, :, :, 0], ALU.mult))
            dve.tensor_tensor(sc3, sc3, cred[:, 2, :].unsqueeze(2).to_broadcast([P, 16, N_CMP]), ALU.mult).then_inc(cmp_prob, 1)
            attention("a")
            attention("b")
            for f in range(KD):
                wait_full(dve, ("up", f))
                tmp = SMx[:, f % 2, :, :]
                dve.tensor_tensor(tmp, bank(("up", f))[:, :].rearrange("p (b n) -> p b n", b=2), mgate[:, f, :, :],
                                  ALU.mult).then_inc(bank_freed["d"], 1)
                wait_freed(dve, ("up", f))
                dve.tensor_tensor(merged[:, f, :], tmp[:, 0, :], tmp[:, 1, :], ALU.add).then_inc(merged_done, 1)
            wide_read("out", X, True)

            norm_scale("norm2", X)
            norm_out("norm2", HT)

            def top16(values, spare, v, ix):
                link(dve.max(v[:, 0:8], values))
                dve.max_index(ix[:, 0:8], v[:, 0:8], values)
                link(dve.match_replace(spare, v[:, 0:8], values, LOW))
                link(dve.max(v[:, 8:16], spare))
                return dve.max_index(ix[:, 8:16], v[:, 8:16], spare)

            for m in range(8):
                wait_freed(dve, ("sc", m))
                t = m // 4
                for h in range(2 * (m % 4), 2 * (m % 4) + 2):
                    for s in range(2):
                        ins = top16(sc[:, t, h, s, :], srep[:, s, :], v16[:, t, h, s, :], i16[:, t, h, s, :])
                    link(ins)
                    link(dve.tensor_tensor(cand[:, 0, :, :], v16[:, t, h, 0, :].unsqueeze(2).to_broadcast([P, TOPK, TOPK]),
                                           v16[:, t, h, 1, :].unsqueeze(1).to_broadcast([P, TOPK, TOPK]), ALU.add))
                    link(top16(cand[:, 0, :, :].rearrange("p a b -> p (a b)"), cand[:, 1, :, :].rearrange("p a b -> p (a b)"),
                               tv[:, t, h, :], ti[:, t, h * TOPK:(h + 1) * TOPK]))
            link(dve.tensor_copy(gsum[:, 0, :, :], tv[:, :, :, 0]))
            dve.tensor_tensor(tv[:, :, :, :], tv[:, :, :, :], gsum[:, 0, :, :].unsqueeze(3).to_broadcast([P, T, 8, TOPK]),
                              ALU.subtract).then_inc(gate_less, 1)
            link(dve.tensor_scalar(tab[:, 0, :, :], ti[:, :, :], 4, None, ALU.logical_shift_right))
            link(dve.tensor_scalar(tab[:, 1, :, :], ti[:, :, :], 15, None, ALU.bitwise_and))
            link(dve.tensor_copy(tabf[:, :, :, :], tab[:, :, :, :]))
            link(dve.tensor_copy(i16f[:, :, :, :, :], i16[:, :, :, :, :]))
            for t in range(T):
                for s in range(2):
                    link(dve.tensor_tensor(onehot16[:, :, :], tabf[:, s, t, :].unsqueeze(2).to_broadcast([P, P, TOPK]),
                                           iota[:, 0:TOPK].unsqueeze(1).to_broadcast([P, P, TOPK]), ALU.is_equal))
                    o4 = onehot16[:, :, :].rearrange("p (h k) j -> p h k j", h=PEER_HEADS)
                    link(dve.tensor_tensor(o4, o4, i16f[:, t, :, s, :].unsqueeze(2).to_broadcast([P, PEER_HEADS, TOPK, TOPK]),
                                           ALU.mult))
                    link(dve.tensor_reduce(ex[:, 1 - s, t, :], onehot16[:, :, :], AXX, ALU.add))
            dve.wait_ge(gate_exp, 1)
            link(dve.tensor_reduce(gsum[:, 0, :, :], tv[:, :, :, :], AXX, ALU.add))
            link(dve.reciprocal(gsum[:, 1, :, :], gsum[:, 0, :, :]))
            dve.tensor_tensor(tv[:, :, :, :], tv[:, :, :, :], gsum[:, 1, :, :].unsqueeze(3).to_broadcast([P, T, 8, TOPK]),
                              ALU.mult).then_inc(ex_done, 1)
            wait_freed(dve, ("et", 2))
            with dve.Fori(0, S // 8) as i:
                for half in range(2):
                    dve.wait_ge(hot_full, i * 2 + half)
                    for j in range(4):
                        n = i * 8 + (4 * half + j)
                        dve.tensor_scalar(hots[:, half, j, 0, :], iota, eT[:, 0, bass.ds(n, 1)], None, ALU.is_equal)
                        ins = dve.tensor_scalar(hots[:, half, j, 1, :], iota, eT[:, 1, bass.ds(n, 1)],
                                                eT[:, 2, bass.ds(n, 1)], ALU.is_equal, ALU.mult)
                    ins.then_inc(hot_made, 1)
            dve.memset(wexp[:, 0, :], 0.0).then_inc(a_w, 1)
            with dve.Fori(0, NKEYS // 4) as i:
                for s in range(4):
                    e = i * 4 + s
                    dve.wait_ge(a_gelu, i * 4 + (s + 1))
                    dve.wait_ge(a_v, i * 4 + s)
                    dve.tensor_tensor(wexp[:, s % 2, :].unsqueeze(1), act_a[:, s % 2, :].unsqueeze(1),
                                      gates[:, bass.ds(e, 1), :], ALU.mult).then_inc(a_w, 1)
            dve.wait_ge(a_v, NKEYS + 1)
            for t in range(T):
                for h in range(2):
                    o = X[:, t, h * 512:(h + 1) * 512]
                    dve.tensor_tensor(o, o, PS[4 + 2 * t + h][:, :], ALU.add).then_inc(wide_out, 1)

            wait_wide(dve, "peer")
            norm_scale("attn", X)
            norm_out("attn", HT)
            norm_scale("mem0", memory)
            for n in range(3):
                copy_bank(("qkv", n, 0), qkv[:, 0, 512 * n:512 * (n + 1)], bank(("qkv", n, 0))[:, :])
            norm_out("mem0", memT)
            for i in range(DEPTH2):
                if i == 0:
                    hg = smalls[:, HG2].rearrange("p (n d) -> p n d", n=2)
                    head_norm(1, (sq2, qkv[:, :, 0:1280]), hstat2, [(N_HEADS, hg[:, 0, :]), (N_KV, hg[:, 1, :])], rope_axial)
                    wide_read("xv0", vx, False)
                    attention("self")
                    wide_read("wo", X, True)
                    wait_wide(dve, "wo")
                else:
                    norm_scale("pool", X)
                    wide_read("xv1", vx, False)
                    dve.wait_ge(in_wide, 16)
                    for t in range(T):
                        for g2 in range(2):
                            wait_full(dve, ("py", t, g2))
                            cols = slice(g2 * 512, (g2 + 1) * 512)
                            tmp = SM2[:, g2, :, :].rearrange("p a b -> p (a b)")
                            dve.tensor_tensor(tmp, bank(("py", t, g2))[:, :], wideg[:, 0, cols],
                                              ALU.mult).then_inc(bank_freed["d"], 1)
                            wait_freed(dve, ("py", t, g2))
                            dve.tensor_tensor(X[:, t, cols], X[:, t, cols], tmp, ALU.add).then_inc(pool_done, 1)
                norm_scale(f"x{i}", X)
                norm_out(f"x{i}", HT)
                attention(f"x{i}")
                wide_read(f"xo{i}", X, True)
                norm_scale(f"ffn{i}", X)
                norm_out(f"ffn{i}", HT)
                if i == 0:
                    norm_scale("mem1", memory)
                    norm_out("mem1", memT)
                for f in range(NF + 1):
                    if f < NF:
                        dve.wait_ge(conv_a, NF * i + f + 1)
                        b = bank(("ffu", i, f))
                        for tap in (0, 2):
                            for c in range(2):
                                w = conv[:, i, c * NF + f, tap:tap + 1]
                                u = b[:, c * S:(c + 1) * S]
                                o, v = (slice(1, S), slice(0, S - 1)) if tap == 0 else (slice(0, S - 1), slice(1, S))
                                y = cv[:, f % 2, c, o]
                                ins = dve.scalar_tensor_tensor(out=y, in0=u[:, v], scalar=w, in1=y, op0=ALU.mult, op1=ALU.add)
                            if tap == 0:
                                link(ins)
                            else:
                                ins.then_inc(conv_d, 1)
                        dve.wait_ge(conv_d, NF * i + f + 1)
                        dve.sem_inc(bank_freed["d"], 1)
                    if f:
                        dve.wait_ge(conv_s, NF * i + f)
                        g = (f - 1) % 2
                        dve.tensor_tensor(ff[:, f - 1, :], cv[:, g, 0, :], cv[:, g, 1, :], ALU.mult).then_inc(conv_m, 1)
                wide_read(f"ffd{i}", X, True)
            norm_scale("final", X)
            for t in range(T):
                dve.wait_ge(norm_h, 2 * len(NORMS) - 1 + t)
                dve.tensor_tensor(H[:, t, :], H[:, t, :], wideg[:, 1, :], ALU.mult).then_inc(final_h, 1)


def pairs(w, axis, heads, kv):
    w = np.moveaxis(w, axis, 0)
    group = heads // kv
    w = w.reshape(kv // 2, 2, group, HD, -1).transpose(0, 2, 1, 3, 4).reshape(heads * HD, -1)
    return np.moveaxis(w, 0, axis)


def square_block(w, k, n):
    b = np.zeros((k, P, n), np.float32)
    b[:w.shape[0] // P, :, :w.shape[1]] = w.reshape(w.shape[0] // P, P, w.shape[1])
    return b.transpose(1, 0, 2).reshape(P, BLK)


def weight_arrays(a):
    w_in = a["w_in"][0]
    at = np.cumsum([0, 512, 512, 512, 512, 128, 128, 128, 128, 128, 128, 24])
    aq, ak, av, bq, kc, vc, ks, vs, kw, vw, bg = (w_in[:, at[i]:at[i + 1]] for i in range(11))
    first = np.concatenate([aq, pairs(bq, 1, 8, 2), ak, ks, kw, av, vs, vw, kc, vc, bg], axis=1)
    mg = w_in[:, at[11]:]
    out = {}
    for n in range(N_WIN):
        out["win", n] = square_block(first[:, 512 * n:512 * n + 512], 8, 512)
    for n in range(4):
        out["mg", n] = square_block(mg[:, 512 * n:512 * n + 512], 8, 512)
        out["wq", n] = square_block(a["peer_wq"][0][:, 512 * n:512 * n + 512], 8, 512)
    for n, w in enumerate((a["cmp_k_w1"][0], a["cmp_v_w1"][0])):
        out["cmp", n] = square_block(w, 16, 256)
    out["up", 0] = square_block(a["w_up_a"][0], 4, D)
    out["up", 1] = square_block(pairs(a["w_up_b"][0], 0, 8, 2), 4, D)
    for n in range(2):
        out["out", n] = square_block(a["w_out"][0][512 * n:512 * n + 512], 4, D)
    w = a["attn_w_qkv_2"][0]
    w = np.concatenate([pairs(w[:, :N_HEADS * HD], 1, N_HEADS, N_KV), w[:, N_HEADS * HD:]], axis=1)
    for n in range(3):
        out["qkv", n] = square_block(w[:, 512 * n:512 * n + 512], 8, 512)
    w = pairs(a["attn_w_o_2"][0], 0, N_HEADS, N_KV)
    for n in range(2):
        out["wo", n] = square_block(w[512 * n:512 * n + 512], 4, D)
    w = a["pool_w_2"][0].reshape(4, 2, P, S).transpose(2, 0, 1, 3).reshape(P, 2048)
    out["pool", 0] = np.concatenate([w, np.zeros((P, BLK - 2048), np.float32)], axis=1)
    for i in range(DEPTH2):
        for n in range(2):
            cols, rows = slice(512 * n, 512 * n + 512), slice(512 * n, 512 * n + 512)
            out["xk", i, n] = square_block(a["xattn_w_kv_2"][i][:, :D][:, cols], 8, 512)
            out["xv", i, n] = square_block(a["xattn_w_kv_2"][i][:, D:][rows], 4, D)
            out["xq", i, n] = square_block(a["xattn_w_q_2"][i][:, cols], 8, 512)
            out["xo", i, n] = square_block(a["xattn_w_o_2"][i][rows], 4, D)
        w = a["ffn_w_up_2"][i].reshape(D, 2, NF, P).transpose(0, 2, 1, 3).reshape(D, 2 * D_FF)
        for n in range(NF // 2):
            out["ffu", i, n] = square_block(w[:, 512 * n:512 * n + 512], 8, 512)
        for n in range(-(-NF // 4)):
            out["ffd", i, n] = square_block(a["ffn_w_down_2"][i][512 * n:512 * n + 512], 4, D)
    return out


def by_partition(v):
    return v.reshape(-1, P).T


def on_all(v):
    return np.broadcast_to(v.reshape(1, -1), (P, v.size))


def tables():
    pos = np.arange(S, dtype=np.float32)
    inv = np.float32(500000.0) ** (-np.arange(0, 16, 2, dtype=np.float32) / np.float32(16))
    ang = pos[:, None] * inv[None, :]
    rope1 = np.stack([np.cos(ang), np.sin(ang)]).reshape(2, T, P, 8).transpose(2, 0, 1, 3)
    inv = np.float32(10000.0) ** (-np.arange(16, dtype=np.float32) / np.float32(16))
    row, col = np.floor(pos / GRID_W).astype(np.float32), (pos % GRID_W).astype(np.float32)
    ang = np.stack([row[:, None] * inv, col[:, None] * inv], axis=1)
    rope2 = np.stack([np.cos(ang), np.sin(ang)]).reshape(2, T, P, 2, 16).transpose(2, 0, 1, 3, 4)
    tokens = np.arange(S)
    causal = np.where(tokens[None, :] <= tokens[:, None], 0.0, NEG).reshape(T, P, S).transpose(1, 0, 2)
    ends = np.arange(N_CMP) * CMP_STRIDE + CMP_LEN - 1
    seen = ends[None, :] <= tokens[:, None]
    cmask = np.where(seen, 0.0, NEG).reshape(T, P, N_CMP).transpose(1, 0, 2)
    some = seen.any(axis=1).astype(np.float32).reshape(T, P).T
    band = np.zeros((4, S, S), np.float32)
    for g, w in enumerate(POOL_WINDOWS):
        for t in range(S):
            lo, hi = max(t - w // 2, 0), min(t + w - w // 2, S)
            band[g, lo:hi, t] = 1.0 / (hi - lo)
            band[g, t, t] -= 1.0
    band = band.reshape(4, T, P, S).transpose(2, 0, 1, 3).reshape(P, 8, S)
    flat = lambda v: np.asarray(v, np.float32).reshape(P, -1)
    return flat(rope1), flat(rope2), flat(causal), flat(cmask), flat(some), np.ascontiguousarray(band)


def lay_out(a):
    rope1, rope2, causal, cmask, some, band = tables()
    blocks = weight_arrays(a)
    gains = [a["norm1_g"][0], a["norm2_g"][0], a["attn_norm_2"][0], a["mem_norm_2"][0], a["xattn_norm_2"][0], a["ffn_norm_2"][0],
             a["mem_norm_2"][1], a["pool_norm_2"][0], a["xattn_norm_2"][1], a["ffn_norm_2"][1]]
    conv = np.stack([np.concatenate([a["ffn_conv_w_2"][i], a["ffn_conv_b_2"][i][None]]) for i in range(DEPTH2)])
    conv = conv.reshape(DEPTH2, 4, 2 * NF, P).transpose(3, 0, 2, 1).reshape(P, -1)
    small = np.concatenate(
        [np.eye(P, dtype=np.float32), on_all(np.arange(NKEYS, dtype=np.float32))] + [by_partition(g) for g in gains]
        + [conv, by_partition(a["b_merge"][0].reshape(-1)), a["peer_k1"][0].T, a["peer_k2"][0].T,
           np.full((P, 1), EPS, np.float32), rope1, rope2]
        + [on_all(a[n][0]) for n in ("a_q_g", "b_q_g", "a_k_g", "b_ks_g", "b_kw_g", "attn_q_gain_2", "attn_k_gain_2")], axis=1)
    layer1 = np.concatenate(
        [causal, cmask, some] + [a[n][0].reshape(16, P).T for n in ("cmp_pos_k", "cmp_pos_v")]
        + [on_all(a[n][0]) for n in ("cmp_k_b1", "cmp_v_b1", "cmp_k_b2", "cmp_v_b2")]
        + [a[n][0].reshape(2, P, HD).transpose(1, 0, 2).reshape(P, -1) for n in ("cmp_k_w2", "cmp_v_w2")]
        + [on_all(a["b_kc_g"][0])], axis=1)
    assert small.shape[1] == SM.at and layer1.shape[1] == L1.at
    return {
        "x": a["x"], "mem": a["mem_2"],
        "weights": np.stack([blocks[name] for name in BLOCKS]),
        "expert_u": a["peer_u"][0].reshape(NKEYS, NKEYS, KD, P).transpose(0, 3, 2, 1).reshape(NKEYS, P, KD * NKEYS),
        "expert_v": a["peer_v"][0].reshape(NKEYS, NKEYS, D),
        "small": small, "layer1": layer1, "band": band,
        "wide_gains": np.broadcast_to(np.stack([a["pool_scale_2"][0], a["final_norm_2"]])[None], (P, 2, D)),
    }


def kernel(**inputs):
    import concourse.bacc as bacc
    from concourse.bass_utils import run_bass_kernel_spmd

    nc = bacc.Bacc("TRN2", target_bir_lowering=False, num_devices=1)
    arrays, args = {}, []
    for name, v in lay_out({k: np.asarray(v) for k, v in inputs.items()}).items():
        arrays[name] = np.ascontiguousarray(v)
        args.append(nc.dram_tensor(name, v.shape, F32, kind="ExternalInput").ap())
    args.append(nc.dram_tensor("result", (1, S, D), F32, kind="ExternalOutput").ap())
    block_stack(nc, *args)
    r = run_bass_kernel_spmd(nc, [arrays], core_ids=[0])
    return r.results[0]["result"]
```

```python
from contextlib import ExitStack

import numpy as np
import concourse.bass as bass
from concourse import mybir

F32 = mybir.dt.float32
F32R = mybir.dt.float32r
U32 = mybir.dt.uint32
ALU = mybir.AluOpType
ACT = mybir.ActivationFunctionType
AXX = mybir.AxisListType.X

P = 128
S = 256
T = S // P
D = 1024
KD = D // P
HD = 64
NEG = -1e30
LOW = -3.0e38
EPS = 1e-6

A_HEADS = B_HEADS = 8
KV_HEADS = 2
N_NORMED = 28
NORMED = N_NORMED * HD
AV, VS, VW, KC, VC, BG = NORMED, NORMED + 512, NORMED + 640, NORMED + 768, NORMED + 896, NORMED + 1024
PROJ = BG + 3 * B_HEADS
N_WIN = -(-PROJ // 512)
CMP_LEN, CMP_STRIDE, CMP_HID = 32, 16, 256
N_CMP = (S - CMP_LEN) // CMP_STRIDE + 1
PEER_HEADS, NKEYS, TOPK = 8, 128, 16

DEPTH2 = 2
N_HEADS, N_KV = 16, 4
QKV = (N_HEADS + 2 * N_KV) * HD
X_HEADS, X_HD = 4, 256
D_FF = 2816
NF = D_FF // P
POOL_WINDOWS = (2, 4, 8, 16)
GRID_W = 64

BEGIN = 2
UNIT_COLS = 1024
RAW = 8
NSPLIT = 4


def weight_units():
    out = [("win", n, q) for n in range(N_WIN) for q in range(4)] + [("mg", c) for c in range(8)]
    out += [("cmp", kv, q) for kv in range(2) for q in range(4)] + [("mg", c) for c in range(8, 16)]
    out += [("up", f) for f in range(KD)] + [("out", k) for k in range(KD)] + [("wq", c) for c in range(16)]
    for i in range(DEPTH2):
        out += [("xk", i, c) for c in range(KD)] + [("xv", i, k) for k in range(KD)]
    out += [("qkv", n, q) for n in range(3) for q in range(4)]
    for i in range(DEPTH2):
        out += [("wo", k) for k in range(KD)] if i == 0 else [("pool", g) for g in range(2)]
        out += [("xq", i, c) for c in range(KD)] + [("xo", i, k) for k in range(KD)]
        out += [("ffu", i, c) for c in range(2 * NF)] + [("ffd", i, k) for k in range(NF)]
    return out


UNITS = weight_units()
UNIT = {name: n for n, name in enumerate(UNITS)}
FIRST2 = UNIT[("qkv", 0, 0)]


def bank_groups():
    out = [(("win", n, t), "da"[t]) for n in range(N_WIN) for t in range(T)]
    out += [(("win2", kv), "d") for kv in range(2)]
    out += [(("mg", g), "a") for g in range(4)]
    out += [(("hid", kv), "d") for kv in range(2)] + [(("mg", 4), "a")]
    out += [(("hidT", kv), "d") for kv in range(2)] + [(("mg", 5), "a")]
    out += [(("c2", kv), "d") for kv in range(2)] + [(("mg", 6), "a")]
    out += [(("kcT",), "d"), (("mg", 7), "a")]
    out += [(("qkt", m), "a") for m in range(7)]
    out += [(("scmp", g), "d") for g in range(KV_HEADS)] + [(("pct", m), "a") for m in range(4)]
    out += [(("ya", p), "d") for p in range(4)] + [(("yb", r), "d") for r in range(4)]
    out += [(("up", f), "d") for f in range(KD)]
    out += [(("pq", g), "a") for g in range(8)] + [(("sc", m), "a") for m in range(8)]
    out += [(("xk", i, g), "a") for i in range(DEPTH2) for g in range(4)] + [(("et", m), "a") for m in range(3)]
    out += [(("qkv", n, t), "da"[t]) for n in range(3) for t in range(T)]
    for i in range(DEPTH2):
        if i == 0:
            out += [(("qkt2", m), "a") for m in range(5)] + [(("y2", p), "d") for p in range(8)]
        else:
            out += [(("pm", g), "d") for g in range(4)] + [(("py", t, g), "d") for g in range(2) for t in range(T)]
        out += [(("xq", i, g), "a") for g in range(4)] + [(("yx", i, h), "d") for h in range(X_HEADS)]
        out += [(("ffu", i, f), "d") for f in range(NF)]
    return out


GROUPS = bank_groups()
GROUP = {name: q for q, (name, _) in enumerate(GROUPS)}
RING = 4


def freed(q):
    who = GROUPS[q][1]
    return who, sum(1 for _, w in GROUPS[:q + 1] if w == who)


NORMS = ["norm1", "mem", "norm2", "attn", "x0", "ffn0", "pool", "x1", "ffn1", "final"]
TURNS = ["norm1", "norm2", "mem0", "mem1", "attn", "x0", "ffn0", "x1", "ffn1"]
GAINS_OF = TURNS + ["pool"]
WIDE = ["out", "xv0", "xv1", "peer", "wo", "xo0", "ffd0", "xo1", "ffd1"]
JOBS = {"ab": 0, "self": 24, "x0": 40, "x1": 44}


class Columns:

    def __init__(self, at=0):
        self.at = at

    def take(self, n):
        self.at += n
        return slice(self.at - n, self.at)


SM = Columns()
IDENT, IOTA, GAINS = SM.take(P), SM.take(NKEYS), SM.take(len(GAINS_OF) * KD)
CONV, BMERGE, PKEYS = SM.take(DEPTH2 * 2 * NF * 4), SM.take(2 * KD), SM.take(2 * NKEYS)
EPSC, ROPE1, ROPE2 = SM.take(1), SM.take(2 * T * 8), SM.take(2 * T * 2 * 16)
HG1, HG2 = SM.take(5 * HD), SM.take(2 * HD)
L1 = Columns()
MASK, CMASK, CANY, CPOS = L1.take(T * S), L1.take(T * N_CMP), L1.take(T), L1.take(2 * 16)
CB1, CB2, CW2, KCG = L1.take(2 * CMP_HID), L1.take(2 * HD), L1.take(2 * 2 * HD), L1.take(HD)


def block_stack(nc: bass.Bass, x, mem, weights, expert_u, expert_v, small, layer1, band, wide_gains, out):
    with ExitStack() as ctx:
        def sb(name, shape, dt=F32):
            return ctx.enter_context(nc.sbuf_tensor(name, shape, dt))

        def sem(name):
            return ctx.enter_context(nc.semaphore(name))

        smalls = sb("smalls", [P, SM.at])
        stat = sb("stat", [P, 8])
        att = sb("att", [P, 4, 4, T])
        HT = sb("HT", [P, 2, KD, S], F32R)
        wsplit = sb("wsplit", [P, NSPLIT, 2, UNIT_COLS], F32R)
        act_e = sb("act_e", [P, 2, S])
        wexp = sb("wexp", [P, 2, 2, S], F32R)
        raw0 = sb("raw0", [P, 4, UNIT_COLS])
        PS = [ctx.enter_context(nc.psum_tensor(f"bank{b}", [P, 512], F32)) for b in range(8)]

        ident = smalls[:, IDENT]
        iota = smalls[:, IOTA]
        eps = smalls[:, EPSC]
        gains = smalls[:, GAINS].rearrange("p (n k) -> p n k", k=KD)
        conv = smalls[:, CONV].rearrange("p (i f c) -> p i f c", i=DEPTH2, c=4)
        pkeys = smalls[:, PKEYS].rearrange("p (h n) -> p h n", h=2)
        rope1 = smalls[:, ROPE1].rearrange("p (c t j) -> p c t j", c=2, t=T)
        rope2 = smalls[:, ROPE2].rearrange("p (c t a j) -> p c t a j", c=2, t=T, a=2)

        def tensor(scope, name, *dims, dt=F32):
            return scope.enter_context(nc.sbuf_tensor(name, [P, *dims], dt))

        def area(t, cols, *dims, dt=None):
            v = t[:, cols.take(int(np.prod(dims)))]
            if dt is not None:
                v = v.bitcast(dt)
            names = " ".join(f"d{i}" for i in range(len(dims)))
            sizes = {f"d{i}": d for i, d in enumerate(dims)}
            return v.rearrange(f"p ({names}) -> p {names}", **sizes) if len(dims) > 1 else v

        first = ExitStack()
        raw1a = tensor(first, "raw1a", 4, UNIT_COLS)
        X1 = tensor(first, "X1", T, D)
        layer = ExitStack()
        mgate = tensor(layer, "mgate", KD, 2, S)
        H1 = mgate[:, 0:4, :, :].rearrange("p k b s -> p (k b s)").rearrange("p (t d) -> p t d", t=T)
        projv = tensor(layer, "projv", T, PROJ - NORMED)
        yT = tensor(layer, "yT", 2, 2, 4, S, dt=F32R)
        inner = ExitStack()
        projq = tensor(inner, "projq", T, NORMED)
        c = Columns()
        projq_flat = projq[:, :, :].rearrange("p t n -> p (t n)")
        SMx, Pr, PT = area(projq_flat, c, 2, T, S), area(projq_flat, c, 3, T, S), area(projq_flat, c, 2, T, S)
        blocksT = tensor(inner, "blocksT", 2, 2, 16, 2, N_CMP, dt=F32R)
        attn1 = tensor(inner, "attn1", 20 * S + 2048 + L1.at + 2000)
        c = Columns()
        qkT = area(attn1, c, 20, S)
        sq1 = attn1[:, 0:2 * T * 512].rearrange("p (b t n) -> p b t n", b=2, t=T)
        pcT = area(attn1, c, B_HEADS, S)
        c.at = 20 * S
        rtmp1 = area(attn1, c, 4, T, N_NORMED, 8)
        c.at = 20 * S
        blocks = area(attn1, c, 2, 16, 2, N_CMP)
        c.at = 20 * S + 2048
        consts1 = area(attn1, c, L1.at)
        gate3 = area(attn1, c, T, 3 * B_HEADS)
        hstat1 = area(attn1, c, 3, T, N_NORMED)
        hid = area(attn1, c, 2, CMP_HID)
        hidT = area(attn1, c, 2, 2, 2 * N_CMP)
        kvc = area(attn1, c, 2, KV_HEADS, HD)
        ctmp = area(attn1, c, 2, KV_HEADS, HD)
        cst = area(attn1, c, 3, KV_HEADS)
        kcT = area(attn1, c, 16)
        scmp = area(attn1, c, 16, 16)
        cred = area(attn1, c, 3, 16)
        assert c.at <= 20 * S + 2048 + L1.at + 2000
        inner.close()
        inner = ExitStack()
        merged = tensor(inner, "merged", 2, KD, S, dt=F32R)
        uptmp = tensor(inner, "uptmp", 2, 2, S)
        inner.close()
        layer.close()
        mask = consts1[:, MASK].rearrange("p (t n) -> p t n", t=T)
        cmask = consts1[:, CMASK].rearrange("p (t n) -> p t n", t=T)
        cany = consts1[:, CANY]
        cpos = consts1[:, CPOS].rearrange("p (v k) -> p v k", v=2)
        cb1 = consts1[:, CB1].rearrange("p (v n) -> p v n", v=2)
        cb2 = consts1[:, CB2].rearrange("p (v n) -> p v n", v=2)
        cw2 = consts1[:, CW2].rearrange("p (v k n) -> p v k n", v=2, k=2)
        kcg = consts1[:, KCG]

        choice = ExitStack()
        Hp = tensor(choice, "Hp", T, D)
        memN = tensor(choice, "memN", T, D)
        memT = tensor(choice, "memT", 2, KD, S, dt=F32R)
        kout = tensor(choice, "kout", KD, S)
        pick = tensor(choice, "pick", 16 * S + T * PEER_HEADS * 2 * NKEYS + 6500)
        c = Columns()
        pq = area(pick, c, 16, S)
        sc = area(pick, c, T, PEER_HEADS, 2, NKEYS)
        srep = area(pick, c, 2, NKEYS)
        v16 = area(pick, c, T, PEER_HEADS, 2, TOPK)
        i16 = area(pick, c, T, PEER_HEADS, 2, TOPK, dt=U32)
        i16f = area(pick, c, T, PEER_HEADS, 2, TOPK)
        cand = area(pick, c, 2, TOPK, TOPK)
        tv = area(pick, c, T, PEER_HEADS, TOPK)
        ti = area(pick, c, T, PEER_HEADS * TOPK, dt=U32)
        tab = area(pick, c, 2, T, PEER_HEADS * TOPK, dt=U32)
        tabf = area(pick, c, 2, T, PEER_HEADS * TOPK)
        onehot16 = area(pick, c, PEER_HEADS * TOPK, TOPK)
        ex = area(pick, c, 2, T, PEER_HEADS * TOPK)
        gsum = area(pick, c, 2, T, PEER_HEADS)
        choice.close()
        first.close()

        run = ExitStack()
        gates = tensor(run, "gates", NKEYS, S)
        run.close()
        eT = raw0[:, 1, 0:3 * S].rearrange("p (k t) -> p k t", k=3)
        few = stat[:, :].rearrange("p (b w j) -> p b w j", b=2, w=2)
        hots = raw0[:, 2:4, :].rearrange("p b (w j n) -> p b w j n", w=2, j=4)

        second = ctx.enter_context(ExitStack())
        raw1b = tensor(second, "raw1b", 4, UNIT_COLS)
        X2 = tensor(second, "X2", T, D)
        H2 = tensor(second, "H2", T, D)
        kv_in = tensor(second, "kv_in", 2, 2048)
        kxT = kv_in[:, 0, :].rearrange("p (k s) -> p k s", k=KD)
        vx = kv_in[:, 1, :].rearrange("p (t d) -> p t d", t=T)
        wideg = tensor(second, "wideg", 2, D)
        bandm = tensor(second, "bandm", 8, S)
        ptmp = tensor(second, "ptmp", 2, 512)
        inner = ExitStack()
        oT = tensor(inner, "oT", 2, KD, S, dt=F32R)
        qkv = tensor(inner, "qkv", T, QKV)
        qkv_flat = qkv[:, :, :].rearrange("p t n -> p (t n)")
        qxT = qkv_flat[:, 0:KD * S].rearrange("p (k t) -> p k t", k=KD)
        qkT2 = tensor(inner, "qkT2", 12, S)
        rtmp2 = tensor(inner, "rtmp2", T, 4, 8, 2, 16)
        probs2 = tensor(inner, "probs2", 2560)
        c = Columns()
        Pr2, PT2 = area(probs2, c, 3, T, S), area(probs2, c, 2, T, S)
        sq2 = probs2[:, 0:2 * T * 512].rearrange("p (b t n) -> p b t n", b=2, t=T)
        hstat2 = tensor(inner, "hstat2", 3, T, 20)
        inner.close()
        inner = ExitStack()
        ff = tensor(inner, "ff", 2, NF, S, dt=F32R)
        cv = tensor(inner, "cv", 2, 2, S)
        inner.close()

        def head_block(n, end, src, sq, st):
            width = min(512, end - 512 * n)
            heads = slice(8 * n, 8 * n + width // HD)
            return src[:, :, 512 * n:512 * n + width], sq[:, n % 2, :, 0:width], [st[:, w, :, heads] for w in range(3)]

        def head_block1(n):
            return head_block(n, NORMED, projq, sq1, hstat1)

        def head_block2(n):
            return head_block(n, (N_HEADS + N_KV) * HD, qkv, sq2, hstat2)

        park = nc.dram_tensor("parked", (5, P, 2048), F32).ap()

        def sb_raw(u):
            later = raw1a if u < FIRST2 else raw1b
            return raw0[:, u % RAW, :] if u % RAW < 4 else later[:, u % RAW - 4, :]

        def f32(ap):
            return ap.bitcast(F32)

        in_x, in_small, in_layer1 = sem("in_x"), sem("in_small"), sem("in_layer1")
        in_mem, in_band, in_wide, in_kv = sem("in_mem"), sem("in_band"), sem("in_wide"), sem("in_kv")
        w_landed = [sem(f"w_landed{s}") for s in range(RAW)]
        w_hi, w_freed = sem("w_hi_made"), sem("w_freed")
        w_lo = [sem("w_lo_by_vector"), sem("w_lo_by_pool")]
        u_landed = [sem(f"u_landed{s}") for s in range(2)]
        v_landed = [sem(f"v_landed{s}") for s in range(2)]
        u_hi, u_lo, v_hi, v_lo = sem("u_hi_made"), sem("u_lo_made"), sem("v_hi_made"), sem("v_lo_made")
        x_parked, k_parked, v_parked = sem("x_parked"), sem("k_parked"), sem("v_parked")
        bank_full = sem("bank_full")
        bank_freed = {"a": sem("bank_freed_by_scalar"), "d": sem("bank_freed_by_vector")}
        norm_sq, norm_root, norm_h, norm_t = sem("norm_sq"), sem("norm_root"), sem("norm_h"), sem("norm_t")
        norm_a, norm_d = sem("norm_hi_by_scalar"), sem("norm_lo_by_vector")
        wide_done, wide_out = sem("wide_done"), sem("wide_out")
        head_sq, head_sum, head_root, head_done = sem("head_sq"), sem("head_sum"), sem("head_root"), sem("head_done")
        pads = sem("key_pads_zeroed")
        gate3_done, blocks_done, merged_done = sem("gate3_done"), sem("blocks_done"), sem("merged_done")
        cmp_gelu, cmp_sum, cmp_root = sem("cmp_gelu"), sem("cmp_sum"), sem("cmp_root")
        cmp_key, cmp_less, cmp_exp, cmp_prob = sem("cmp_key"), sem("cmp_less"), sem("cmp_exp"), sem("cmp_prob")
        s_full, s_max, s_exp, s_prob = sem("scores_full"), sem("scores_max"), sem("scores_exp"), sem("scores_prob")
        t_full, t_out, y_full = sem("probsT_full"), sem("probsT_out"), sem("y_full")
        gate_less, gate_exp, ex_done = sem("gate_less"), sem("gate_exp"), sem("experts_done")
        few_made, few_seen = sem("few_made"), sem("few_seen")
        hot_by_d, hot_by_p = sem("hot_by_vector"), sem("hot_by_pool")
        hot_full, hot_out = sem("hot_full"), sem("hot_out")
        a_full, a_gelu, a_mul, a_hi = sem("a_full"), sem("a_gelu"), sem("a_times_gates"), sem("a_hi_made")
        a_w, a_v = sem("a_weighted"), sem("a_times_v")
        conv_a, conv_d, conv_s, conv_m = sem("conv_mid"), sem("conv_sum"), sem("conv_silu"), sem("conv_mul")
        pool_hi, pool_lo = sem("pool_hi"), sem("pool_lo")
        pool_done, final_h = sem("pool_done"), sem("final_h")
        chain = sem("vector_chain")
        stored = sem("stored")

        def bank(name):
            return PS[4 + GROUP[name] % RING]

        def wait_full(eng, name):
            eng.wait_ge(bank_full, sum(1 for n, _ in GROUPS[:GROUP[name] + 1] if n[0] not in ("ya", "yb", "y2", "yx")))

        def wait_freed(eng, name):
            who, count = freed(GROUP[name])
            eng.wait_ge(bank_freed[who], count)

        def wait_normed(eng, name):
            eng.wait_ge(norm_d, KD * (TURNS.index(name) + 1))

        def wait_wide(eng, name):
            eng.wait_ge(wide_out, 4 * (WIDE.index(name) + 1))

        def wait_unit_used(eng, u):
            eng.wait_ge(w_lo[0], u // 2)
            eng.wait_ge(w_lo[1], u // 2)

        def units_to(name):
            kind, at = name[0], name[1:]
            last = {
                "win": lambda: ("win", at[0], 3), "qkv": lambda: ("qkv", at[0], 3), "mg": lambda: ("mg", 2 * at[0] + 1),
                "hid": lambda: ("cmp", at[0], 3), "up": lambda: ("up", at[0]), "pq": lambda: ("wq", 2 * at[0] + 1),
                "xk": lambda: ("xk", at[0], 2 * at[1] + 1), "xq": lambda: ("xq", at[0], 2 * at[1] + 1),
                "ffu": lambda: ("ffu", at[0], 2 * at[1] + 1), "py": lambda: ("pool", at[1]),
                "out": lambda: ("out", KD - 1), "wo": lambda: ("wo", KD - 1), "xv": lambda: ("xv", at[0], KD - 1),
                "xo": lambda: ("xo", at[0], KD - 1), "ffd": lambda: ("ffd", at[0], NF - 1)}
            return UNIT[last[kind]()] + 1 if kind in last else 0

        def split_word(name):
            return (name[:-1], int(name[-1])) if name[-1].isdigit() else (name,)

        def tok(t):
            return slice(t * P, (t + 1) * P)

        def heads_v(at, h):
            return slice(at - NORMED + h * HD, at - NORMED + (h + 1) * HD)

        def a_jobs():
            for h in range(A_HEADS):
                yield dict(
                    q=lambda t, h=h: [qkT[:, h // 2, tok(t)]], k=[qkT[:, 8 + h, :]], gate=None,
                    v=lambda kt, h=h: [projv[:, kt, heads_v(AV, h)]], rows=slice(HD * (h % 2), HD * (h % 2) + HD), cmp=None,
                    y=("ya", h // 2), first=True, last=h % 2 == 1, dest=[yT[:, :, 0, h // 2, :]])

        def b_jobs():
            for r in range(4):
                for g in range(KV_HEADS):
                    h = 4 * g + r
                    for j, (slot, vat) in enumerate(((16, VS), (18, VW))):
                        yield dict(
                            q=lambda t, r=r: [qkT[:, 4 + r, tok(t)]], k=[qkT[:, slot + g, :]],
                            gate=lambda t, h=h, j=j: gate3[:, t, 3 * h + 1 + j:3 * h + 2 + j],
                            v=lambda kt, g=g, vat=vat: [projv[:, kt, heads_v(vat, g)]], rows=slice(HD * g, HD * g + HD),
                            cmp=(g, h) if j == 0 else None, y=("yb", r), first=j == 0, last=(g, j) == (1, 1),
                            dest=[yT[:, :, 1, r, :]])

        def self_jobs():
            for p in range(8):
                for i in range(2):
                    kv = 2 * (p // 4) + i
                    vat = (N_HEADS + N_KV + kv) * HD
                    yield dict(
                        q=lambda t, p=p: [qkT2[:, p, tok(t)]], k=[qkT2[:, 8 + kv, :]], gate=None,
                        v=lambda kt, vat=vat: [qkv[:, kt, vat:vat + HD]], rows=slice(HD * i, HD * i + HD), cmp=None,
                        y=("y2", p), first=True, last=i == 1, dest=[oT[:, :, p, :]])

        def cross_jobs(i):
            for h in range(X_HEADS):
                yield dict(
                    q=lambda t, h=h: [qxT[:, 2 * h + d, tok(t)] for d in range(2)],
                    k=[kxT[:, 2 * h + d, :] for d in range(2)], gate=None,
                    v=lambda kt, h=h: [vx[:, kt, (2 * h + d) * P:(2 * h + d + 1) * P] for d in range(2)],
                    rows=slice(0, P), cmp=None, y=("yx", i, h), first=True, last=True,
                    dest=[oT[:, :, 2 * h, :], oT[:, :, 2 * h + 1, :]])

        USES = {
            "ab": (list(a_jobs()) + list(b_jobs()), SMx, Pr, PT, HD ** -0.5),
            "self": (list(self_jobs()), None, Pr2, PT2, HD ** -0.5),
            "x0": (list(cross_jobs(0)), None, Pr2, PT2, X_HD ** -0.5),
            "x1": (list(cross_jobs(1)), None, Pr2, PT2, X_HD ** -0.5),
        }

        def win_parts(n, t):
            end = min(512 * (n + 1), PROJ)
            parts = []
            if 512 * n < NORMED:
                m = min(end, NORMED)
                parts.append((projq[:, t, 512 * n:m], slice(0, m - 512 * n)))
            if end > NORMED:
                m = max(512 * n, NORMED)
                parts.append((projv[:, t, m - NORMED:end - NORMED], slice(m - 512 * n, end - 512 * n)))
            return parts

        tokens_first = "b (t p) d -> p (b t) d"
        block = ctx.enter_context(nc.Block())

        @block.sync
        def _(sp):
            def load(n, u):
                sp.dma_start(sb_raw(u), weights[n]).then_inc(w_landed[u % RAW], 16)

            def load_turns(n0, n1):
                with sp.Fori(n0 // RAW, n1 // RAW) as i:
                    for s in range(RAW):
                        sp.wait_ge(w_lo[s % 2], i * (RAW // 2) + (s // 2 + 1 - RAW // 2))
                        load(i * RAW + s, n0 + s)

            sp.dma_start(X1[:, :, :], x.rearrange(tokens_first, p=P)).then_inc(in_x, 16)
            load(0, 0)
            load(1, 1)
            sp.dma_start(consts1, layer1).then_inc(in_layer1, 16)
            for u in range(2, RAW):
                load(u, u)
            load_turns(RAW, FIRST2)
            wait_unit_used(sp, FIRST2)
            sp.dma_start(raw0[:, 0, :], expert_u[0]).then_inc(u_landed[0], 16)
            sp.wait_ge(hot_full, BEGIN + S // 4)
            sp.dma_start(raw0[:, 2, :], expert_v[0]).then_inc(v_landed[0], 16)
            sp.dma_start(raw0[:, 1, :], expert_u[1]).then_inc(u_landed[1], 16)
            sp.dma_start(raw0[:, 3, :], expert_v[1]).then_inc(v_landed[1], 16)
            with sp.Fori(1, NKEYS // 2) as i:
                for s in range(2):
                    sp.wait_ge(u_lo, i * 2 + (s - 1))
                    sp.dma_start(raw0[:, s, :], expert_u[i * 2 + s]).then_inc(u_landed[s], 16)
                    sp.wait_ge(v_lo, i * 2 + (s - 1))
                    sp.dma_start(raw0[:, 2 + s, :], expert_v[i * 2 + s]).then_inc(v_landed[s], 16)
            sp.wait_ge(a_mul, NKEYS)
            sp.wait_ge(x_parked, 16)
            sp.dma_start(X2[:, :, :], park[0].rearrange("p (t d) -> p t d", t=T)).then_inc(in_x, 16)
            sp.wait_ge(u_lo, NKEYS)
            sp.wait_ge(v_lo, NKEYS)
            for u in range(FIRST2, FIRST2 + RAW):
                load(u, u)
            sp.wait_ge(k_parked, 32)
            sp.wait_ge(v_parked, 32)
            sp.dma_start(kv_in[:, :, :], park[1:3].rearrange("w p d -> p w d")).then_inc(in_kv, 16)
            sp.dma_start(bandm[:, :, :], band).then_inc(in_band, 16)
            sp.dma_start(wideg[:, :, :], wide_gains).then_inc(in_wide, 16)
            whole = len(UNITS) // RAW * RAW
            load_turns(FIRST2 + RAW, whole)
            for u in range(whole, len(UNITS)):
                sp.wait_ge(w_lo[u % 2], (u - RAW) // 2 + 1)
                load(u, u)
            sp.wait_ge(final_h, 2)
            sp.dma_start(out.rearrange(tokens_first, p=P), H2[:, :, :]).then_inc(stored, 16)
            sp.wait_ge(stored, 16)

        @block.tensor
        def _(pe):
            state = {"frees": 0}

            def mm(out, lhsT, rhs, start, stop, **kw):
                ins = pe.matmul(out, lhsT, rhs, start=start, stop=stop, **kw)
                if state["frees"]:
                    ins.then_inc(w_freed, 1)
                    state["frees"] = 0
                return ins

            def mm3(out, left, right, start, stop, **kw):
                for n, (a, b) in enumerate(((0, 0), (0, 1), (1, 0))):
                    ins = mm(out, left(a), right(b), start and n == 0, stop and n == 2, **kw)
                return ins

            def weights_of(*name):
                u = UNIT[name]
                pe.wait_ge(w_lo[u % 2], u // 2 + 1)
                state["frees"] = u not in (0, FIRST2)
                return lambda part: wsplit[:, u % NSPLIT, part, :]

            def tiles_of(w, **sizes):
                return lambda part: w(part).rearrange("p (k n) -> p k n", **sizes)

            def open_bank(name):
                q = GROUP[name]
                if q >= RING:
                    wait_freed(pe, GROUPS[q - RING][0])
                return PS[4 + q % RING]

            def turn(name, H):
                pe.wait_ge(norm_h, 2 * (NORMS.index("mem" if name[:3] == "mem" else name) + 1))
                for b in range(4):
                    for k in range(2):
                        for t in range(T):
                            c = 2 * b + k
                            ins = pe.transpose(PS[b][:, (k * T + t) * P:(k * T + t + 1) * P],
                                               H[:, t, c * P:(c + 1) * P], ident)
                    ins.then_inc(norm_t, 1)

            def feature_tile(out, unit, src):
                w = tiles_of(weights_of(*unit), k=KD)
                for k in range(KD):
                    ins = mm3(out, lambda a: w(a)[:, k, :], lambda b: src[:, b, k, :], k == 0, k == KD - 1)
                return ins

            def feature_groups(kind, units, n, src):
                for g in range(n):
                    b = open_bank(kind + (g,))
                    for c in range(2):
                        ins = feature_tile(b[:, c * S:(c + 1) * S], units + (2 * g + c,), src)
                    ins.then_inc(bank_full, 1)

            def token_major(kind, blocks, src, last_width=512):
                for n in range(blocks):
                    banks = [open_bank((kind, n, t)) for t in range(T)]
                    width = last_width if n == blocks - 1 else 512
                    for q in range(4):
                        w = tiles_of(weights_of(kind, n, q), k=2)
                        for t in range(T):
                            for k in range(2):
                                ins = mm3(banks[t][:, 0:width], lambda a: src[:, a, 2 * q + k, tok(t)],
                                          lambda b: w(b)[:, k, 0:width], q == k == 0, q == 3 and k == 1)
                            if q == 3:
                                ins.then_inc(bank_full, 1)

            def wide(name, unit, src, kt, ready):
                if WIDE.index(name):
                    wait_wide(pe, WIDE[WIDE.index(name) - 1])
                for k in range(kt):
                    ready(k)
                    w = weights_of(*unit, k)
                    for t in range(T):
                        for h in range(2):
                            ins = mm3(PS[2 * t + h][:, :], lambda a: src[:, a, k, tok(t)],
                                      lambda b: w(b)[:, h * 512:(h + 1) * 512], k == 0, k == kt - 1)
                ins.then_inc(wide_done, 1)

            def attention(use):
                jobs, _, Pb, Tb, _ = USES[use]
                j0, n = JOBS[use], len(jobs)
                for step in range(n + 3):
                    if step < n:
                        job, j = jobs[step], j0 + step
                        if step >= 2:
                            pe.wait_ge(s_exp, j - 1)
                        for t in range(T):
                            qs = job["q"](t)
                            for d, q in enumerate(qs):
                                ins = mm(PS[j % 2][:, t * S:(t + 1) * S], q, job["k"][d], d == 0, d == len(qs) - 1)
                        ins.then_inc(s_full, 1)
                    if 2 <= step <= n + 1:
                        j = j0 + step - 2
                        pe.wait_ge(s_prob, j + 1)
                        if step >= 4:
                            pe.wait_ge(t_out, j - 1)
                        for kt in range(T):
                            for t in range(T):
                                ins = pe.transpose(PS[2 + j % 2][:, kt * S + t * P:kt * S + (t + 1) * P],
                                                   Pb[:, j % 3, t, kt * P:(kt + 1) * P], ident)
                        ins.then_inc(t_full, 1)
                    if step >= 3:
                        job, j = jobs[step - 3], j0 + step - 3
                        if step == 3 or jobs[step - 4]["y"] != job["y"]:
                            b = open_bank(job["y"])
                        if job["cmp"] is not None:
                            g, h = job["cmp"]
                            wait_freed(pe, ("pct", h // 2))
                            mm(b[job["rows"], 0:S], kvc[0:N_CMP, 1, g, :], pcT[0:N_CMP, h, :], True, False)
                        pe.wait_ge(t_out, j + 1)
                        for d in range(len(job["dest"])):
                            for kt in range(T):
                                first = job["first"] and job["cmp"] is None
                                more = job["y"][0] == "yb" and job["cmp"] is not None
                                ins = mm(b[job["rows"], d * S:(d + 1) * S], job["v"](kt)[d], Tb[:, j % 2, kt, :],
                                         first and kt == 0, kt == T - 1 and not more)
                        ins.then_inc(y_full, 1)

            pe.wait_ge(in_small, 16)
            turn("norm1", H1)
            wait_normed(pe, "norm1")
            token_major("win", N_WIN, HT, PROJ - 512 * (N_WIN - 1))
            for kv, at in enumerate((KC, VC)):
                b = open_bank(("win2", kv))
                wait_freed(pe, ("win", N_WIN - 1, 0))
                wait_freed(pe, ("win", N_WIN - 1, 1))
                for g in range(KV_HEADS):
                    for par in range(2):
                        for t in range(T):
                            ins = mm(b[HD * par:HD * par + HD, g * P + t * HD:g * P + (t + 1) * HD],
                                     projv[:, t, heads_v(at, g)], ident[:, par::2], True, True)
                ins.then_inc(bank_full, 1)

            def merge_gates(gs):
                for g in gs:
                    b = open_bank(("mg", g))
                    for c in range(2):
                        ins = feature_tile(b[:, c * S:(c + 1) * S], ("mg", 2 * g + c), HT)
                    ins.then_inc(bank_full, 1)

            merge_gates(range(4))
            pe.wait_ge(blocks_done, 2)
            for kv in range(2):
                b = open_bank(("hid", kv))
                for q in range(4):
                    w = tiles_of(weights_of("cmp", kv, q), k=4)
                    for kk in range(4):
                        k = 4 * q + kk
                        ins = mm3(b[0:2 * N_CMP, 0:CMP_HID], lambda a: blocksT[:, a, kv, k, :, :].rearrange("p g n -> p (g n)"),
                                  lambda c: w(c)[:, kk, :], k == 0, k == 15)
                ins.then_inc(bank_full, 1)
            merge_gates([4])
            pe.wait_ge(in_layer1, 16)
            for kv in range(2):
                b = open_bank(("hidT", kv))
                pe.wait_ge(cmp_gelu, kv + 1)
                for k in range(2):
                    ins = pe.transpose(b[:, k * 32:k * 32 + 2 * N_CMP], hid[0:2 * N_CMP, kv, k * P:(k + 1) * P],
                                       ident[0:2 * N_CMP, 0:2 * N_CMP])
                ins.then_inc(bank_full, 1)
            merge_gates([5])
            for kv in range(2):
                b = open_bank(("c2", kv))
                wait_freed(pe, ("hidT", kv))
                for g in range(KV_HEADS):
                    for k in range(2):
                        ins = mm(b[0:N_CMP, g * HD:(g + 1) * HD], hidT[:, kv, k, g * N_CMP:(g + 1) * N_CMP],
                                 cw2[:, kv, k, :], k == 0, k == 1)
                ins.then_inc(bank_full, 1)
            merge_gates([6])
            b = open_bank(("kcT",))
            pe.wait_ge(cmp_key, 1)
            for g in range(KV_HEADS):
                ins = mm(b[HD * g:HD * g + HD, 0:N_CMP], kvc[0:N_CMP, 0, g, :], ident[0:N_CMP, 0:N_CMP], True, True)
            ins.then_inc(bank_full, 1)
            merge_gates([7])
            pe.wait_ge(head_done, 4)
            for m in range(7):
                b = open_bank(("qkt", m))
                for s in range(2):
                    for t in range(T):
                        ins = pe.transpose(b[:, s * S + t * P:s * S + (t + 1) * P],
                                           projq[:, t, (2 * m + s) * P:(2 * m + s + 1) * P], ident)
                ins.then_inc(bank_full, 1)
            wait_freed(pe, ("qkt", 3))
            wait_freed(pe, ("kcT",))
            for h in range(B_HEADS):
                g, r = h // 4, h % 4
                if r == 0:
                    b = open_bank(("scmp", g))
                for t in range(T):
                    ins = mm(b[:, (2 * r + t) * 16:(2 * r + t) * 16 + N_CMP], qkT[HD * g:HD * g + HD, 4 + r, tok(t)],
                             kcT[HD * g:HD * g + HD, 0:N_CMP], True, True)
                if r == 3:
                    ins.then_inc(bank_full, 1)
            wait_freed(pe, ("qkt", 6))
            pe.wait_ge(pads, 1)
            pe.wait_ge(cmp_prob, 1)
            for m in range(4):
                b = open_bank(("pct", m))
                for s in range(2):
                    for t in range(T):
                        ins = pe.transpose(b[0:N_CMP, s * S + t * P:s * S + (t + 1) * P],
                                           scmp[:, (2 * m + s) * T + t, 0:N_CMP], ident)
                ins.then_inc(bank_full, 1)
            attention("ab")
            wait_freed(pe, ("yb", 3))
            for f in range(KD):
                b = open_bank(("up", f))
                w = tiles_of(weights_of("up", f), k=8)
                for br in range(2):
                    for k in range(4):
                        ins = mm3(b[:, br * S:(br + 1) * S], lambda a: w(a)[:, 4 * br + k, :],
                                  lambda c: yT[:, c, br, k, :], k == 0, k == 3)
                ins.then_inc(bank_full, 1)
            wide("out", ("out",), merged, KD, lambda k: pe.wait_ge(merged_done, k + 1))

            turn("norm2", Hp)
            wait_normed(pe, "norm2")
            feature_groups(("pq",), ("wq",), 8, HT)
            for m in range(8):
                t, hp = m // 4, m % 4
                b = open_bank(("sc", m))
                wait_freed(pe, ("pq", 2 * hp + 1))
                for s in range(4):
                    ins = mm(b[:, s * P:(s + 1) * P], pq[:, 4 * hp + s, tok(t)], pkeys[:, s % 2, :], True, True)
                ins.then_inc(bank_full, 1)
            for i in range(DEPTH2):
                if i:
                    wait_wide(pe, "xv0")
                turn(f"mem{i}", memN)
                wait_normed(pe, f"mem{i}")
                feature_groups(("xk", i), ("xk", i), 4, memT)
                wide(f"xv{i}", ("xv", i), memT, KD, lambda k: None)
            pe.wait_ge(ex_done, 1)
            for m in range(3):
                b = open_bank(("et", m))
                for t in range(T):
                    src = ex[:, m, t, :] if m < 2 else tv[:, t, :, :].rearrange("p h k -> p (h k)")
                    ins = pe.transpose(b[:, tok(t)], src, ident)
                    if m == t == 0:
                        ins.then_inc(w_freed, 1)
                ins.then_inc(bank_full, 1)
            wait_wide(pe, "xv1")
            pe.sem_inc(hot_full, BEGIN)
            with pe.Fori(0, S // 8) as i:
                for half in range(2):
                    pe.wait_ge(hot_by_d, i * 2 + (half + 1))
                    pe.wait_ge(hot_by_p, i * 2 + (half + 1))
                    pe.wait_ge(hot_out, i * 2 + (half - 1 + BEGIN))
                    for j in range(4):
                        ins = pe.matmul(PS[half][:, j * P:(j + 1) * P], hots[:, half, 0, j, :], hots[:, half, 1, j, :],
                                        start=True, stop=True)
                    ins.then_inc(hot_full, 1)
            pe.wait_ge(hot_out, BEGIN + S // 4)

            def times_u(e, s):
                pe.wait_ge(u_lo, e + 1)
                if not isinstance(e, int) or e >= 2:
                    pe.wait_ge(a_gelu, e - 1)
                w = tiles_of(lambda part: wsplit[:, s, part, :], k=KD)
                for k in range(KD):
                    ins = mm3(PS[s][:, 0:S], lambda a: w(a)[:, k, :], lambda b: HT[:, b, k, :], k == 0, k == KD - 1)
                ins.then_inc(a_full, 1)

            def times_v(e, s, stop=False):
                pe.wait_ge(v_lo, e + 1)
                pe.wait_ge(a_w, e + (1 + BEGIN))
                for t in range(T):
                    for h in range(2):
                        ins = mm3(PS[4 + 2 * t + h][:, :], lambda a: wexp[:, s, a, tok(t)],
                                  lambda b: wsplit[:, 2 + s, b, h * 512:(h + 1) * 512], False, stop, skip_group_check=True)
                ins.then_inc(a_v, 1)

            pe.wait_ge(a_w, BEGIN)
            for b in range(4):
                ins = pe.matmul(PS[4 + b][:, :], act_e[:, 0, 0:P], smalls[:, 0:512], start=True, stop=False,
                                skip_group_check=True)
            ins.then_inc(a_v, BEGIN)
            times_u(0, 0)
            times_u(1, 1)
            times_v(0, 0)
            with pe.Fori(1, NKEYS // 2) as i:
                for s in range(2):
                    times_u(i * 2 + s, s)
                    times_v(i * 2 + (s - 1), 1 - s)
            times_v(NKEYS - 1, 1, stop=True)

            wait_wide(pe, "peer")
            turn("attn", H2)
            wait_normed(pe, "attn")
            token_major("qkv", 3, HT)
            for m in range(5):
                b = open_bank(("qkt2", m))
                pe.wait_ge(head_done, 6 if m < 4 else 7)
                for s in range(2):
                    for t in range(T):
                        ins = pe.transpose(b[:, s * S + t * P:s * S + (t + 1) * P],
                                           qkv[:, t, (2 * m + s) * P:(2 * m + s + 1) * P], ident)
                ins.then_inc(bank_full, 1)
            wait_freed(pe, ("qkt2", 4))
            pe.wait_ge(pads, 2)
            attention("self")
            wide("wo", ("wo",), oT, KD, lambda k: wait_freed(pe, ("y2", k)))
            for i in range(DEPTH2):
                if i:
                    pe.wait_ge(norm_h, 2 * (NORMS.index("pool") + 1))
                    pe.wait_ge(in_band, 16)
                    for g in range(4):
                        b = open_bank(("pm", g))
                        for c in range(2):
                            for s in range(T):
                                at = (2 * g + c) * P
                                ins = mm(b[:, c * S:(c + 1) * S], H2[:, s, at:at + P], bandm[:, 2 * g + s, :], s == 0, s == 1)
                        ins.then_inc(bank_full, 1)
                    for g2 in range(2):
                        w = weights_of("pool", g2)
                        pe.wait_ge(pool_lo, 4 * (g2 + 1))
                        for t in range(T):
                            b = open_bank(("py", t, g2))
                            for u in range(2):
                                for c in range(2):
                                    ct = 4 * g2 + 2 * u + c
                                    at = (2 * u + c) * S
                                    ins = mm3(b[:, u * S:(u + 1) * S], lambda a: oT[:, a, ct, tok(t)],
                                              lambda v: w(v)[:, at:at + S], c == 0, c == 1)
                            ins.then_inc(bank_full, 1)
                turn(f"x{i}", H2)
                wait_normed(pe, f"x{i}")
                feature_groups(("xq", i), ("xq", i), 4, HT)
                wait_freed(pe, ("xq", i, 3))
                pe.wait_ge(in_kv, 16 * (i + 1))
                attention(f"x{i}")
                wide(f"xo{i}", ("xo", i), oT, KD, lambda k: wait_freed(pe, ("yx", i, k // 2)))
                turn(f"ffn{i}", H2)
                wait_normed(pe, f"ffn{i}")
                feature_groups(("ffu", i), ("ffu", i), NF, HT)
                wide(f"ffd{i}", ("ffd", i), ff, NF, lambda k: pe.wait_ge(conv_m, NF * i + k + 1))

        @block.gpsimd
        def _(pool):
            def lo_turn(i, n0, slots):
                for s in slots:
                    pool.wait_ge(w_hi, i * RAW + (s + 1))
                    pool.tensor_tensor(wsplit[:, s % NSPLIT, 1, :], sb_raw(n0 + s), f32(wsplit[:, s % NSPLIT, 0, :]),
                                       ALU.subtract).then_inc(w_lo[1], 1)

            odd = range(1, RAW, 2)
            with pool.Fori(0, FIRST2 // RAW) as i:
                lo_turn(i, 0, odd)
            wait_unit_used(pool, FIRST2)
            wait_freed(pool, ("et", 2))
            with pool.Fori(0, S // 8) as i:
                for half in range(2):
                    pool.wait_ge(hot_full, i * 2 + (half - 1 + BEGIN))
                    pool.wait_ge(few_made, i * 2 + (half + 1))
                    pool.sem_inc(few_seen, 1)
                    for j in (0, 1):
                        ins = pool.tensor_scalar(hots[:, half, 1, 2 + j, :], iota, few[:, half, 0, j:j + 1],
                                                 few[:, half, 1, j:j + 1], ALU.is_equal, ALU.mult)
                    ins.then_inc(hot_by_p, 1)

            with pool.Fori(0, NKEYS // 2) as i:
                for s in range(2):
                    pool.wait_ge(u_hi, i * 2 + (s + 1))
                    pool.tensor_tensor(wsplit[:, s, 1, :], raw0[:, s, :], f32(wsplit[:, s, 0, :]), ALU.subtract)\
                        .then_inc(u_lo, 1)
            turns = len(UNITS) // RAW
            with pool.Fori(FIRST2 // RAW, turns) as i:
                lo_turn(i, FIRST2, odd)
            lo_turn(turns, FIRST2, range(1, len(UNITS) % RAW, 2))

        @block.scalar
        def _(act):
            split, limit = [0], [FIRST2]

            def split_to(u1):
                for u in range(split[0], min(u1, limit[0])):
                    act.wait_ge(w_landed[u % RAW], 16 * (u // RAW + 1))
                    if u >= NSPLIT:
                        act.wait_ge(w_freed, u - NSPLIT + 1)
                    act.activation(wsplit[:, u % NSPLIT, 0, :], sb_raw(u), ACT.Copy).then_inc(w_hi, 1)
                    split[0] = u + 1

            def full(name):
                split_to(units_to(name) + 3)
                wait_full(act, name)

            def norm_sums(name, src, H):
                i = NORMS.index(name)
                before = [TURNS.index(n) + 1 for n in NORMS[:i] if n in TURNS]
                if before:
                    act.wait_ge(norm_t, 4 * before[-1])
                for t in range(T):
                    act.activation(H[:, t, :], src[:, t, :], ACT.Square, accum_out=stat[:, t:t + 1]).then_inc(norm_sq, 1)
                act.wait_ge(norm_sq, 2 * i + 2)
                act.activation(stat[:, 2:4], stat[:, 0:2], ACT.Sqrt, bias=eps, scale=1.0 / D).then_inc(norm_root, 1)

            def norm_out(name, dst):
                i, n = TURNS.index(name), GAINS_OF.index(name)
                for b in range(4):
                    act.wait_ge(norm_t, 4 * i + b + 1)
                    for c in (2 * b, 2 * b + 1):
                        act.activation(dst[:, 0, c, :], PS[b][:, (c % 2) * S:(c % 2 + 1) * S], ACT.Copy,
                                       scale=gains[:, n, c:c + 1]).then_inc(norm_a, 1)

            def copy_bank(name, dst, width=512, rows=P):
                full(name)
                src = bank(name)[0:rows, 0:width]
                if len(dst.shape) == 3:
                    src = src.rearrange("p (a b) -> p a b", a=dst.shape[1])
                act.activation(dst, src, ACT.Copy).then_inc(bank_freed["a"], 1)

            def copy_keys(name, dst):
                full(name)
                src = bank(name)[:, :].rearrange("p (a b) -> p a b", a=2)
                act.activation(dst[0:HD, 0:4:2, :], src[0:HD], ACT.Copy)
                act.activation(dst[HD:P, 1:4:2, :], src[HD:P], ACT.Copy).then_inc(bank_freed["a"], 1)

            def head_roots(k, group, hd, sq, st):
                for t in range(T):
                    wait_freed(act, group + (t,))
                act.activation(sq, hd, ACT.Square).then_inc(head_sq, 1)
                act.wait_ge(head_sum, k + 1)
                act.activation(st[1], st[0], ACT.Sqrt, bias=eps, scale=1.0 / HD).then_inc(head_root, 1)

            def attention(use):
                jobs, Sb, Pb, Tb, scale = USES[use]
                j0, n = JOBS[use], len(jobs)
                for step in range(n + 2):
                    if step < n:
                        j = j0 + step
                        act.wait_ge(s_max, j + 1)
                        if step >= 3:
                            act.wait_ge(t_full, j - 2)
                        for t in range(T):
                            src = Sb[:, j % 2, t, :] if Sb is not None else PS[j % 2][:, t * S:(t + 1) * S]
                            ins = act.activation(Pb[:, j % 3, t, :], src, ACT.Exp, bias=att[:, 1, j % 4, t:t + 1], scale=scale,
                                                 accum_out=att[:, 2, j % 4, t:t + 1])
                        ins.then_inc(s_exp, 1)
                    if step >= 2:
                        j = j0 + step - 2
                        act.wait_ge(t_full, j + 1)
                        if step >= 4:
                            act.wait_ge(y_full, j - 1)
                        act.activation(Tb[:, j % 2, :, :], PS[2 + j % 2][:, :].rearrange("p (a b) -> p a b", a=T),
                                       ACT.Copy).then_inc(t_out, 1)

            act.dma_start(smalls[:, :], small).then_inc(in_small, 16)
            act.wait_ge(in_x, 16)
            act.wait_ge(in_small, 16)
            norm_sums("norm1", X1, H1)
            split_to(3)
            norm_out("norm1", HT)
            for n in range(N_WIN):
                full(("win", n, 1))
                for dst, cols in win_parts(n, 1):
                    ins = act.activation(dst, bank(("win", n, 1))[:, cols], ACT.Copy)
                ins.then_inc(bank_freed["a"], 1)
                if n < 4:
                    head_roots(n, ("win", n), *head_block1(n))
            wait_freed(act, ("win", N_WIN - 1, 0))
            wait_freed(act, ("win", N_WIN - 1, 1))
            act.activation(gate3, projv[:, :, BG - NORMED:PROJ - NORMED], ACT.Sigmoid).then_inc(gate3_done, 1)

            def merge_gates(gs):
                for g in gs:
                    full(("mg", g))
                    for c in range(2):
                        n = 2 * g + c
                        ins = act.activation(mgate[:, n % KD, n // KD, :], bank(("mg", g))[:, c * S:(c + 1) * S],
                                             ACT.Sigmoid, bias=smalls[:, BMERGE][:, n:n + 1])
                    ins.then_inc(bank_freed["a"], 1)

            merge_gates(range(4))
            merge_gates([4])
            for kv in range(2):
                wait_freed(act, ("hid", kv))
                act.activation(hid[0:2 * N_CMP, kv, :], hid[0:2 * N_CMP, kv, :], ACT.Gelu_apprx_tanh).then_inc(cmp_gelu, 1)
            merge_gates([5])
            merge_gates([6])
            act.wait_ge(cmp_sum, 1)
            act.activation(cst[0:N_CMP, 1, :], cst[0:N_CMP, 0, :], ACT.Sqrt, bias=eps[0:N_CMP], scale=1.0 / HD).then_inc(cmp_root, 1)
            merge_gates([7])
            for m in range(7):
                if m < 4:
                    copy_bank(("qkt", m), qkT[:, 2 * m:2 * m + 2, :])
                else:
                    copy_keys(("qkt", m), qkT[:, 8 + 4 * (m - 4):12 + 4 * (m - 4), :])
            act.wait_ge(cmp_less, 1)
            act.activation(scmp[:, :, 0:N_CMP], scmp[:, :, 0:N_CMP], ACT.Exp, scale=HD ** -0.5).then_inc(cmp_exp, 1)
            for m in range(4):
                copy_bank(("pct", m), pcT[0:N_CMP, 2 * m:2 * m + 2, :], rows=N_CMP)
            attention("ab")
            split_to(UNIT["out", 0] + 3)
            act.wait_ge(merged_done, KD)
            act.dma_start(memN[:, :, :], mem.rearrange(tokens_first, p=P)).then_inc(in_mem, 16)
            split_to(UNIT["out", 4])
            act.wait_ge(in_mem, 16)
            norm_sums("mem", memN, Hp)
            split_to(units_to(("out",)) + 3)

            wait_wide(act, "out")
            act.dma_start(park[0], X1[:, :, :].rearrange("p t d -> p (t d)")).then_inc(x_parked, 16)
            norm_sums("norm2", X1, Hp)
            norm_out("norm2", HT)
            for g in range(8):
                copy_bank(("pq", g), pq[:, 2 * g:2 * g + 2, :])
            for m in range(8):
                t, hp = m // 4, m % 4
                copy_bank(("sc", m), sc[:, t, 2 * hp:2 * hp + 2, :, :].rearrange("p h s n -> p (h s n)"))
            for i in range(DEPTH2):
                norm_out(f"mem{i}", memT)
                if i:
                    act.wait_ge(k_parked, 16)
                for g in range(4):
                    copy_bank(("xk", i, g), kout[:, 2 * g:2 * g + 2, :])
                wait_freed(act, ("xk", i, 3))
                act.dma_start(park[1 + 2 * i], kout[:, :, :].rearrange("p k s -> p (k s)")).then_inc(k_parked, 16)
                split_to(units_to(("xv", i)) + 3)
                act.wait_ge(wide_done, 2 + i)
                if i:
                    act.wait_ge(v_parked, 16)
                for t in range(T):
                    for h in range(2):
                        act.activation(Hp[:, t, h * 512:(h + 1) * 512], PS[2 * t + h][:, :], ACT.Copy).then_inc(wide_out, 1)
                wait_wide(act, f"xv{i}")
                act.dma_start(park[2 + 2 * i], Hp[:, :, :].rearrange("p t d -> p (t d)")).then_inc(v_parked, 16)
            act.wait_ge(gate_less, 1)
            act.activation(tv[:, :, :, :], tv[:, :, :, :], ACT.Exp).then_inc(gate_exp, 1)
            wait_unit_used(act, FIRST2)
            for m in range(3):
                copy_bank(("et", m), eT[:, m, :], S)
            act.wait_ge(x_parked, 16)
            act.wait_ge(k_parked, 32)
            act.wait_ge(v_parked, 32)
            act.sem_inc(hot_out, BEGIN)
            with act.Fori(0, S // 8) as i:
                for half in range(2):
                    act.wait_ge(hot_full, i * 2 + (half + 1 + BEGIN))
                    act.activation(gates[:, :, bass.ds(i * 8 + 4 * half, 4)].rearrange("p i t -> p t i"),
                                   PS[half][:, :].rearrange("p (t i) -> p t i", t=4), ACT.Copy).then_inc(hot_out, 1)
            act.wait_ge(hot_out, BEGIN + S // 4)

            def first_part(e, s, landed, turn, used, count, place, made):
                act.wait_ge(landed[s], turn)
                if count is not None:
                    act.wait_ge(used, count)
                act.activation(wsplit[:, place + s, 0, :], raw0[:, place + s, :], ACT.Copy).then_inc(made, 1)

            def gelu(e, s):
                act.wait_ge(a_full, e + 1)
                act.wait_ge(a_w, e + (BEGIN - 1))
                act.activation(act_e[:, s, :], PS[s][:, 0:S], ACT.Gelu_apprx_tanh).then_inc(a_gelu, 1)

            act.wait_ge(w_freed, FIRST2)
            first_part(0, 0, u_landed, 16, a_full, None, 0, u_hi)
            first_part(0, 0, v_landed, 16, a_v, None, 2, v_hi)
            first_part(1, 1, u_landed, 16, a_full, None, 0, u_hi)
            act.wait_ge(a_v, BEGIN)
            with act.Fori(0, NKEYS // 2 - 1) as i:
                for s in range(2):
                    e = i * 2 + s
                    gelu(e, s)
                    first_part(e + 2, s, u_landed, i * 16 + 32, a_full, i * 2 + (s + 1), 0, u_hi)
                    first_part(e + 1, 1 - s, v_landed, i * 16 + (16 if s == 0 else 32), a_v, i * 2 + (s + BEGIN), 2, v_hi)
            gelu(NKEYS - 2, 0)
            first_part(NKEYS - 1, 1, v_landed, 8 * NKEYS, a_v, NKEYS - 2 + BEGIN, 2, v_hi)
            gelu(NKEYS - 1, 1)
            act.wait_ge(a_v, NKEYS + BEGIN)

            limit[0] = len(UNITS)
            split_to(FIRST2 + 3)
            wait_wide(act, "peer")
            norm_sums("attn", X2, H2)
            norm_out("attn", HT)
            for n in range(3):
                copy_bank(("qkv", n, 1), qkv[:, 1, 512 * n:512 * (n + 1)])
                head_roots(4 + n, ("qkv", n), *head_block2(n))
            for m in range(4):
                copy_bank(("qkt2", m), qkT2[:, 2 * m:2 * m + 2, :])
            copy_keys(("qkt2", 4), qkT2[:, 8:12, :])
            attention("self")
            split_to(units_to(("wo",)) + 3)
            wait_wide(act, "wo")
            for i in range(DEPTH2):
                if i:
                    norm_sums("pool", X2, H2)
                    for g in range(4):
                        full(("pm", g))
                        for c in range(2):
                            ct = 2 * g + c
                            ins = act.activation(oT[:, 0, ct, :], bank(("pm", g))[:, c * S:(c + 1) * S], ACT.Copy,
                                                 scale=gains[:, GAINS_OF.index("pool"), ct:ct + 1])
                        ins.then_inc(pool_hi, 1)
                    split_to(units_to(("py", 0, 1)) + 3)
                    act.wait_ge(pool_done, 4)
                norm_sums(f"x{i}", X2, H2)
                norm_out(f"x{i}", HT)
                for g in range(4):
                    copy_bank(("xq", i, g), qxT[:, 2 * g:2 * g + 2, :])
                attention(f"x{i}")
                if i == 0:
                    act.wait_ge(y_full, JOBS["x1"])
                    act.dma_start(kv_in[:, :, :], park[3:5].rearrange("w p d -> p w d")).then_inc(in_kv, 16)
                split_to(units_to(("xo", i)) + 3)
                wait_wide(act, f"xo{i}")
                norm_sums(f"ffn{i}", X2, H2)
                norm_out(f"ffn{i}", HT)
                for f in range(NF + 1):
                    if f < NF:
                        full(("ffu", i, f))
                        if f >= 2:
                            act.wait_ge(conv_m, NF * i + f - 1)
                        for c in range(2):
                            w = conv[:, i, c * NF + f, :]
                            ins = act.activation(cv[:, f % 2, c, :], bank(("ffu", i, f))[:, c * S:(c + 1) * S], ACT.Identity,
                                                 bias=w[:, 3:4], scale=w[:, 1:2])
                        ins.then_inc(conv_a, 1)
                    if f:
                        act.wait_ge(conv_d, NF * i + f)
                        g = (f - 1) % 2
                        act.activation(cv[:, g, 0, :], cv[:, g, 0, :], ACT.Silu).then_inc(conv_s, 1)
                split_to(units_to(("ffd", i)) + 3)
                wait_wide(act, f"ffd{i}")
            norm_sums("final", X2, H2)

        @block.vector
        def _(dve):
            links, split, limit = [0], [0], [FIRST2]

            def split_to(u1):
                for u in range(split[0], min(u1, limit[0])):
                    if u % 2 == 0:
                        dve.wait_ge(w_hi, u + 1)
                        dve.tensor_tensor(wsplit[:, u % NSPLIT, 1, :], sb_raw(u), f32(wsplit[:, u % NSPLIT, 0, :]),
                                          ALU.subtract).then_inc(w_lo[0], 1)
                    split[0] = u + 1

            def full(name):
                split_to(units_to(name) + 3)
                wait_full(dve, name)

            def link(ins):
                ins.then_inc(chain, 1)
                links[0] += 1
                dve.wait_ge(chain, links[0])

            def parts(hi, lo, src):
                link(dve.tensor_copy(hi, src))
                return dve.tensor_tensor(lo, src, f32(hi), ALU.subtract)

            def norm_scale(name, src, H):
                i = NORMS.index(name)
                dve.wait_ge(norm_root, i + 1)
                link(dve.reciprocal(stat[:, 4:6], stat[:, 2:4]))
                for t in range(T):
                    dve.tensor_scalar(H[:, t, :], src[:, t, :], stat[:, 4 + t:5 + t], None, ALU.mult).then_inc(norm_h, 1)

            def norm_out(name, dst):
                i, n = TURNS.index(name), GAINS_OF.index(name)
                for b in range(4):
                    dve.wait_ge(norm_a, KD * i + 2 * b + 2)
                    for c in (2 * b, 2 * b + 1):
                        dve.scalar_tensor_tensor(out=dst[:, 1, c, :], in0=PS[b][:, (c % 2) * S:(c % 2 + 1) * S],
                                                 scalar=gains[:, n, c:c + 1], in1=f32(dst[:, 0, c, :]), op0=ALU.mult,
                                                 op1=ALU.subtract).then_inc(norm_d, 1)

            def copy_bank(name, dst, src):
                full(name)
                dve.tensor_copy(dst, src).then_inc(bank_freed["d"], 1)

            def wide_read(name, dst):
                split_to(units_to(split_word(name)) + 3)
                dve.wait_ge(wide_done, sum(1 for n in WIDE[:WIDE.index(name) + 1] if n != "peer"))
                for t in range(T):
                    for h in range(2):
                        o = dst[:, t, h * 512:(h + 1) * 512]
                        dve.tensor_tensor(o, o, PS[2 * t + h][:, :], ALU.add).then_inc(wide_out, 1)

            def head_norm(k, hd, sq, st, kinds, rope, ahead):
                n = hd.shape[2] // HD
                hv = hd.rearrange("p t (h d) -> p t h d", d=HD)
                dve.wait_ge(head_sq, k + 1)
                dve.tensor_reduce(st[0], sq.rearrange("p t (h d) -> p t h d", d=HD), AXX, ALU.add).then_inc(head_sum, 1)
                split_to(ahead + 4)
                dve.wait_ge(head_root, k + 1)
                link(dve.reciprocal(st[2], st[1]))
                link(dve.tensor_tensor(hv, hv, st[2].unsqueeze(3).to_broadcast([P, T, n, HD]), ALU.mult))
                at = 0
                for m, gain in kinds:
                    v = hv[:, :, at:at + m, :]
                    ins = dve.tensor_tensor(v, v, gain.unsqueeze(1).unsqueeze(1).to_broadcast([P, T, m, HD]), ALU.mult)
                    at += m
                link(ins)
                split_to(ahead + 5)
                rope(hv, n)

            def rotate(x1, x2, c, s, tmp):
                dve.tensor_tensor(tmp[0], x1, c, ALU.mult)
                dve.tensor_tensor(tmp[1], x2, s, ALU.mult)
                dve.tensor_tensor(tmp[2], x2, c, ALU.mult)
                link(dve.tensor_tensor(tmp[3], x1, s, ALU.mult))
                dve.tensor_tensor(x1, tmp[0], tmp[1], ALU.subtract)
                return dve.tensor_tensor(x2, tmp[2], tmp[3], ALU.add)

            def rope_first(hv, n):
                c, s = (rope1[:, w, :, :].unsqueeze(2).to_broadcast([P, T, n, 8]) for w in range(2))
                rotate(hv[:, :, :, 0:8], hv[:, :, :, 8:16], c, s,
                       [rtmp1[:, w, :, 0:n, :] for w in range(4)]).then_inc(head_done, 1)

            def rope_axial(hv, n):
                for t in range(T):
                    h2 = hv[:, t, :, :].rearrange("p h (a x j) -> p h a x j", a=2, x=2)
                    c, s = (rope2[:, w, t, :, :].unsqueeze(1).to_broadcast([P, n, 2, 16]) for w in range(2))
                    ins = rotate(h2[:, :, :, 0, :], h2[:, :, :, 1, :], c, s, [rtmp2[:, t, w, 0:n] for w in range(4)])
                ins.then_inc(head_done, 1)

            def attention(use):
                jobs, Sb, Pb, Tb, scale = USES[use]
                j0, n = JOBS[use], len(jobs)
                for step in range(n + 4):
                    if step < n:
                        j = j0 + step
                        dve.wait_ge(s_full, j + 1)
                        if step >= 2:
                            dve.wait_ge(s_exp, j - 1)
                        mx = att[:, 0, j % 4, :]
                        b = PS[j % 2][:, :].rearrange("p (t n) -> p t n", t=T)
                        if Sb is not None:
                            for t in range(T):
                                ins = dve.tensor_tensor_reduce(Sb[:, j % 2, t, :], b[:, t, :], mask[:, t, :], 1.0, LOW, ALU.add,
                                                               ALU.max, mx[:, t:t + 1])
                            link(ins)
                        else:
                            link(dve.tensor_reduce(mx, b, AXX, ALU.max))
                        dve.tensor_scalar(att[:, 1, j % 4, :], mx, -scale, None, ALU.mult).then_inc(s_max, 1)
                    if 1 <= step <= n:
                        job, j = jobs[step - 1], j0 + step - 1
                        dve.wait_ge(s_exp, j + 1)
                        link(dve.reciprocal(att[:, 3, j % 4, :], att[:, 2, j % 4, :]))
                        for t in range(T):
                            r, p = att[:, 3, j % 4, t:t + 1], Pb[:, j % 3, t, :]
                            if job["gate"] is None:
                                ins = dve.tensor_scalar(p, p, r, None, ALU.mult)
                            else:
                                ins = dve.tensor_scalar(p, p, r, job["gate"](t), ALU.mult, ALU.mult)
                        ins.then_inc(s_prob, 1)
                    if step >= 4 and jobs[step - 4]["last"]:
                        job, j = jobs[step - 4], j0 + step - 4
                        dve.wait_ge(y_full, j + 1)
                        for d, dest in enumerate(job["dest"]):
                            ins = parts(dest[:, 0, :], dest[:, 1, :], bank(job["y"])[:, d * S:(d + 1) * S])
                        ins.then_inc(bank_freed["d"], 1)

            dve.wait_ge(in_x, 16)
            dve.wait_ge(in_small, 16)
            norm_scale("norm1", X1, H1)
            split_to(3)
            norm_out("norm1", HT)
            hg = smalls[:, HG1].rearrange("p (n d) -> p n d", n=5)
            kinds = [[(8, hg[:, 0, :])], [(8, hg[:, 1, :])], [(8, hg[:, 2, :])], [(2, hg[:, 3, :]), (2, hg[:, 4, :])]]
            for n in range(N_WIN):
                full(("win", n, 0))
                for dst, cols in win_parts(n, 0):
                    ins = dve.tensor_copy(dst, bank(("win", n, 0))[:, cols])
                ins.then_inc(bank_freed["d"], 1)
                if n < 4:
                    head_norm(n, *head_block1(n), kinds[n], rope_first, units_to(("win", n, 0)))
            dve.memset(qkT[HD:P, 8:20:2, :], 0.0)
            dve.memset(qkT[0:HD, 9:20:2, :], 0.0).then_inc(pads, 1)
            dve.wait_ge(in_layer1, 16)
            for kv in range(2):
                full(("win2", kv))
                for g in range(KV_HEADS):
                    for kh in range(2):
                        src = bank(("win2", kv))[:, g * P + 8 * kh:g * P + 8 * kh + 8 * N_CMP]
                        pos = cpos[:, kv, 8 * kh:8 * kh + 8].unsqueeze(2).to_broadcast([P, 8, N_CMP])
                        ins = dve.tensor_tensor(blocks[:, kv, 8 * kh:8 * kh + 8, g, :],
                                                src.rearrange("p (n k) -> p k n", k=8), pos, ALU.add)
                ins.then_inc(bank_freed["d"], 1)
                wait_freed(dve, ("win2", kv))
                parts(*(blocksT[:, part, kv, :, :, :].rearrange("p k g n -> p (k g n)") for part in range(2)),
                      blocks[:, kv, :, :, :].rearrange("p k g n -> p (k g n)")).then_inc(blocks_done, 1)
            for kv in range(2):
                full(("hid", kv))
                dve.tensor_tensor(hid[0:2 * N_CMP, kv, :], bank(("hid", kv))[0:2 * N_CMP, 0:CMP_HID],
                                  cb1[0:2 * N_CMP, kv, :], ALU.add).then_inc(bank_freed["d"], 1)
            split_to(units_to(("mg", 4)) + 3)
            for kv in range(2):
                copy_bank(("hidT", kv), hidT[:, kv, :, :],
                          bank(("hidT", kv))[:, 0:64].rearrange("p (k n) -> p k n", k=2)[:, :, 0:2 * N_CMP])
            split_to(units_to(("mg", 5)) + 3)
            w = slice(0, N_CMP)
            for kv in range(2):
                full(("c2", kv))
                dve.tensor_tensor(kvc[w, kv, :, :], bank(("c2", kv))[w, 0:2 * HD].rearrange("p (g d) -> p g d", g=2),
                                  cb2[w, kv, :].unsqueeze(1).to_broadcast([N_CMP, 2, HD]), ALU.add).then_inc(bank_freed["d"], 1)
            wait_freed(dve, ("c2", 0))
            link(dve.tensor_tensor(ctmp[w, 0, :, :], kvc[w, 0, :, :], kvc[w, 0, :, :], ALU.mult))
            dve.tensor_reduce(cst[w, 0, :], ctmp[w, 0, :, :], AXX, ALU.add).then_inc(cmp_sum, 1)
            split_to(units_to(("mg", 6)) + 3)
            dve.wait_ge(cmp_root, 1)
            link(dve.reciprocal(cst[w, 2, :], cst[w, 1, :]))
            link(dve.tensor_tensor(kvc[w, 0, :, :], kvc[w, 0, :, :], cst[w, 2, :].unsqueeze(2).to_broadcast([N_CMP, 2, HD]),
                                   ALU.mult))
            dve.tensor_tensor(kvc[w, 0, :, :], kvc[w, 0, :, :], kcg[w].unsqueeze(1).to_broadcast([N_CMP, 2, HD]),
                              ALU.mult).then_inc(cmp_key, 1)
            copy_bank(("kcT",), kcT[:, 0:N_CMP], bank(("kcT",))[:, 0:N_CMP])
            split_to(units_to(("mg", 7)) + 3)
            sc4 = scmp[:, :, :].rearrange("p (h t) n -> p h t n", t=T)[:, :, :, w]
            sc3 = scmp[:, :, w]
            for g in range(KV_HEADS):
                full(("scmp", g))
                src = bank(("scmp", g))[:, 0:4 * T * 16].rearrange("p (r t n) -> p r t n", r=4, t=T)[:, :, :, w]
                dve.tensor_tensor(sc4[:, 4 * g:4 * g + 4], src, cmask.unsqueeze(1).to_broadcast([P, 4, T, N_CMP]),
                                  ALU.add).then_inc(bank_freed["d"], 1)
            wait_freed(dve, ("scmp", 1))
            link(dve.tensor_reduce(cred[:, 0, :], sc3, AXX, ALU.max))
            dve.tensor_tensor(sc3, sc3, cred[:, 0, :].unsqueeze(2).to_broadcast([P, 16, N_CMP]), ALU.subtract)\
               .then_inc(cmp_less, 1)
            dve.wait_ge(cmp_exp, 1)
            link(dve.tensor_reduce(cred[:, 1, :], sc3, AXX, ALU.add))
            link(dve.reciprocal(cred[:, 2, :], cred[:, 1, :]))
            r2 = cred[:, 2, :].rearrange("p (h t) -> p h t", t=T)
            link(dve.tensor_tensor(r2, r2, cany.unsqueeze(1).to_broadcast([P, 8, T]), ALU.mult))
            dve.wait_ge(gate3_done, 1)
            link(dve.tensor_tensor(r2, r2, gate3.rearrange("p t (h b) -> p h t b", b=3)[:, :, :, 0], ALU.mult))
            dve.tensor_tensor(sc3, sc3, cred[:, 2, :].unsqueeze(2).to_broadcast([P, 16, N_CMP]), ALU.mult).then_inc(cmp_prob, 1)
            attention("ab")
            for f in range(KD):
                full(("up", f))
                tmp = uptmp[:, f % 2, :, :]
                dve.tensor_tensor(tmp, bank(("up", f))[:, :].rearrange("p (b n) -> p b n", b=2), mgate[:, f, :, :],
                                  ALU.mult).then_inc(bank_freed["d"], 1)
                wait_freed(dve, ("up", f))
                link(dve.tensor_tensor(tmp[:, 0, :], tmp[:, 0, :], tmp[:, 1, :], ALU.add))
                parts(merged[:, 0, f, :], merged[:, 1, f, :], tmp[:, 0, :]).then_inc(merged_done, 1)
            split_to(UNIT["out", 4])
            norm_scale("mem", memN, memN)
            wide_read("out", X1)

            norm_scale("norm2", X1, Hp)
            norm_out("norm2", HT)

            def top16(values, spare, v, ix):
                link(dve.max(v[:, 0:8], values))
                dve.max_index(ix[:, 0:8], v[:, 0:8], values)
                link(dve.match_replace(spare, v[:, 0:8], values, LOW))
                link(dve.max(v[:, 8:16], spare))
                return dve.max_index(ix[:, 8:16], v[:, 8:16], spare)

            first_kv = UNIT["xk", 0, 0]
            split_to(first_kv + 3)
            for m in range(8):
                wait_freed(dve, ("sc", m))
                t = m // 4
                for h in range(2 * (m % 4), 2 * (m % 4) + 2):
                    for s in range(2):
                        ins = top16(sc[:, t, h, s, :], srep[:, s, :], v16[:, t, h, s, :], i16[:, t, h, s, :])
                    link(ins)
                    link(dve.tensor_tensor(cand[:, 0, :, :], v16[:, t, h, 0, :].unsqueeze(2).to_broadcast([P, TOPK, TOPK]),
                                           v16[:, t, h, 1, :].unsqueeze(1).to_broadcast([P, TOPK, TOPK]), ALU.add))
                    link(top16(cand[:, 0, :, :].rearrange("p a b -> p (a b)"), cand[:, 1, :, :].rearrange("p a b -> p (a b)"),
                               tv[:, t, h, :], ti[:, t, h * TOPK:(h + 1) * TOPK]))
                    step = t * PEER_HEADS + h
                    if step == 0:
                        norm_out("mem0", memT)
                    if step == 6:
                        split_to(units_to(("xv", 0)) + 3)
                        norm_out("mem1", memT)
                    split_to(first_kv + 2 * (step + 1) + 3)
            link(dve.tensor_copy(gsum[:, 0, :, :], tv[:, :, :, 0]))
            dve.tensor_tensor(tv[:, :, :, :], tv[:, :, :, :], gsum[:, 0, :, :].unsqueeze(3).to_broadcast([P, T, 8, TOPK]),
                              ALU.subtract).then_inc(gate_less, 1)
            link(dve.tensor_scalar(tab[:, 0, :, :], ti[:, :, :], 4, None, ALU.logical_shift_right))
            link(dve.tensor_scalar(tab[:, 1, :, :], ti[:, :, :], 15, None, ALU.bitwise_and))
            link(dve.tensor_copy(tabf[:, :, :, :], tab[:, :, :, :]))
            link(dve.tensor_copy(i16f[:, :, :, :, :], i16[:, :, :, :, :]))
            for t in range(T):
                for s in range(2):
                    link(dve.tensor_tensor(onehot16[:, :, :], tabf[:, s, t, :].unsqueeze(2).to_broadcast([P, P, TOPK]),
                                           iota[:, 0:TOPK].unsqueeze(1).to_broadcast([P, P, TOPK]), ALU.is_equal))
                    o4 = onehot16[:, :, :].rearrange("p (h k) j -> p h k j", h=PEER_HEADS)
                    link(dve.tensor_tensor(o4, o4, i16f[:, t, :, s, :].unsqueeze(2).to_broadcast([P, PEER_HEADS, TOPK, TOPK]),
                                           ALU.mult))
                    link(dve.tensor_reduce(ex[:, 1 - s, t, :], onehot16[:, :, :], AXX, ALU.add))
            dve.wait_ge(gate_exp, 1)
            link(dve.tensor_reduce(gsum[:, 0, :, :], tv[:, :, :, :], AXX, ALU.add))
            link(dve.reciprocal(gsum[:, 1, :, :], gsum[:, 0, :, :]))
            dve.tensor_tensor(tv[:, :, :, :], tv[:, :, :, :], gsum[:, 1, :, :].unsqueeze(3).to_broadcast([P, T, 8, TOPK]),
                              ALU.mult).then_inc(ex_done, 1)
            wait_unit_used(dve, FIRST2)
            wait_freed(dve, ("et", 2))
            with dve.Fori(0, S // 8) as i:
                for half in range(2):
                    dve.wait_ge(hot_full, i * 2 + (half - 1 + BEGIN))
                    dve.tensor_copy(few[:, half, :, :], eT[:, 1:3, bass.ds(i * 8 + (4 * half + 2), 2)]).then_inc(few_made, 1)
                    dve.tensor_tensor(hots[:, half, 0, :, :], iota.unsqueeze(1).to_broadcast([P, 4, NKEYS]),
                                      eT[:, 0, bass.ds(i * 8 + 4 * half, 4)].unsqueeze(2).to_broadcast([P, 4, NKEYS]),
                                      ALU.is_equal)
                    for j in (0, 1):
                        n = i * 8 + (4 * half + j)
                        ins = dve.tensor_scalar(hots[:, half, 1, j, :], iota, eT[:, 1, bass.ds(n, 1)],
                                                eT[:, 2, bass.ds(n, 1)], ALU.is_equal, ALU.mult)
                    ins.then_inc(hot_by_d, 1)
            dve.memset(act_e[:, 0, :], 0.0).then_inc(a_w, BEGIN)

            def v_second_part(e, s):
                dve.wait_ge(v_hi, e + 1)
                dve.tensor_tensor(wsplit[:, 2 + s, 1, :], raw0[:, 2 + s, :], f32(wsplit[:, 2 + s, 0, :]),
                                  ALU.subtract).then_inc(v_lo, 1)

            def weigh(e, s):
                dve.wait_ge(a_gelu, e + 1)
                dve.wait_ge(a_v, e + (BEGIN - 1))
                g = gates[:, bass.ds(e, 1), :] if not isinstance(e, int) else gates[:, e:e + 1, :]
                dve.tensor_tensor(act_e[:, s, :].unsqueeze(1), act_e[:, s, :].unsqueeze(1), g, ALU.mult).then_inc(a_mul, 1)
                dve.wait_ge(a_mul, e + 1)
                dve.tensor_copy(wexp[:, s, 0, :], act_e[:, s, :]).then_inc(a_hi, 1)
                dve.wait_ge(a_hi, e + 1)
                dve.tensor_tensor(wexp[:, s, 1, :], act_e[:, s, :], f32(wexp[:, s, 0, :]), ALU.subtract).then_inc(a_w, 1)

            v_second_part(0, 0)
            with dve.Fori(0, NKEYS // 2 - 1) as i:
                for s in range(2):
                    weigh(i * 2 + s, s)
                    v_second_part(i * 2 + (s + 1), 1 - s)
            weigh(NKEYS - 2, 0)
            v_second_part(NKEYS - 1, 1)
            weigh(NKEYS - 1, 1)
            dve.wait_ge(in_x, 32)
            dve.wait_ge(a_v, NKEYS + BEGIN)
            for t in range(T):
                for h in range(2):
                    o = X2[:, t, h * 512:(h + 1) * 512]
                    dve.tensor_tensor(o, o, PS[4 + 2 * t + h][:, :], ALU.add).then_inc(wide_out, 1)

            limit[0] = len(UNITS)
            wait_wide(dve, "peer")
            norm_scale("attn", X2, H2)
            split_to(FIRST2 + 3)
            norm_out("attn", HT)
            hg = smalls[:, HG2].rearrange("p (n d) -> p n d", n=2)
            for n in range(3):
                copy_bank(("qkv", n, 0), qkv[:, 0, 512 * n:512 * (n + 1)], bank(("qkv", n, 0))[:, :])
                head_norm(4 + n, *head_block2(n), [(8, hg[:, 0, :])] if n < 2 else [(N_KV, hg[:, 1, :])], rope_axial,
                          units_to(("qkv", n, 0)) - (2 if n == 2 else 0))
            dve.memset(qkT2[HD:P, 8:12:2, :], 0.0)
            dve.memset(qkT2[0:HD, 9:12:2, :], 0.0).then_inc(pads, 1)
            attention("self")
            wide_read("wo", X2)
            wait_wide(dve, "wo")
            for i in range(DEPTH2):
                if i:
                    norm_scale("pool", X2, H2)
                    for g in range(4):
                        dve.wait_ge(pool_hi, g + 1)
                        for c in range(2):
                            ct = 2 * g + c
                            ins = dve.scalar_tensor_tensor(
                                out=oT[:, 1, ct, :], in0=bank(("pm", g))[:, c * S:(c + 1) * S],
                                scalar=gains[:, GAINS_OF.index("pool"), ct:ct + 1], in1=f32(oT[:, 0, ct, :]),
                                op0=ALU.mult, op1=ALU.subtract).then_inc(pool_lo, 1)
                        dve.wait_ge(pool_lo, 2 * g + 2)
                        dve.sem_inc(bank_freed["d"], 1)
                    dve.wait_ge(in_wide, 16)
                    for g2 in range(2):
                        for t in range(T):
                            full(("py", t, g2))
                            cols = slice(g2 * 512, (g2 + 1) * 512)
                            tmp = ptmp[:, t, :]
                            dve.tensor_tensor(tmp, bank(("py", t, g2))[:, :], wideg[:, 0, cols],
                                              ALU.mult).then_inc(bank_freed["d"], 1)
                            wait_freed(dve, ("py", t, g2))
                            dve.tensor_tensor(X2[:, t, cols], X2[:, t, cols], tmp, ALU.add).then_inc(pool_done, 1)
                norm_scale(f"x{i}", X2, H2)
                norm_out(f"x{i}", HT)
                split_to(units_to(("xq", i, 3)) + 3)
                attention(f"x{i}")
                wide_read(f"xo{i}", X2)
                norm_scale(f"ffn{i}", X2, H2)
                norm_out(f"ffn{i}", HT)
                for f in range(NF + 1):
                    if f < NF:
                        split_to(units_to(("ffu", i, f)) + 3)
                        dve.wait_ge(conv_a, NF * i + f + 1)
                        b = bank(("ffu", i, f))
                        for tap in (0, 2):
                            for c in range(2):
                                w = conv[:, i, c * NF + f, tap:tap + 1]
                                u = b[:, c * S:(c + 1) * S]
                                o, v = (slice(1, S), slice(0, S - 1)) if tap == 0 else (slice(0, S - 1), slice(1, S))
                                y = cv[:, f % 2, c, o]
                                ins = dve.scalar_tensor_tensor(out=y, in0=u[:, v], scalar=w, in1=y, op0=ALU.mult, op1=ALU.add)
                            if tap == 0:
                                link(ins)
                            else:
                                ins.then_inc(conv_d, 1)
                        dve.wait_ge(conv_d, NF * i + f + 1)
                        dve.sem_inc(bank_freed["d"], 1)
                    if f:
                        dve.wait_ge(conv_s, NF * i + f)
                        g = (f - 1) % 2
                        link(dve.tensor_tensor(cv[:, g, 0, :], cv[:, g, 0, :], cv[:, g, 1, :], ALU.mult))
                        parts(ff[:, 0, f - 1, :], ff[:, 1, f - 1, :], cv[:, g, 0, :]).then_inc(conv_m, 1)
                wide_read(f"ffd{i}", X2)
            norm_scale("final", X2, H2)
            dve.wait_ge(in_wide, 16)
            for t in range(T):
                dve.wait_ge(norm_h, 2 * len(NORMS) - 1 + t)
                dve.tensor_tensor(H2[:, t, :], H2[:, t, :], wideg[:, 1, :], ALU.mult).then_inc(final_h, 1)


def pairs(w, axis, heads, kv):
    w = np.moveaxis(w, axis, 0)
    group = heads // kv
    w = w.reshape(kv // 2, 2, group, HD, -1).transpose(0, 2, 1, 3, 4).reshape(heads * HD, -1)
    return np.moveaxis(w, 0, axis)


def features(w):
    k, n = w.shape[0] // P, w.shape[1] // P
    return w.reshape(k, P, n, P).transpose(2, 1, 0, 3).reshape(n, P, k * P)


def rows(w, n, k):
    full = np.zeros((w.shape[0], n), np.float32)
    full[:, :w.shape[1]] = w
    return full.reshape(-1, k, P, n).transpose(0, 2, 1, 3).reshape(-1, P, k * n)


def weight_arrays(a):
    w_in = a["w_in"][0]
    at = np.cumsum([0, 512, 512, 512, 512, 128, 128, 128, 128, 128, 128, 24])
    aq, ak, av, bq, kc, vc, ks, vs, kw, vw, bg = (w_in[:, at[i]:at[i + 1]] for i in range(11))
    first = np.concatenate([aq, pairs(bq, 1, 8, 2), ak, ks, kw, av, vs, vw, kc, vc, bg], axis=1)
    out = {}

    def put(kind, units):
        for n, unit in enumerate(units):
            out[kind + (n,)] = unit

    for n in range(N_WIN):
        put(("win", n), rows(first[:, 512 * n:512 * n + 512], 512, 2))
    put(("mg",), features(w_in[:, at[11]:]))
    put(("wq",), features(a["peer_wq"][0]))
    for n, w in enumerate((a["cmp_k_w1"][0], a["cmp_v_w1"][0])):
        put(("cmp", n), rows(w, CMP_HID, 4))
    put(("up",), features(np.concatenate([a["w_up_a"][0], pairs(a["w_up_b"][0], 0, 8, 2)], axis=0)))
    put(("out",), rows(a["w_out"][0], D, 1))
    w = a["attn_w_qkv_2"][0]
    w = np.concatenate([pairs(w[:, :N_HEADS * HD], 1, N_HEADS, N_KV), w[:, N_HEADS * HD:]], axis=1)
    for n in range(3):
        put(("qkv", n), rows(w[:, 512 * n:512 * n + 512], 512, 2))
    put(("wo",), rows(pairs(a["attn_w_o_2"][0], 0, N_HEADS, N_KV), D, 1))
    put(("pool",), a["pool_w_2"][0].reshape(2, 4, P, S).transpose(0, 2, 1, 3).reshape(2, P, UNIT_COLS))
    for i in range(DEPTH2):
        put(("xk", i), features(a["xattn_w_kv_2"][i][:, :D]))
        put(("xv", i), rows(a["xattn_w_kv_2"][i][:, D:], D, 1))
        put(("xq", i), features(a["xattn_w_q_2"][i]))
        put(("xo", i), rows(a["xattn_w_o_2"][i], D, 1))
        put(("ffu", i), features(a["ffn_w_up_2"][i].reshape(D, 2, NF, P).transpose(0, 2, 1, 3).reshape(D, 2 * D_FF)))
        put(("ffd", i), rows(a["ffn_w_down_2"][i], D, 1))
    return out


def by_partition(v):
    return v.reshape(-1, P).T


def on_all(v):
    return np.broadcast_to(v.reshape(1, -1), (P, v.size))


def tables():
    pos = np.arange(S, dtype=np.float32)
    inv = np.float32(500000.0) ** (-np.arange(0, 16, 2, dtype=np.float32) / np.float32(16))
    ang = pos[:, None] * inv[None, :]
    rope1 = np.stack([np.cos(ang), np.sin(ang)]).reshape(2, T, P, 8).transpose(2, 0, 1, 3)
    inv = np.float32(10000.0) ** (-np.arange(16, dtype=np.float32) / np.float32(16))
    row, col = np.floor(pos / GRID_W).astype(np.float32), (pos % GRID_W).astype(np.float32)
    ang = np.stack([row[:, None] * inv, col[:, None] * inv], axis=1)
    rope2 = np.stack([np.cos(ang), np.sin(ang)]).reshape(2, T, P, 2, 16).transpose(2, 0, 1, 3, 4)
    tokens = np.arange(S)
    causal = np.where(tokens[None, :] <= tokens[:, None], 0.0, NEG).reshape(T, P, S).transpose(1, 0, 2)
    ends = np.arange(N_CMP) * CMP_STRIDE + CMP_LEN - 1
    seen = ends[None, :] <= tokens[:, None]
    cmask = np.where(seen, 0.0, NEG).reshape(T, P, N_CMP).transpose(1, 0, 2)
    some = seen.any(axis=1).astype(np.float32).reshape(T, P).T
    band = np.zeros((4, S, S), np.float32)
    for g, w in enumerate(POOL_WINDOWS):
        for t in range(S):
            lo, hi = max(t - w // 2, 0), min(t + w - w // 2, S)
            band[g, lo:hi, t] = 1.0 / (hi - lo)
            band[g, t, t] -= 1.0
    band = band.reshape(4, T, P, S).transpose(2, 0, 1, 3).reshape(P, 8, S)
    flat = lambda v: np.asarray(v, np.float32).reshape(P, -1)
    return flat(rope1), flat(rope2), flat(causal), flat(cmask), flat(some), np.ascontiguousarray(band)


def lay_out(a):
    rope1, rope2, causal, cmask, some, band = tables()
    units = weight_arrays(a)
    gain_of = {"norm1": a["norm1_g"][0], "norm2": a["norm2_g"][0], "attn": a["attn_norm_2"][0], "pool": a["pool_norm_2"][0]}
    for i in range(DEPTH2):
        gain_of.update({f"mem{i}": a["mem_norm_2"][i], f"x{i}": a["xattn_norm_2"][i], f"ffn{i}": a["ffn_norm_2"][i]})
    gains = [gain_of[n] for n in GAINS_OF]
    conv = np.stack([np.concatenate([a["ffn_conv_w_2"][i], a["ffn_conv_b_2"][i][None]]) for i in range(DEPTH2)])
    conv = conv.reshape(DEPTH2, 4, 2 * NF, P).transpose(3, 0, 2, 1).reshape(P, -1)
    small = np.concatenate(
        [np.eye(P, dtype=np.float32), on_all(np.arange(NKEYS, dtype=np.float32))] + [by_partition(g) for g in gains]
        + [conv, by_partition(a["b_merge"][0].reshape(-1)), a["peer_k1"][0].T, a["peer_k2"][0].T,
           np.full((P, 1), EPS, np.float32), rope1, rope2]
        + [on_all(a[n][0]) for n in ("a_q_g", "b_q_g", "a_k_g", "b_ks_g", "b_kw_g", "attn_q_gain_2", "attn_k_gain_2")], axis=1)
    layer1 = np.concatenate(
        [causal, cmask, some] + [a[n][0].reshape(16, P).T for n in ("cmp_pos_k", "cmp_pos_v")]
        + [on_all(a[n][0]) for n in ("cmp_k_b1", "cmp_v_b1", "cmp_k_b2", "cmp_v_b2")]
        + [a[n][0].reshape(2, P, HD).transpose(1, 0, 2).reshape(P, -1) for n in ("cmp_k_w2", "cmp_v_w2")]
        + [on_all(a["b_kc_g"][0])], axis=1)
    assert small.shape[1] == SM.at and layer1.shape[1] == L1.at
    return {
        "x": a["x"], "mem": a["mem_2"],
        "weights": np.stack([units[name] for name in UNITS]),
        "expert_u": a["peer_u"][0].reshape(NKEYS, NKEYS, KD, P).transpose(0, 3, 2, 1).reshape(NKEYS, P, KD * NKEYS),
        "expert_v": a["peer_v"][0].reshape(NKEYS, NKEYS, D),
        "small": small, "layer1": layer1, "band": band,
        "wide_gains": np.broadcast_to(np.stack([a["pool_scale_2"][0], a["final_norm_2"]])[None], (P, 2, D)),
    }


def kernel(**inputs):
    import concourse.bacc as bacc
    from concourse.bass_utils import run_bass_kernel_spmd

    nc = bacc.Bacc("TRN2", target_bir_lowering=False, num_devices=1)
    arrays, args = {}, []
    for name, v in lay_out({k: np.asarray(v) for k, v in inputs.items()}).items():
        arrays[name] = np.ascontiguousarray(v)
        args.append(nc.dram_tensor(name, v.shape, F32, kind="ExternalInput").ap())
    args.append(nc.dram_tensor("result", (1, S, D), F32, kind="ExternalOutput").ap())
    block_stack(nc, *args)
    r = run_bass_kernel_spmd(nc, [arrays], core_ids=[0])
    return r.results[0]["result"]
```

```python
from contextlib import ExitStack

import numpy as np
import concourse.bass as bass
from concourse import mybir

F32 = mybir.dt.float32
F32R = mybir.dt.float32r
U32 = mybir.dt.uint32
ALU = mybir.AluOpType
ACT = mybir.ActivationFunctionType
AXX = mybir.AxisListType.X

P = 128
S = 256
T = S // P
D = 1024
KD = D // P
HD = 64
NEG = -1e30
LOW = -3.0e38
EPS = 1e-6

A_HEADS = B_HEADS = 8
KV_HEADS = 2
N_NORMED = 28
NORMED = N_NORMED * HD
AV, VS, VW, KC, VC, BG = NORMED, NORMED + 512, NORMED + 640, NORMED + 768, NORMED + 896, NORMED + 1024
PROJ = BG + 3 * B_HEADS
N_WIN = -(-PROJ // 512)
CMP_LEN, CMP_STRIDE, CMP_HID = 32, 16, 256
N_CMP = (S - CMP_LEN) // CMP_STRIDE + 1
PEER_HEADS, NKEYS, TOPK = 8, 128, 16

DEPTH2 = 2
N_HEADS, N_KV = 16, 4
QKV = (N_HEADS + 2 * N_KV) * HD
X_HEADS, X_HD = 4, 256
D_FF = 2816
NF = D_FF // P
POOL_WINDOWS = (2, 4, 8, 16)
GRID_W = 64

UNIT_COLS = 1024
RAW = 8
NSPLIT = 4
BEGIN = 2
POOL_TOKENS = ((3,), (2, 3))


def weight_units():
    out = [("win", n, q) for n in range(N_WIN) for q in range(4)] + [("mg", c) for c in range(8)]
    out += [("cmp", kv, q) for kv in range(2) for q in range(4)] + [("mg", c) for c in range(8, 16)]
    out += [("up", f) for f in range(KD)] + [("out", k) for k in range(KD)] + [("wq", c) for c in range(16)]
    for i in range(DEPTH2):
        out += [("xk", i, c) for c in range(KD)] + [("xv", i, k) for k in range(KD)]
    out += [("qkv", n, q) for n in range(3) for q in range(4)]
    for i in range(DEPTH2):
        out += [("wo", k) for k in range(KD)] if i == 0 else [("pool", g) for g in range(2)]
        out += [("xq", i, c) for c in range(KD)] + [("xo", i, k) for k in range(KD)]
        out += [("ffu", i, c) for c in range(2 * NF)] + [("ffd", i, k) for k in range(NF)]
    return out


UNITS = weight_units()
UNIT = {name: n for n, name in enumerate(UNITS)}
CHOICE = UNIT[("wq", 0)]
FIRST2 = UNIT[("qkv", 0, 0)]


def bank_groups():
    out = [(("win", n, t), "da"[t]) for n in range(N_WIN) for t in range(T)]
    out += [(("win2", kv), "d") for kv in range(2)]
    out += [(("mg", g), "a") for g in range(4)]
    out += [(("hid", kv), "d") for kv in range(2)] + [(("mg", 4), "a")]
    out += [(("hidT", kv), "d") for kv in range(2)] + [(("mg", 5), "a")]
    out += [(("c2", kv), "d") for kv in range(2)] + [(("mg", 6), "a")]
    out += [(("kcT",), "d"), (("mg", 7), "a")]
    out += [(("qkt", m), "a") for m in range(7)]
    out += [(("scmp", g), "d") for g in range(KV_HEADS)] + [(("ya", p), "d") for p in range(4)]
    out += [(("pct", m), "a") for m in range(4)] + [(("yb", r), "d") for r in range(4)]
    out += [(("up", f), "d") for f in range(KD)]
    for hp in range(4):
        out += [(("pq", g), "a") for g in (2 * hp, 2 * hp + 1)] + [(("sc", m), "a") for m in (2 * hp, 2 * hp + 1)]
    out += [(("xk", i, g), "a") for i in range(DEPTH2) for g in range(4)] + [(("et", m), "a") for m in range(3)]
    out += [(("qkv", n, t), "da"[t]) for n in range(3) for t in range(T)]
    for i in range(DEPTH2):
        if i == 0:
            out += [(("qkt2", m), "a") for m in range(5)] + [(("y2", p), "d") for p in range(8)]
        else:
            out += [(("pm", g), "d") for g in range(4)] + [(("py", t, g), "d") for t in range(T) for g in range(2)]
        out += [(("xq", i, g), "a") for g in range(4)] + [(("yx", i, h), "d") for h in range(X_HEADS)]
        out += [(("ffu", i, f), "d") for f in range(NF)]
    return out


GROUPS = bank_groups()
GROUP = {name: q for q, (name, _) in enumerate(GROUPS)}
RING = 4


def freed(q):
    who = GROUPS[q][1]
    return who, sum(1 for _, w in GROUPS[:q + 1] if w == who)


NORMS = ["norm1", "mem", "norm2", "attn", "x0", "ffn0", "pool", "x1", "ffn1", "final"]
TURNS = ["norm1", "norm2", "mem0", "mem1", "attn", "x0", "ffn0", "x1", "ffn1"]
GAINS_OF = TURNS + ["pool"]
WIDE = ["out", "xv0", "xv1", "peer", "wo", "xo0", "ffd0", "xo1", "ffd1"]
JOBS = {"ab": 0, "self": 24, "x0": 40, "x1": 44}


class Columns:

    def __init__(self, at=0):
        self.at = at

    def take(self, n):
        self.at += n
        return slice(self.at - n, self.at)


SM = Columns()
IDENT, EPSC, GAINS, IOTA = SM.take(P), SM.take(1), SM.take(len(GAINS_OF) * KD), SM.take(NKEYS)
SMALL1 = IOTA.start
CONV, BMERGE, PKEYS = SM.take(DEPTH2 * 2 * NF * 4), SM.take(2 * KD), SM.take(2 * NKEYS)
ROPE1, ROPE2 = SM.take(2 * T * 8), SM.take(2 * T * 2 * 16)
HG1, HG2 = SM.take(5 * HD), SM.take(2 * HD)
L1 = Columns()
MASK, CMASK, CANY, CPOS = L1.take(T * S), L1.take(T * N_CMP), L1.take(T), L1.take(2 * 16)
CB1, CB2, CW2, KCG = L1.take(2 * CMP_HID), L1.take(2 * HD), L1.take(2 * 2 * HD), L1.take(HD)


def block_stack(nc: bass.Bass, x, mem, weights, expert_u, expert_v, small, layer1, band, wide_gains, out):
    with ExitStack() as ctx:
        def sb(name, shape, dt=F32):
            return ctx.enter_context(nc.sbuf_tensor(name, shape, dt))

        def sem(name):
            return ctx.enter_context(nc.semaphore(name))

        smalls = sb("smalls", [P, SM.at])
        stat = sb("stat", [P, 8])
        att = sb("att", [P, 3, 4, T])
        HT = sb("HT", [P, 2, KD, S], F32R)
        wsplit = sb("wsplit", [P, NSPLIT, 2, UNIT_COLS], F32R)
        root_table = sb("root_table", [P, 1])
        act_e = sb("act_e", [P, 2, S])
        wexp = sb("wexp", [P, 2, 2, S], F32R)
        raw0 = sb("raw0", [P, 4, UNIT_COLS])
        PS = [ctx.enter_context(nc.psum_tensor(f"bank{b}", [P, 512], F32)) for b in range(8)]

        ident = smalls[:, IDENT]
        iota = smalls[:, IOTA]
        eps = smalls[:, EPSC]
        gains = smalls[:, GAINS].rearrange("p (n k) -> p n k", k=KD)
        conv = smalls[:, CONV].rearrange("p (i f c) -> p i f c", i=DEPTH2, c=4)
        pkeys = smalls[:, PKEYS].rearrange("p (h n) -> p h n", h=2)
        rope1 = smalls[:, ROPE1].rearrange("p (c t j) -> p c t j", c=2, t=T)
        rope2 = smalls[:, ROPE2].rearrange("p (c t a j) -> p c t a j", c=2, t=T, a=2)

        def tensor(scope, name, *dims, dt=F32):
            return scope.enter_context(nc.sbuf_tensor(name, [P, *dims], dt))

        def area(t, cols, *dims, dt=None):
            v = t[:, cols.take(int(np.prod(dims)))]
            if dt is not None:
                v = v.bitcast(dt)
            names = " ".join(f"d{i}" for i in range(len(dims)))
            sizes = {f"d{i}": d for i, d in enumerate(dims)}
            return v.rearrange(f"p ({names}) -> p {names}", **sizes) if len(dims) > 1 else v

        first = ExitStack()
        raw1a = tensor(first, "raw1a", 4, UNIT_COLS)
        X1 = tensor(first, "X1", T, D)
        layer = ExitStack()
        mgate = tensor(layer, "mgate", KD, 2, S)
        H1 = mgate[:, 0:4, :, :].rearrange("p k b s -> p (k b s)").rearrange("p (t d) -> p t d", t=T)
        projv = tensor(layer, "projv", T, PROJ - NORMED)
        yT = tensor(layer, "yT", 2, 2, 4, S, dt=F32R)
        inner = ExitStack()
        projq = tensor(inner, "projq", T, NORMED)
        c = Columns()
        projq_flat = projq[:, :, :].rearrange("p t n -> p (t n)")
        SMx, Pr, PT = area(projq_flat, c, 2, T, S), area(projq_flat, c, 3, T, S), area(projq_flat, c, 2, T, S)
        blocksT = tensor(inner, "blocksT", 2, 2, 16, 2, N_CMP, dt=F32R)
        attn1 = tensor(inner, "attn1", 20 * S + 2048 + L1.at + 2000)
        c = Columns()
        qkT = area(attn1, c, 20, S)
        sq1 = attn1[:, 0:2 * T * 512].rearrange("p (b t n) -> p b t n", b=2, t=T)
        pcT = area(attn1, c, B_HEADS, S)
        c.at = 20 * S
        rtmp1 = area(attn1, c, 4, T, N_NORMED, 8)
        c.at = 20 * S
        blocks = area(attn1, c, 2, 16, 2, N_CMP)
        c.at = 20 * S + 2048
        consts1 = area(attn1, c, L1.at)
        gate3 = area(attn1, c, T, 3 * B_HEADS)
        hstat1 = area(attn1, c, 3, T, N_NORMED)
        hid = area(attn1, c, 2, CMP_HID)
        hidT = area(attn1, c, 2, 2, 2 * N_CMP)
        kvc = area(attn1, c, 2, KV_HEADS, HD)
        ctmp = area(attn1, c, 2, KV_HEADS, HD)
        cst = area(attn1, c, 3, KV_HEADS)
        kcT = area(attn1, c, 16)
        scmp = area(attn1, c, 16, 16)
        cred = area(attn1, c, 3, 16)
        assert c.at <= 20 * S + 2048 + L1.at + 2000
        inner.close()
        inner = ExitStack()
        merged = tensor(inner, "merged", 2, KD, S, dt=F32R)
        uptmp = tensor(inner, "uptmp", 2, 2, S)
        inner.close()
        layer.close()
        mask = consts1[:, MASK].rearrange("p (t n) -> p t n", t=T)
        cmask = consts1[:, CMASK].rearrange("p (t n) -> p t n", t=T)
        cany = consts1[:, CANY]
        cpos = consts1[:, CPOS].rearrange("p (v k) -> p v k", v=2)
        cb1 = consts1[:, CB1].rearrange("p (v n) -> p v n", v=2)
        cb2 = consts1[:, CB2].rearrange("p (v n) -> p v n", v=2)
        cw2 = consts1[:, CW2].rearrange("p (v k n) -> p v k n", v=2, k=2)
        kcg = consts1[:, KCG]

        choice = ExitStack()
        Hp = tensor(choice, "Hp", T, D)
        memN = tensor(choice, "memN", T, D)
        memT = tensor(choice, "memT", 2, KD, S, dt=F32R)
        kout = tensor(choice, "kout", KD, S)
        pick = tensor(choice, "pick", 16 * S + T * PEER_HEADS * 2 * NKEYS + 6500)
        c = Columns()
        pq = area(pick, c, 16, S)
        sc = area(pick, c, T, PEER_HEADS, 2, NKEYS)
        srep = area(pick, c, 2, NKEYS)
        v16 = area(pick, c, T, PEER_HEADS, 2, TOPK)
        i16 = area(pick, c, T, PEER_HEADS, 2, TOPK, dt=U32)
        i16f = area(pick, c, T, PEER_HEADS, 2, TOPK)
        cand = area(pick, c, 2, TOPK, TOPK)
        tv = area(pick, c, T, PEER_HEADS, TOPK)
        ti = area(pick, c, T, PEER_HEADS * TOPK, dt=U32)
        tab = area(pick, c, 2, T, PEER_HEADS * TOPK, dt=U32)
        tabf = area(pick, c, 2, T, PEER_HEADS * TOPK)
        onehot16 = pq[:, :, :].rearrange("p a t -> p (a t)").rearrange("p (s n j) -> p s n j", s=2, j=TOPK)
        ex = area(pick, c, 2, T, PEER_HEADS * TOPK)
        gsum = area(pick, c, 2, T, PEER_HEADS)
        choice.close()
        first.close()

        run = ExitStack()
        gates = tensor(run, "gates", NKEYS, S)
        run.close()
        eT = raw0[:, 1, 0:3 * S].rearrange("p (k t) -> p k t", k=3)
        few = att[:, :, :, :].rearrange("p a b t -> p (a b t)")[:, 0:20].rearrange("p (b w j) -> p b w j", b=2, w=2)
        hots = raw0[:, 2:4, :].rearrange("p b (w j n) -> p b w j n", w=2, j=4)

        second = ctx.enter_context(ExitStack())
        raw1b = tensor(second, "raw1b", 4, UNIT_COLS)
        X2 = tensor(second, "X2", T, D)
        H2 = tensor(second, "H2", T, D)
        kv_in = tensor(second, "kv_in", 2, 2048)
        kxT = kv_in[:, 0, :].rearrange("p (k s) -> p k s", k=KD)
        vx = kv_in[:, 1, :].rearrange("p (t d) -> p t d", t=T)
        wideg = tensor(second, "wideg", 2, D)
        bandm = tensor(second, "bandm", 8, S)
        ptmp = tensor(second, "ptmp", 2, 512)
        inner = ExitStack()
        oT = tensor(inner, "oT", 2, KD, S, dt=F32R)
        qkv = tensor(inner, "qkv", T, QKV)
        qkv_flat = qkv[:, :, :].rearrange("p t n -> p (t n)")
        qxT = qkv_flat[:, 0:KD * S].rearrange("p (k t) -> p k t", k=KD)
        qkT2 = tensor(inner, "qkT2", 12, S)
        rtmp2 = tensor(inner, "rtmp2", T, 4, 8, 2, 16)
        probs2 = tensor(inner, "probs2", 2560)
        c = Columns()
        Pr2, PT2 = area(probs2, c, 3, T, S), area(probs2, c, 2, T, S)
        sq2 = probs2[:, 0:2 * T * 512].rearrange("p (b t n) -> p b t n", b=2, t=T)
        hstat2 = tensor(inner, "hstat2", 3, T, 20)
        inner.close()
        inner = ExitStack()
        ff = tensor(inner, "ff", 2, NF, S, dt=F32R)
        cv = tensor(inner, "cv", 2, 2, S)
        inner.close()

        def head_block(n, end, src, sq, st):
            width = min(512, end - 512 * n)
            heads = slice(8 * n, 8 * n + width // HD)
            return src[:, :, 512 * n:512 * n + width], sq[:, n % 2, :, 0:width], [st[:, w, :, heads] for w in range(3)]

        def head_block1(n):
            return head_block(n, NORMED, projq, sq1, hstat1)

        def head_block2(n):
            return head_block(n, (N_HEADS + N_KV) * HD, qkv, sq2, hstat2)

        park = nc.dram_tensor("parked", (5, P, 2048), F32).ap()

        def sb_raw(u):
            later = raw1a if u < FIRST2 else raw1b
            return raw0[:, u % RAW, :] if u % RAW < 4 else later[:, u % RAW - 4, :]

        def f32(ap):
            return ap.bitcast(F32)

        in_x, in_x2 = [sem(f"in_x{t}") for t in range(T)], sem("in_x_again")
        in_small, in_more, in_layer1 = sem("in_small"), sem("in_more"), sem("in_layer1")
        in_mem, in_band, in_wide, in_kv = sem("in_mem"), sem("in_band"), sem("in_wide"), sem("in_kv")
        w_landed = [sem(f"w_landed{s}") for s in range(RAW)]
        w_hi, w_freed = sem("w_hi_made"), sem("w_freed")
        w_lo_even, w_lo_odd, w_lo_choice = sem("w_lo_by_vector"), sem("w_lo_by_pool"), sem("w_lo_even_by_pool")
        u_landed = [sem(f"u_landed{s}") for s in range(2)]
        v_landed = [sem(f"v_landed{s}") for s in range(2)]
        u_hi, u_lo, v_hi, v_lo = sem("u_hi_made"), sem("u_lo_made"), sem("v_hi_made"), sem("v_lo_made")
        x_parked, k_parked, v_parked = sem("x_parked"), sem("k_parked"), [sem(f"v_parked{t}") for t in range(T)]
        bank_full = sem("bank_full")
        bank_freed = {"a": sem("bank_freed_by_scalar"), "d": sem("bank_freed_by_vector")}
        norm_sq, norm_root, norm_h, norm_t = sem("norm_sq"), sem("norm_root"), sem("norm_h"), sem("norm_t")
        norm_a, norm_d = sem("norm_hi_by_scalar"), sem("norm_lo_by_vector")
        wide_done, wide_out = sem("wide_done"), sem("wide_out")
        head_sq, head_sum, head_root, head_done = sem("head_sq"), sem("head_sum"), sem("head_root"), sem("head_done")
        pads = sem("key_pads_zeroed")
        gate3_done, blocks_done, merged_done = sem("gate3_done"), sem("blocks_done"), sem("merged_done")
        cmp_gelu, cmp_sum, cmp_root = sem("cmp_gelu"), sem("cmp_sum"), sem("cmp_root")
        cmp_key, cmp_less, cmp_exp, cmp_prob = sem("cmp_key"), sem("cmp_less"), sem("cmp_exp"), sem("cmp_prob")
        s_full, s_max, s_exp, s_prob = sem("scores_full"), sem("scores_max"), sem("scores_exp"), sem("scores_prob")
        t_full, t_out, y_full = sem("probsT_full"), sem("probsT_out"), sem("y_full")
        gate_less, gate_exp, ex_done = sem("gate_less"), sem("gate_exp"), sem("experts_done")
        few_made, few_seen = sem("few_made"), sem("few_seen")
        hot_by_d, hot_by_p = sem("hot_by_vector"), sem("hot_by_pool")
        hot_full, hot_out = sem("hot_full"), sem("hot_out")
        a_full, a_gelu, a_mul, a_hi = sem("a_full"), sem("a_gelu"), sem("a_times_gates"), sem("a_hi_made")
        a_w, a_v = sem("a_weighted"), sem("a_times_v")
        conv_a, conv_d, conv_s, conv_m = sem("conv_mid"), sem("conv_sum"), sem("conv_silu"), sem("conv_mul")
        pool_hi, pool_lo = sem("pool_hi"), sem("pool_lo")
        pool_done, final_h = sem("pool_done"), sem("final_h")
        chain = sem("vector_chain")
        stored = [sem(f"stored{n}") for n in range(2 * T)]

        def bank(name):
            return PS[4 + GROUP[name] % RING]

        def wait_full(eng, name):
            eng.wait_ge(bank_full, sum(1 for n, _ in GROUPS[:GROUP[name] + 1] if n[0] not in ("ya", "yb", "y2", "yx")))

        def wait_freed(eng, name):
            who, count = freed(GROUP[name])
            eng.wait_ge(bank_freed[who], count)

        def wait_wide(eng, name):
            eng.wait_ge(wide_out, 4 * (WIDE.index(name) + 1))

        def wait_wide_done(eng, name, t):
            eng.wait_ge(wide_done, T * WIDE.index(name) + t + 1)

        def lo_made(u):
            if u % 2:
                return w_lo_odd, u // 2 + 1
            if CHOICE <= u < FIRST2:
                return w_lo_choice, (u - CHOICE) // 2 + 1
            return w_lo_even, u // 2 + 1 - (0 if u < CHOICE else (FIRST2 - CHOICE) // 2)

        def wait_first_units_used(eng):
            for u in (CHOICE - 2, FIRST2 - 2, FIRST2 - 1):
                eng.wait_ge(*lo_made(u))

        def units_to(name):
            kind, at = name[0], name[1:]
            last = {
                "win": lambda: ("win", at[0], 3), "qkv": lambda: ("qkv", at[0], 3), "mg": lambda: ("mg", 2 * at[0] + 1),
                "hid": lambda: ("cmp", at[0], 3), "up": lambda: ("up", at[0]), "pq": lambda: ("wq", 2 * at[0] + 1),
                "xk": lambda: ("xk", at[0], 2 * at[1] + 1), "xq": lambda: ("xq", at[0], 2 * at[1] + 1),
                "ffu": lambda: ("ffu", at[0], 2 * at[1] + 1), "py": lambda: ("pool", 0),
                "out": lambda: ("out", KD - 1), "wo": lambda: ("wo", KD - 1), "xv": lambda: ("xv", at[0], KD - 1),
                "xo": lambda: ("xo", at[0], KD - 1), "ffd": lambda: ("ffd", at[0], NF - 1)}
            return UNIT[last[kind]()] + 1 if kind in last else 0

        def units_of_turn(name):
            first = {"norm1": ("win", 0, 0), "norm2": ("wq", 0), "attn": ("qkv", 0, 0), "x": ("xq",), "ffn": ("ffu",)}
            key = first.get(name) or first.get(name[:-1])
            return UNIT[key if name in first else key + (int(name[-1]), 0)] + 3 if key else 0

        def split_word(name):
            return (name[:-1], int(name[-1])) if name[-1].isdigit() else (name,)

        def tok(t):
            return slice(t * P, (t + 1) * P)

        def heads_v(at, h):
            return slice(at - NORMED + h * HD, at - NORMED + (h + 1) * HD)

        def a_jobs():
            for h in range(A_HEADS):
                yield dict(
                    q=lambda t, h=h: [qkT[:, h // 2, tok(t)]], k=[qkT[:, 8 + h, :]], gate=None,
                    v=lambda kt, h=h: [projv[:, kt, heads_v(AV, h)]], rows=slice(HD * (h % 2), HD * (h % 2) + HD), cmp=None,
                    y=("ya", h // 2), first=True, last=h % 2 == 1, dest=[yT[:, :, 0, h // 2, :]])

        def b_jobs():
            for r in range(4):
                for g in range(KV_HEADS):
                    h = 4 * g + r
                    for j, (slot, vat) in enumerate(((16, VS), (18, VW))):
                        yield dict(
                            q=lambda t, r=r: [qkT[:, 4 + r, tok(t)]], k=[qkT[:, slot + g, :]],
                            gate=lambda t, h=h, j=j: gate3[:, t, 3 * h + 1 + j:3 * h + 2 + j],
                            v=lambda kt, g=g, vat=vat: [projv[:, kt, heads_v(vat, g)]], rows=slice(HD * g, HD * g + HD),
                            cmp=(g, h) if j == 0 else None, y=("yb", r), first=j == 0, last=(g, j) == (1, 1),
                            dest=[yT[:, :, 1, r, :]])

        def self_jobs():
            for p in range(8):
                for i in range(2):
                    kv = 2 * (p // 4) + i
                    vat = (N_HEADS + N_KV + kv) * HD
                    yield dict(
                        q=lambda t, p=p: [qkT2[:, p, tok(t)]], k=[qkT2[:, 8 + kv, :]], gate=None,
                        v=lambda kt, vat=vat: [qkv[:, kt, vat:vat + HD]], rows=slice(HD * i, HD * i + HD), cmp=None,
                        y=("y2", p), first=True, last=i == 1, dest=[oT[:, :, p, :]])

        def cross_jobs(i):
            for h in range(X_HEADS):
                yield dict(
                    q=lambda t, h=h: [qxT[:, 2 * h + d, tok(t)] for d in range(2)],
                    k=[kxT[:, 2 * h + d, :] for d in range(2)], gate=None,
                    v=lambda kt, h=h: [vx[:, kt, (2 * h + d) * P:(2 * h + d + 1) * P] for d in range(2)],
                    rows=slice(0, P), cmp=None, y=("yx", i, h), first=True, last=True,
                    dest=[oT[:, :, 2 * h, :], oT[:, :, 2 * h + 1, :]])

        def seen(use, t):
            return (t + 1) * P if use == "ab" else S

        def turned_blocks(use):
            if use == "ab":
                return [(0, 0, 0), (0, 1, P), (1, 1, 2 * P)]
            return [(kt, t, kt * S + t * P) for kt in range(T) for t in range(T)]

        def value_products(use, job):
            if job["y"][0] == "yb":
                return [(1, 2 * P, P, P, False, False), (0, 0, S, 0, False, True)]
            if use == "ab":
                return [(kt, at, P, t * P, kt == 0, kt == t) for kt, t, at in turned_blocks(use)]
            return [(kt, kt * S, S, 0, kt == 0, kt == T - 1) for kt in range(T)]

        def flat(ap):
            return ap.rearrange("p a b -> p (a b)")

        USES = {
            "ab": (list(a_jobs()) + list(b_jobs()), SMx, Pr, PT),
            "self": (list(self_jobs()), None, Pr2, PT2), "x0": (list(cross_jobs(0)), None, Pr2, PT2),
            "x1": (list(cross_jobs(1)), None, Pr2, PT2),
        }

        def win_parts(n, t):
            end = min(512 * (n + 1), PROJ)
            parts = []
            if 512 * n < NORMED:
                m = min(end, NORMED)
                parts.append((projq[:, t, 512 * n:m], slice(0, m - 512 * n)))
            if end > NORMED:
                m = max(512 * n, NORMED)
                parts.append((projv[:, t, m - NORMED:end - NORMED], slice(m - 512 * n, end - 512 * n)))
            return parts

        tokens_first = "b (t p) d -> p (b t) d"
        block = ctx.enter_context(nc.Block())

        @block.sync
        def _(sp):
            def load(n, u):
                sp.dma_start(sb_raw(u), weights[n]).then_inc(w_landed[u % RAW], 16)

            def load_turns(n0, n1):
                with sp.Fori(n0 // RAW, n1 // RAW) as i:
                    for s in range(RAW):
                        made, count = lo_made(n0 + s - RAW)
                        sp.wait_ge(made, i * (RAW // 2) + (count - n0 // 2))
                        load(i * RAW + s, n0 + s)

            for t in range(T):
                sp.dma_start(X1[:, t, :], x[0, tok(t), :]).then_inc(in_x[t], 16)
            for u in range(4):
                load(u, u)
            sp.dma_start(smalls[:, SMALL1:], small[:, SMALL1:]).then_inc(in_more, 16)
            sp.dma_start(consts1, layer1).then_inc(in_layer1, 16)
            for u in range(4, RAW):
                load(u, u)
            load_turns(RAW, CHOICE + RAW)
            load_turns(CHOICE + RAW, FIRST2 - RAW)
            for i in range(DEPTH2):
                for t in range(T):
                    sp.wait_ge(wide_out, 4 * WIDE.index(f"xv{i}") + 2 * (t + 1))
                    sp.dma_start(park[2 + 2 * i][:, t * D:(t + 1) * D], Hp[:, t, :]).then_inc(v_parked[t], 16)
                if i == 0:
                    load_turns(FIRST2 - RAW, FIRST2)
            wait_first_units_used(sp)
            sp.dma_start(raw0[:, 0, :], expert_u[0]).then_inc(u_landed[0], 16)
            sp.wait_ge(hot_full, BEGIN + S // 4)
            sp.dma_start(raw0[:, 2, :], expert_v[0]).then_inc(v_landed[0], 16)
            sp.dma_start(raw0[:, 1, :], expert_u[1]).then_inc(u_landed[1], 16)
            sp.dma_start(raw0[:, 3, :], expert_v[1]).then_inc(v_landed[1], 16)
            with sp.Fori(1, NKEYS // 2) as i:
                for s in range(2):
                    sp.wait_ge(u_lo, i * 2 + (s - 1))
                    sp.dma_start(raw0[:, s, :], expert_u[i * 2 + s]).then_inc(u_landed[s], 16)
                    sp.wait_ge(v_lo, i * 2 + (s - 1))
                    sp.dma_start(raw0[:, 2 + s, :], expert_v[i * 2 + s]).then_inc(v_landed[s], 16)
            sp.wait_ge(a_mul, NKEYS)
            sp.wait_ge(x_parked, 16)
            sp.dma_start(X2[:, :, :], park[0].rearrange("p (t d) -> p t d", t=T)).then_inc(in_x2, 16)
            sp.wait_ge(u_lo, NKEYS)
            sp.wait_ge(v_lo, NKEYS)
            for u in range(FIRST2, FIRST2 + RAW):
                load(u, u)

            def load_units(u0, u1):
                for u in range(u0, u1):
                    sp.wait_ge(*lo_made(u - RAW))
                    load(u, u)

            n = FIRST2 + RAW
            load_units(n, n + RAW)
            sp.wait_ge(k_parked, 32)
            for t in range(T):
                sp.wait_ge(v_parked[t], 32)
            sp.dma_start(kv_in[:, :, :], park[1:3].rearrange("w p d -> p w d")).then_inc(in_kv, 16)
            load_units(n + RAW, n + 2 * RAW)
            sp.dma_start(bandm[:, :, :], band).then_inc(in_band, 16)
            load_units(n + 2 * RAW, n + 3 * RAW)
            sp.dma_start(wideg[:, :, :], wide_gains).then_inc(in_wide, 16)
            whole = len(UNITS) // RAW * RAW
            load_turns(n + 3 * RAW, whole)
            load_units(whole, len(UNITS))
            for t in range(T):
                for h in range(2):
                    sp.wait_ge(final_h, 2 * t + h + 1)
                    cols = slice(h * 512, (h + 1) * 512)
                    sp.dma_start(out[0, tok(t), cols], H2[:, t, cols]).then_inc(stored[2 * t + h], 16)
            for done in stored:
                sp.wait_ge(done, 16)

        @block.tensor
        def _(pe):
            state = {"frees": 0}

            def mm(out, lhsT, rhs, start, stop, **kw):
                ins = pe.matmul(out, lhsT, rhs, start=start, stop=stop, **kw)
                if state["frees"]:
                    ins.then_inc(w_freed, 1)
                    state["frees"] = 0
                return ins

            def mm3(out, left, right, start, stop, **kw):
                for n, (a, b) in enumerate(((0, 0), (0, 1), (1, 0))):
                    ins = mm(out, left(a), right(b), start and n == 0, stop and n == 2, **kw)
                return ins

            def weights_of(*name):
                u = UNIT[name]
                pe.wait_ge(*lo_made(u))
                state["frees"] = u not in (0, FIRST2)
                return lambda part: wsplit[:, u % NSPLIT, part, :]

            def tiles_of(w, **sizes):
                return lambda part: w(part).rearrange("p (k n) -> p k n", **sizes)

            def open_bank(name):
                q = GROUP[name]
                if q >= RING:
                    wait_freed(pe, GROUPS[q - RING][0])
                return PS[4 + q % RING]

            def turn(name, H):
                for t in range(T):
                    pe.wait_ge(norm_h, T * NORMS.index("mem" if name[:3] == "mem" else name) + t + 1)
                    for b in range(4):
                        for k in range(2):
                            c = 2 * b + k
                            ins = pe.transpose(PS[b][:, (k * T + t) * P:(k * T + t + 1) * P],
                                               H[:, t, c * P:(c + 1) * P], ident)
                        if t == T - 1:
                            ins.then_inc(norm_t, 1)

            def wait_turned(name, k):
                if name is not None:
                    pe.wait_ge(norm_d, KD * TURNS.index(name) + k + 1)

            def feature_tile(out, unit, src, fresh=None):
                w = tiles_of(weights_of(*unit), k=KD)
                for k in range(KD):
                    wait_turned(fresh, k)
                    ins = mm3(out, lambda a: w(a)[:, k, :], lambda b: src[:, b, k, :], k == 0, k == KD - 1)
                return ins

            def feature_groups(kind, units, groups, src, fresh=None):
                for g in groups:
                    b = open_bank(kind + (g,))
                    for c in range(2):
                        ins = feature_tile(b[:, c * S:(c + 1) * S], units + (2 * g + c,), src, fresh if g == c == 0 else None)
                    ins.then_inc(bank_full, 1)

            def token_major(kind, blocks, src, fresh, last_width=512):
                for n in range(blocks):
                    banks = [open_bank((kind, n, t)) for t in range(T)]
                    width = last_width if n == blocks - 1 else 512
                    for q in range(4):
                        w = tiles_of(weights_of(kind, n, q), k=2)
                        wait_turned(fresh if n == 0 else None, 2 * q + 1)
                        for t in range(T):
                            for k in range(2):
                                ins = mm3(banks[t][:, 0:width], lambda a: src[:, a, 2 * q + k, tok(t)],
                                          lambda b: w(b)[:, k, 0:width], q == k == 0, q == 3 and k == 1)
                            if q == 3:
                                ins.then_inc(bank_full, 1)

            def wide(name, unit, src, kt, ready):
                if WIDE.index(name):
                    wait_wide(pe, WIDE[WIDE.index(name) - 1])
                def products(k, w, t):
                    for h in range(2):
                        ins = mm3(PS[2 * t + h][:, :], lambda a: src[:, a, k, tok(t)],
                                  lambda b: w(b)[:, h * 512:(h + 1) * 512], k == 0, k == kt - 1)
                    return ins

                for k in range(kt - 2):
                    ready(k)
                    w = weights_of(*unit, k)
                    for t in range(T):
                        products(k, w, t)
                ready(kt - 2)
                w = weights_of(*unit, kt - 2)
                products(kt - 2, w, 0)
                ready(kt - 1)
                last = weights_of(*unit, kt - 1)
                frees, state["frees"] = state["frees"], 0
                products(kt - 1, last, 0).then_inc(wide_done, 1)
                products(kt - 2, w, 1)
                state["frees"] = frees
                products(kt - 1, last, 1).then_inc(wide_done, 1)

            def turn_compressed():
                pe.wait_ge(cmp_prob, 1)
                for m in range(4):
                    b = open_bank(("pct", m))
                    for s in range(2):
                        for t in range(T):
                            ins = pe.transpose(b[0:N_CMP, s * S + t * P:s * S + (t + 1) * P],
                                               scmp[:, (2 * m + s) * T + t, 0:N_CMP], ident)
                    ins.then_inc(bank_full, 1)

            def attention(use):
                jobs, _, Pb, Tb = USES[use]
                j0, n = JOBS[use], len(jobs)
                for step in range(n + 3):
                    if step < n:
                        job, j = jobs[step], j0 + step
                        if step >= 2:
                            pe.wait_ge(s_exp, j - 1)
                        for t in range(T):
                            qs = job["q"](t)
                            for d, q in enumerate(qs):
                                w = seen(use, t)
                                ins = mm(PS[j % 2][:, t * S:t * S + w], q, job["k"][d][:, 0:w], d == 0, d == len(qs) - 1)
                        ins.then_inc(s_full, 1)
                    if 2 <= step <= n + 1:
                        j = j0 + step - 2
                        pe.wait_ge(s_prob, j + 1)
                        if step >= 4:
                            pe.wait_ge(t_out, j - 1)
                        for kt, t, at in turned_blocks(use):
                            ins = pe.transpose(PS[2 + j % 2][:, at:at + P], Pb[:, j % 3, t, kt * P:(kt + 1) * P], ident)
                        ins.then_inc(t_full, 1)
                    if step >= 3:
                        job, j = jobs[step - 3], j0 + step - 3
                        if (use, step - 3) == ("ab", A_HEADS):
                            turn_compressed()
                        if step == 3 or jobs[step - 4]["y"] != job["y"]:
                            b = open_bank(job["y"])
                        if job["cmp"] is not None:
                            g, h = job["cmp"]
                            wait_freed(pe, ("pct", h // 2))
                            mm(b[job["rows"], 0:S], kvc[0:N_CMP, 1, g, :], pcT[0:N_CMP, h, :], True, False)
                        pe.wait_ge(t_out, j + 1)
                        first = job["first"] and job["cmp"] is None
                        last = job["y"][0] != "yb" or job["cmp"] is None
                        for d in range(len(job["dest"])):
                            for kt, at, width, to, start, stop in value_products(use, job):
                                ins = mm(b[job["rows"], d * S + to:d * S + to + width], job["v"](kt)[d],
                                         flat(Tb[:, j % 2, :, :])[:, at:at + width], first and start, last and stop)
                        ins.then_inc(y_full, 1)

            pe.wait_ge(in_small, 16)
            turn("norm1", H1)
            token_major("win", N_WIN, HT, "norm1", PROJ - 512 * (N_WIN - 1))
            for kv, at in enumerate((KC, VC)):
                b = open_bank(("win2", kv))
                wait_freed(pe, ("win", N_WIN - 1, 0))
                wait_freed(pe, ("win", N_WIN - 1, 1))
                for g in range(KV_HEADS):
                    for par in range(2):
                        for t in range(T):
                            ins = mm(b[HD * par:HD * par + HD, g * P + t * HD:g * P + (t + 1) * HD],
                                     projv[:, t, heads_v(at, g)], ident[:, par::2], True, True)
                ins.then_inc(bank_full, 1)

            def merge_gates(gs):
                for g in gs:
                    b = open_bank(("mg", g))
                    for c in range(2):
                        ins = feature_tile(b[:, c * S:(c + 1) * S], ("mg", 2 * g + c), HT)
                    ins.then_inc(bank_full, 1)

            merge_gates(range(4))
            pe.wait_ge(blocks_done, 2)
            for kv in range(2):
                b = open_bank(("hid", kv))
                for q in range(4):
                    w = tiles_of(weights_of("cmp", kv, q), k=4)
                    for kk in range(4):
                        k = 4 * q + kk
                        ins = mm3(b[0:2 * N_CMP, 0:CMP_HID], lambda a: blocksT[:, a, kv, k, :, :].rearrange("p g n -> p (g n)"),
                                  lambda c: w(c)[:, kk, :], k == 0, k == 15)
                ins.then_inc(bank_full, 1)
            merge_gates([4])
            pe.wait_ge(in_layer1, 16)
            for kv in range(2):
                b = open_bank(("hidT", kv))
                pe.wait_ge(cmp_gelu, kv + 1)
                for k in range(2):
                    ins = pe.transpose(b[:, k * 32:k * 32 + 2 * N_CMP], hid[0:2 * N_CMP, kv, k * P:(k + 1) * P],
                                       ident[0:2 * N_CMP, 0:2 * N_CMP])
                ins.then_inc(bank_full, 1)
            merge_gates([5])
            for kv in range(2):
                b = open_bank(("c2", kv))
                wait_freed(pe, ("hidT", kv))
                for g in range(KV_HEADS):
                    for k in range(2):
                        ins = mm(b[0:N_CMP, g * HD:(g + 1) * HD], hidT[:, kv, k, g * N_CMP:(g + 1) * N_CMP],
                                 cw2[:, kv, k, :], k == 0, k == 1)
                ins.then_inc(bank_full, 1)
            merge_gates([6])
            b = open_bank(("kcT",))
            pe.wait_ge(cmp_key, 1)
            for g in range(KV_HEADS):
                ins = mm(b[HD * g:HD * g + HD, 0:N_CMP], kvc[0:N_CMP, 0, g, :], ident[0:N_CMP, 0:N_CMP], True, True)
            ins.then_inc(bank_full, 1)
            merge_gates([7])
            pe.wait_ge(head_done, 4)
            for m in range(7):
                b = open_bank(("qkt", m))
                for s in range(2):
                    for t in range(T):
                        ins = pe.transpose(b[:, s * S + t * P:s * S + (t + 1) * P],
                                           projq[:, t, (2 * m + s) * P:(2 * m + s + 1) * P], ident)
                ins.then_inc(bank_full, 1)
            wait_freed(pe, ("qkt", 3))
            wait_freed(pe, ("kcT",))
            for h in range(B_HEADS):
                g, r = h // 4, h % 4
                if r == 0:
                    b = open_bank(("scmp", g))
                for t in range(T):
                    ins = mm(b[:, (2 * r + t) * 16:(2 * r + t) * 16 + N_CMP], qkT[HD * g:HD * g + HD, 4 + r, tok(t)],
                             kcT[HD * g:HD * g + HD, 0:N_CMP], True, True)
                if r == 3:
                    ins.then_inc(bank_full, 1)
            wait_freed(pe, ("qkt", 6))
            pe.wait_ge(pads, 1)
            attention("ab")
            wait_freed(pe, ("yb", 3))
            for f in range(KD):
                b = open_bank(("up", f))
                w = tiles_of(weights_of("up", f), k=8)
                for br in range(2):
                    for k in range(4):
                        ins = mm3(b[:, br * S:(br + 1) * S], lambda a: w(a)[:, 4 * br + k, :],
                                  lambda c: yT[:, c, br, k, :], k == 0, k == 3)
                ins.then_inc(bank_full, 1)
            wide("out", ("out",), merged, KD, lambda k: pe.wait_ge(merged_done, k + 1))

            turn("norm2", Hp)
            pe.wait_ge(in_more, 16)
            for m in range(8):
                hp, t = m // 2, m % 2
                if t == 0:
                    feature_groups(("pq",), ("wq",), range(2 * hp, 2 * hp + 2), HT, "norm2")
                b = open_bank(("sc", m))
                wait_freed(pe, ("pq", 2 * hp + 1))
                for s in range(4):
                    ins = mm(b[:, s * P:(s + 1) * P], pq[:, 4 * hp + s, tok(t)], pkeys[:, s % 2, :], True, True)
                ins.then_inc(bank_full, 1)
            for i in range(DEPTH2):
                if i:
                    wait_wide(pe, "xv0")
                turn(f"mem{i}", memN)
                feature_groups(("xk", i), ("xk", i), range(4), memT, f"mem{i}")
                wide(f"xv{i}", ("xv", i), memT, KD, lambda k: None)
            pe.wait_ge(ex_done, 1)
            for m in range(3):
                b = open_bank(("et", m))
                for t in range(T):
                    src = ex[:, m, t, :] if m < 2 else tv[:, t, :, :].rearrange("p h k -> p (h k)")
                    ins = pe.transpose(b[:, tok(t)], src, ident)
                    if m == t == 0:
                        ins.then_inc(w_freed, 1)
                ins.then_inc(bank_full, 1)
            wait_wide(pe, "xv1")
            pe.sem_inc(hot_full, BEGIN)
            with pe.Fori(0, S // 8) as i:
                for half in range(2):
                    pe.wait_ge(hot_by_d, i * 2 + (half + 1))
                    pe.wait_ge(hot_out, i * 2 + (half - 1 + BEGIN))
                    for j in range(4):
                        if j == POOL_TOKENS[half][0]:
                            pe.wait_ge(hot_by_p, i * 2 + (half + 1))
                        ins = pe.matmul(PS[half][:, j * P:(j + 1) * P], hots[:, half, 0, j, :], hots[:, half, 1, j, :],
                                        start=True, stop=True)
                    ins.then_inc(hot_full, 1)
            pe.wait_ge(hot_out, BEGIN + S // 4)

            def times_u(e, s):
                pe.wait_ge(u_lo, e + 1)
                if not isinstance(e, int) or e >= 2:
                    pe.wait_ge(a_gelu, e - 1)
                w = tiles_of(lambda part: wsplit[:, s, part, :], k=KD)
                for k in range(KD):
                    ins = mm3(PS[s][:, 0:S], lambda a: w(a)[:, k, :], lambda b: HT[:, b, k, :], k == 0, k == KD - 1)
                ins.then_inc(a_full, 1)

            def times_v(e, s, stop=False):
                pe.wait_ge(v_lo, e + 1)
                pe.wait_ge(a_w, e + (1 + BEGIN))
                for t in range(T):
                    if stop and t:
                        ins.then_inc(wide_done, 1)
                    for h in range(2):
                        ins = mm3(PS[4 + 2 * t + h][:, :], lambda a: wexp[:, s, a, tok(t)],
                                  lambda b: wsplit[:, 2 + s, b, h * 512:(h + 1) * 512], False, stop, skip_group_check=True)
                ins.then_inc(wide_done if stop else a_v, 1)

            pe.wait_ge(a_w, BEGIN)
            for b in range(4):
                ins = pe.matmul(PS[4 + b][:, :], act_e[:, 0, 0:P], smalls[:, 0:512], start=True, stop=False,
                                skip_group_check=True)
            ins.then_inc(a_v, BEGIN)
            times_u(0, 0)
            times_u(1, 1)
            times_v(0, 0)
            with pe.Fori(1, NKEYS // 2) as i:
                for s in range(2):
                    times_u(i * 2 + s, s)
                    times_v(i * 2 + (s - 1), 1 - s)
            times_v(NKEYS - 1, 1, stop=True)

            wait_wide(pe, "peer")
            turn("attn", H2)
            token_major("qkv", 3, HT, "attn")
            for m in range(5):
                b = open_bank(("qkt2", m))
                pe.wait_ge(head_done, 6 if m < 4 else 7)
                for s in range(2):
                    for t in range(T):
                        ins = pe.transpose(b[:, s * S + t * P:s * S + (t + 1) * P],
                                           qkv[:, t, (2 * m + s) * P:(2 * m + s + 1) * P], ident)
                ins.then_inc(bank_full, 1)
            wait_freed(pe, ("qkt2", 4))
            pe.wait_ge(pads, 2)
            attention("self")
            wide("wo", ("wo",), oT, KD, lambda k: wait_freed(pe, ("y2", k)))
            for i in range(DEPTH2):
                if i:
                    pe.wait_ge(norm_h, 2 * (NORMS.index("pool") + 1))
                    pe.wait_ge(in_band, 16)
                    for g in range(4):
                        b = open_bank(("pm", g))
                        for c in range(2):
                            for s in range(T):
                                at = (2 * g + c) * P
                                ins = mm(b[:, c * S:(c + 1) * S], H2[:, s, at:at + P], bandm[:, 2 * g + s, :], s == 0, s == 1)
                        ins.then_inc(bank_full, 1)
                    def maps(t, g2, w):
                        b = open_bank(("py", t, g2))
                        for u in range(2):
                            for c in range(2):
                                ct = 4 * g2 + 2 * u + c
                                at = (2 * u + c) * S
                                ins = mm3(b[:, u * S:(u + 1) * S], lambda a: oT[:, a, ct, tok(t)],
                                          lambda v: w(v)[:, at:at + S], c == 0, c == 1)
                        ins.then_inc(bank_full, 1)

                    w0 = weights_of("pool", 0)
                    pe.wait_ge(pool_lo, 4)
                    maps(0, 0, w0)
                    w1 = weights_of("pool", 1)
                    pe.wait_ge(pool_lo, 8)
                    frees, state["frees"] = state["frees"], 0
                    maps(0, 1, w1)
                    maps(1, 0, w0)
                    state["frees"] = frees
                    maps(1, 1, w1)
                turn(f"x{i}", H2)
                feature_groups(("xq", i), ("xq", i), range(4), HT, f"x{i}")
                wait_freed(pe, ("xq", i, 3))
                pe.wait_ge(in_kv, 16 * (i + 1))
                attention(f"x{i}")
                wide(f"xo{i}", ("xo", i), oT, KD, lambda k: wait_freed(pe, ("yx", i, k // 2)))
                turn(f"ffn{i}", H2)
                feature_groups(("ffu", i), ("ffu", i), range(NF), HT, f"ffn{i}")
                wide(f"ffd{i}", ("ffd", i), ff, NF, lambda k: pe.wait_ge(conv_m, NF * i + k + 1))

        @block.gpsimd
        def _(pool):
            def lo_turn(i, n0, slots):
                for s in slots:
                    pool.wait_ge(w_hi, i * RAW + (s + 1))
                    pool.tensor_tensor(wsplit[:, s % NSPLIT, 1, :], sb_raw(n0 + s), f32(wsplit[:, s % NSPLIT, 0, :]),
                                       ALU.subtract).then_inc(lo_made(n0 + s)[0], 1)

            odd = range(1, RAW, 2)
            with pool.Fori(0, CHOICE // RAW) as i:
                lo_turn(i, 0, odd)

            with pool.Fori(CHOICE // RAW, FIRST2 // RAW) as i:
                lo_turn(i, CHOICE, range(RAW))
            wait_first_units_used(pool)
            wait_freed(pool, ("et", 2))
            with pool.Fori(0, S // 16) as i:
                for four in range(4):
                    pool.wait_ge(hot_full, i * 4 + (four - 1 + BEGIN))
                    pool.wait_ge(few_made, i * 2 + (four // 2 + 1))
                    pool.sem_inc(few_seen, 1)
                    for j in POOL_TOKENS[four % 2]:
                        n = 4 * (four % 2) + j - 3
                        ins = pool.tensor_scalar(hots[:, four % 2, 1, j, :], iota, few[:, four // 2, 0, n:n + 1],
                                                 few[:, four // 2, 1, n:n + 1], ALU.is_equal, ALU.mult)
                    ins.then_inc(hot_by_p, 1)

            with pool.Fori(0, NKEYS // 2) as i:
                for s in range(2):
                    pool.wait_ge(u_hi, i * 2 + (s + 1))
                    pool.tensor_tensor(wsplit[:, s, 1, :], raw0[:, s, :], f32(wsplit[:, s, 0, :]), ALU.subtract)\
                        .then_inc(u_lo, 1)
            turns = len(UNITS) // RAW
            with pool.Fori(FIRST2 // RAW, turns) as i:
                lo_turn(i, FIRST2, odd)
            lo_turn(turns, FIRST2, range(1, len(UNITS) % RAW, 2))

        @block.scalar
        def _(act):
            split, limit = [0], [FIRST2]

            def split_to(u1):
                for u in range(split[0], min(u1, limit[0])):
                    act.wait_ge(w_landed[u % RAW], 16 * (u // RAW + 1))
                    if u >= NSPLIT:
                        act.wait_ge(w_freed, u - NSPLIT + 1)
                    act.activation(wsplit[:, u % NSPLIT, 0, :], sb_raw(u), ACT.Copy).then_inc(w_hi, 1)
                    split[0] = u + 1

            def full(name):
                split_to(units_to(name) + 3)
                wait_full(act, name)

            def norm_sums(name, src, H, ready):
                i = NORMS.index(name)
                act.activation(root_table[:, :], eps, ACT.Sqrt)
                before = [TURNS.index(n) + 1 for n in NORMS[:i] if n in TURNS]
                if before:
                    act.wait_ge(norm_t, 4 * before[-1])
                for t in range(T):
                    ready(t)
                    act.activation(H[:, t, :], src[:, t, :], ACT.Square, accum_out=stat[:, t:t + 1]).then_inc(norm_sq, 1)
                    act.wait_ge(norm_sq, T * i + t + 1)
                    act.activation(stat[:, 2 + t:3 + t], stat[:, t:t + 1], ACT.Sqrt, bias=eps, scale=1.0 / D)\
                       .then_inc(norm_root, 1)

            def after_wide(name):
                return lambda t: act.wait_ge(wide_out, 4 * WIDE.index(name) + 2 * (t + 1))

            def norm_out(name, dst):
                i, n = TURNS.index(name), GAINS_OF.index(name)
                for b in range(4):
                    act.wait_ge(norm_t, 4 * i + b + 1)
                    for c in (2 * b, 2 * b + 1):
                        act.activation(dst[:, 0, c, :], PS[b][:, (c % 2) * S:(c % 2 + 1) * S], ACT.Copy,
                                       scale=gains[:, n, c:c + 1]).then_inc(norm_a, 1)

            def copy_bank(name, dst, width=512, rows=P, scale=1.0):
                full(name)
                src = bank(name)[0:rows, 0:width]
                if len(dst.shape) == 3:
                    src = src.rearrange("p (a b) -> p a b", a=dst.shape[1])
                act.activation(dst, src, ACT.Copy, scale=scale).then_inc(bank_freed["a"], 1)

            def copy_keys(name, dst):
                full(name)
                src = bank(name)[:, :].rearrange("p (a b) -> p a b", a=2)
                act.activation(dst[0:HD, 0:4:2, :], src[0:HD], ACT.Copy)
                act.activation(dst[HD:P, 1:4:2, :], src[HD:P], ACT.Copy).then_inc(bank_freed["a"], 1)

            def head_roots(k, group, hd, sq, st):
                for t in range(T):
                    wait_freed(act, group + (t,))
                act.activation(sq, hd, ACT.Square).then_inc(head_sq, 1)
                act.wait_ge(head_sum, k + 1)
                act.activation(st[1], st[0], ACT.Sqrt, bias=eps, scale=1.0 / HD).then_inc(head_root, 1)

            def attention(use):
                jobs, Sb, Pb, Tb = USES[use]
                j0, n = JOBS[use], len(jobs)
                for step in range(n + 2):
                    if step < n:
                        j = j0 + step
                        act.wait_ge(s_max, j + 1)
                        if step >= 3:
                            act.wait_ge(t_full, j - 2)
                        for t in range(T):
                            w = seen(use, t)
                            src = Sb[:, j % 2, t, 0:w] if Sb is not None else PS[j % 2][:, t * S:(t + 1) * S]
                            ins = act.activation(Pb[:, j % 3, t, 0:w], src, ACT.Exp, bias=att[:, 0, j % 4, t:t + 1],
                                                 scale=1.0 if Sb is None else -1.0, accum_out=att[:, 1, j % 4, t:t + 1])
                        ins.then_inc(s_exp, 1)
                    if step >= 2:
                        j = j0 + step - 2
                        act.wait_ge(t_full, j + 1)
                        if step >= 4:
                            act.wait_ge(y_full, j - 1)
                        n_out = P * len(turned_blocks(use))
                        act.activation(Tb[:, j % 2, :, :].rearrange("p a b -> p (a b)")[:, 0:n_out],
                                       PS[2 + j % 2][:, 0:n_out], ACT.Copy).then_inc(t_out, 1)
                    if (use, step - 3) == ("ab", A_HEADS):
                        for m in range(4):
                            copy_bank(("pct", m), pcT[0:N_CMP, 2 * m:2 * m + 2, :], rows=N_CMP)

            act.dma_start(smalls[:, 0:SMALL1], small[:, 0:SMALL1]).then_inc(in_small, 16)
            act.wait_ge(in_small, 16)
            norm_sums("norm1", X1, H1, lambda t: act.wait_ge(in_x[t], 16))
            split_to(3)
            norm_out("norm1", HT)
            for n in range(N_WIN):
                full(("win", n, 1))
                for dst, cols in win_parts(n, 1):
                    ins = act.activation(dst, bank(("win", n, 1))[:, cols], ACT.Copy)
                ins.then_inc(bank_freed["a"], 1)
                if n < 4:
                    head_roots(n, ("win", n), *head_block1(n))
            wait_freed(act, ("win", N_WIN - 1, 0))
            wait_freed(act, ("win", N_WIN - 1, 1))
            act.activation(gate3, projv[:, :, BG - NORMED:PROJ - NORMED], ACT.Sigmoid).then_inc(gate3_done, 1)

            act.wait_ge(in_more, 16)

            def merge_gates(gs):
                for g in gs:
                    full(("mg", g))
                    for c in range(2):
                        n = 2 * g + c
                        ins = act.activation(mgate[:, n % KD, n // KD, :], bank(("mg", g))[:, c * S:(c + 1) * S],
                                             ACT.Sigmoid, bias=smalls[:, BMERGE][:, n:n + 1])
                    ins.then_inc(bank_freed["a"], 1)

            merge_gates(range(4))
            split_to(units_to(("hid", 1)) + 3)
            for kv in range(2):
                wait_freed(act, ("hid", kv))
                act.activation(hid[0:2 * N_CMP, kv, :], hid[0:2 * N_CMP, kv, :], ACT.Gelu_apprx_tanh).then_inc(cmp_gelu, 1)
            merge_gates([4])
            merge_gates([5])
            split_to(units_to(("mg", 6)))
            act.wait_ge(cmp_sum, 1)
            act.activation(cst[0:N_CMP, 1, :], cst[0:N_CMP, 0, :], ACT.Sqrt, bias=eps[0:N_CMP], scale=1.0 / HD).then_inc(cmp_root, 1)
            merge_gates([6])
            merge_gates([7])
            for m in range(7):
                if m < 4:
                    copy_bank(("qkt", m), qkT[:, 2 * m:2 * m + 2, :], scale=HD ** -0.5)
                else:
                    copy_keys(("qkt", m), qkT[:, 8 + 4 * (m - 4):12 + 4 * (m - 4), :])
            act.wait_ge(cmp_less, 1)
            act.activation(scmp[:, :, 0:N_CMP], scmp[:, :, 0:N_CMP], ACT.Exp).then_inc(cmp_exp, 1)
            attention("ab")
            split_to(UNIT["out", 0] + 3)
            act.wait_ge(merged_done, KD)
            act.dma_start(memN[:, :, :], mem.rearrange(tokens_first, p=P)).then_inc(in_mem, 16)
            split_to(UNIT["out", 4])
            norm_sums("mem", memN, Hp, lambda t: act.wait_ge(in_mem, 16))
            split_to(units_to(("out",)) + 2)

            norm_sums("norm2", X1, Hp, after_wide("out"))
            split_to(units_to(("out",)) + 3)
            act.dma_start(park[0], X1[:, :, :].rearrange("p t d -> p (t d)")).then_inc(x_parked, 16)
            norm_out("norm2", HT)
            for m in range(8):
                hp, t = m // 2, m % 2
                if t == 0:
                    for g in (2 * hp, 2 * hp + 1):
                        copy_bank(("pq", g), pq[:, 2 * g:2 * g + 2, :])
                copy_bank(("sc", m), sc[:, t, 2 * hp:2 * hp + 2, :, :].rearrange("p h s n -> p (h s n)"))
            for i in range(DEPTH2):
                norm_out(f"mem{i}", memT)
                if i:
                    act.wait_ge(k_parked, 16)
                for g in range(4):
                    copy_bank(("xk", i, g), kout[:, 2 * g:2 * g + 2, :])
                wait_freed(act, ("xk", i, 3))
                act.dma_start(park[1 + 2 * i], kout[:, :, :].rearrange("p k s -> p (k s)")).then_inc(k_parked, 16)
                split_to(units_to(("xv", i)) + 3)
                if i:
                    act.wait_ge(gate_less, 1)
                    act.activation(tv[:, :, :, :], tv[:, :, :, :], ACT.Exp).then_inc(gate_exp, 1)
                    for t in range(T):
                        act.wait_ge(v_parked[t], 16)
                for t in range(T):
                    wait_wide_done(act, f"xv{i}", t)
                    for h in range(2):
                        act.activation(Hp[:, t, h * 512:(h + 1) * 512], PS[2 * t + h][:, :], ACT.Copy).then_inc(wide_out, 1)
            wait_first_units_used(act)
            for m in range(3):
                copy_bank(("et", m), eT[:, m, :], S)
            act.wait_ge(x_parked, 16)
            act.wait_ge(k_parked, 32)
            for t in range(T):
                act.wait_ge(v_parked[t], 32)
            wait_freed(act, ("et", 2))
            act.sem_inc(hot_out, BEGIN)

            def few_out(pair, i):
                at = i * 16 + (8 * pair + 3)
                src = eT[:, 1:3, at:at + 5] if isinstance(i, int) else eT[:, 1:3, bass.ds(at, 5)]
                act.activation(few[:, pair % 2, :, :], src, ACT.Copy).then_inc(few_made, 1)

            def gates_out(four, i):
                act.wait_ge(hot_full, i * 4 + (four + 1 + BEGIN))
                at = i * 16 + 4 * four
                to = gates[:, :, at:at + 4] if isinstance(i, int) else gates[:, :, bass.ds(at, 4)]
                act.activation(to.rearrange("p i t -> p t i"), PS[four % 2][:, :].rearrange("p (t i) -> p t i", t=4),
                               ACT.Copy).then_inc(hot_out, 1)

            few_out(0, 0)
            with act.Fori(0, S // 16 - 1) as i:
                for four in range(4):
                    if four % 2 == 0:
                        act.wait_ge(hot_full, i * 4 + (four + BEGIN))
                        few_out(four // 2 + 1, i)
                    gates_out(four, i)
            i = S // 16 - 1
            for four in range(4):
                if four == 0:
                    act.wait_ge(hot_full, i * 4 + BEGIN)
                    few_out(1, i)
                gates_out(four, i)
            act.wait_ge(hot_out, BEGIN + S // 4)

            def first_part(e, s, landed, turn, used, count, place, made):
                act.wait_ge(landed[s], turn)
                if count is not None:
                    act.wait_ge(used, count)
                act.activation(wsplit[:, place + s, 0, :], raw0[:, place + s, :], ACT.Copy).then_inc(made, 1)

            def gelu(e, s):
                act.wait_ge(a_full, e + 1)
                act.wait_ge(a_w, e + (BEGIN - 1))
                act.activation(act_e[:, s, :], PS[s][:, 0:S], ACT.Gelu_apprx_tanh).then_inc(a_gelu, 1)

            act.wait_ge(w_freed, FIRST2)
            first_part(0, 0, u_landed, 16, a_full, None, 0, u_hi)
            first_part(0, 0, v_landed, 16, a_v, None, 2, v_hi)
            first_part(1, 1, u_landed, 16, a_full, None, 0, u_hi)
            act.wait_ge(a_v, BEGIN)
            with act.Fori(0, NKEYS // 2 - 1) as i:
                for s in range(2):
                    e = i * 2 + s
                    gelu(e, s)
                    first_part(e + 2, s, u_landed, i * 16 + 32, a_full, i * 2 + (s + 1), 0, u_hi)
                    first_part(e + 1, 1 - s, v_landed, i * 16 + (16 if s == 0 else 32), a_v, i * 2 + (s + BEGIN), 2, v_hi)
            gelu(NKEYS - 2, 0)
            first_part(NKEYS - 1, 1, v_landed, 8 * NKEYS, a_v, NKEYS - 2 + BEGIN, 2, v_hi)
            gelu(NKEYS - 1, 1)

            limit[0] = len(UNITS)
            norm_sums("attn", X2, H2, after_wide("peer"))
            split_to(FIRST2 + 3)
            norm_out("attn", HT)
            for n in range(3):
                copy_bank(("qkv", n, 1), qkv[:, 1, 512 * n:512 * (n + 1)])
                head_roots(4 + n, ("qkv", n), *head_block2(n))
            for m in range(4):
                copy_bank(("qkt2", m), qkT2[:, 2 * m:2 * m + 2, :], scale=HD ** -0.5)
            copy_keys(("qkt2", 4), qkT2[:, 8:12, :])
            attention("self")
            split_to(units_to(("wo",)) + 2)
            for i in range(DEPTH2):
                if i:
                    norm_sums("pool", X2, H2, after_wide("ffd0"))
                    split_to(UNIT["pool", 0] + 3)
                    for g in range(4):
                        full(("pm", g))
                        for c in range(2):
                            ct = 2 * g + c
                            ins = act.activation(oT[:, 0, ct, :], bank(("pm", g))[:, c * S:(c + 1) * S], ACT.Copy,
                                                 scale=gains[:, GAINS_OF.index("pool"), ct:ct + 1])
                        ins.then_inc(pool_hi, 1)
                    split_to(units_to(("py", 0, 1)) + 3)
                norm_sums(f"x{i}", X2, H2, (lambda t: act.wait_ge(pool_done, 2 * (t + 1))) if i else after_wide("wo"))
                split_to(UNIT["xq", i, 0] + 3)
                norm_out(f"x{i}", HT)
                for g in range(4):
                    copy_bank(("xq", i, g), qxT[:, 2 * g:2 * g + 2, :], scale=X_HD ** -0.5)
                attention(f"x{i}")
                if i == 0:
                    act.wait_ge(y_full, JOBS["x1"])
                    act.dma_start(kv_in[:, :, :], park[3:5].rearrange("w p d -> p w d")).then_inc(in_kv, 16)
                split_to(units_to(("xo", i)) + 2)
                norm_sums(f"ffn{i}", X2, H2, after_wide(f"xo{i}"))
                split_to(units_to(("xo", i)) + 3)
                norm_out(f"ffn{i}", HT)
                for f in range(NF + 1):
                    if f < NF:
                        full(("ffu", i, f))
                        if f >= 2:
                            act.wait_ge(conv_m, NF * i + f - 1)
                        for c in range(2):
                            w = conv[:, i, c * NF + f, :]
                            ins = act.activation(cv[:, f % 2, c, :], bank(("ffu", i, f))[:, c * S:(c + 1) * S], ACT.Identity,
                                                 bias=w[:, 3:4], scale=w[:, 1:2])
                        ins.then_inc(conv_a, 1)
                    if f:
                        act.wait_ge(conv_d, NF * i + f)
                        g = (f - 1) % 2
                        act.activation(cv[:, g, 0, :], cv[:, g, 0, :], ACT.Silu).then_inc(conv_s, 1)
                split_to(units_to(("ffd", i)) + 2)
            norm_sums("final", X2, H2, after_wide("ffd1"))

        @block.vector
        def _(dve):
            links, split, limit = [0], [0], [CHOICE]

            def split_to(u1):
                for u in range(split[0], min(u1, limit[0])):
                    if u % 2 == 0:
                        dve.wait_ge(w_hi, u + 1)
                        dve.tensor_tensor(wsplit[:, u % NSPLIT, 1, :], sb_raw(u), f32(wsplit[:, u % NSPLIT, 0, :]),
                                          ALU.subtract).then_inc(w_lo_even, 1)
                    split[0] = u + 1

            def full(name):
                split_to(units_to(name) + 3)
                wait_full(dve, name)

            def link(ins):
                ins.then_inc(chain, 1)
                links[0] += 1
                dve.wait_ge(chain, links[0])

            def parts(hi, lo, src):
                link(dve.tensor_copy(hi, src))
                return dve.tensor_tensor(lo, src, f32(hi), ALU.subtract)

            def norm_scale(name, src, H):
                for t in range(T):
                    dve.wait_ge(norm_root, T * NORMS.index(name) + t + 1)
                    link(dve.reciprocal(stat[:, 4 + t:5 + t], stat[:, 2 + t:3 + t]))
                    dve.tensor_scalar(H[:, t, :], src[:, t, :], stat[:, 4 + t:5 + t], None, ALU.mult).then_inc(norm_h, 1)

            def norm_out(name, dst):
                split_to(units_of_turn(name))
                i, n = TURNS.index(name), GAINS_OF.index(name)
                for b in range(4):
                    dve.wait_ge(norm_a, KD * i + 2 * b + 2)
                    for c in (2 * b, 2 * b + 1):
                        dve.scalar_tensor_tensor(out=dst[:, 1, c, :], in0=PS[b][:, (c % 2) * S:(c % 2 + 1) * S],
                                                 scalar=gains[:, n, c:c + 1], in1=f32(dst[:, 0, c, :]), op0=ALU.mult,
                                                 op1=ALU.subtract).then_inc(norm_d, 1)

            def copy_bank(name, dst, src):
                full(name)
                dve.tensor_copy(dst, src).then_inc(bank_freed["d"], 1)

            def wide_read(name, dst):
                split_to(units_to(split_word(name)) + 2)
                for t in range(T):
                    wait_wide_done(dve, name, t)
                    for h in range(2):
                        o = dst[:, t, h * 512:(h + 1) * 512]
                        dve.tensor_tensor(o, o, PS[2 * t + h][:, :], ALU.add).then_inc(wide_out, 1)

            def head_norm(k, hd, sq, st, kinds, rope, ahead):
                n = hd.shape[2] // HD
                hv = hd.rearrange("p t (h d) -> p t h d", d=HD)
                dve.wait_ge(head_sq, k + 1)
                dve.tensor_reduce(st[0], sq.rearrange("p t (h d) -> p t h d", d=HD), AXX, ALU.add).then_inc(head_sum, 1)
                split_to(ahead + 4)
                dve.wait_ge(head_root, k + 1)
                link(dve.reciprocal(st[2], st[1]))
                link(dve.tensor_tensor(hv, hv, st[2].unsqueeze(3).to_broadcast([P, T, n, HD]), ALU.mult))
                at = 0
                for m, gain in kinds:
                    v = hv[:, :, at:at + m, :]
                    ins = dve.tensor_tensor(v, v, gain.unsqueeze(1).unsqueeze(1).to_broadcast([P, T, m, HD]), ALU.mult)
                    at += m
                link(ins)
                split_to(ahead + 5)
                rope(hv, n)

            def rotate(x1, x2, c, s, tmp):
                dve.tensor_tensor(tmp[0], x1, c, ALU.mult)
                dve.tensor_tensor(tmp[1], x2, s, ALU.mult)
                dve.tensor_tensor(tmp[2], x2, c, ALU.mult)
                link(dve.tensor_tensor(tmp[3], x1, s, ALU.mult))
                dve.tensor_tensor(x1, tmp[0], tmp[1], ALU.subtract)
                return dve.tensor_tensor(x2, tmp[2], tmp[3], ALU.add)

            def rope_first(hv, n):
                c, s = (rope1[:, w, :, :].unsqueeze(2).to_broadcast([P, T, n, 8]) for w in range(2))
                rotate(hv[:, :, :, 0:8], hv[:, :, :, 8:16], c, s,
                       [rtmp1[:, w, :, 0:n, :] for w in range(4)]).then_inc(head_done, 1)

            def rope_axial(hv, n):
                for t in range(T):
                    h2 = hv[:, t, :, :].rearrange("p h (a x j) -> p h a x j", a=2, x=2)
                    c, s = (rope2[:, w, t, :, :].unsqueeze(1).to_broadcast([P, n, 2, 16]) for w in range(2))
                    ins = rotate(h2[:, :, :, 0, :], h2[:, :, :, 1, :], c, s, [rtmp2[:, t, w, 0:n] for w in range(4)])
                ins.then_inc(head_done, 1)

            w = slice(0, N_CMP)
            sc3 = scmp[:, :, w]

            def compressed_softmax():
                dve.wait_ge(cmp_exp, 1)
                link(dve.tensor_reduce(cred[:, 1, :], sc3, AXX, ALU.add))
                link(dve.reciprocal(cred[:, 2, :], cred[:, 1, :]))
                r2 = cred[:, 2, :].rearrange("p (h t) -> p h t", t=T)
                link(dve.tensor_tensor(r2, r2, cany.unsqueeze(1).to_broadcast([P, 8, T]), ALU.mult))
                dve.wait_ge(gate3_done, 1)
                link(dve.tensor_tensor(r2, r2, gate3.rearrange("p t (h b) -> p h t b", b=3)[:, :, :, 0], ALU.mult))
                dve.tensor_tensor(sc3, sc3, cred[:, 2, :].unsqueeze(2).to_broadcast([P, 16, N_CMP]), ALU.mult).then_inc(cmp_prob, 1)

            def attention(use):
                jobs, Sb, Pb, Tb = USES[use]
                j0, n = JOBS[use], len(jobs)
                for step in range(n + 4):
                    if step < n:
                        j = j0 + step
                        dve.wait_ge(s_full, j + 1)
                        if step >= 2:
                            dve.wait_ge(s_exp, j - 1)
                        less = att[:, 0, j % 4, :]
                        b = PS[j % 2][:, :].rearrange("p (t n) -> p t n", t=T)
                        if Sb is not None:
                            for t in range(T):
                                w = seen(use, t)
                                ins = dve.tensor_tensor_reduce(Sb[:, j % 2, t, 0:w], b[:, t, 0:w], mask[:, t, 0:w], -1.0, -LOW,
                                                               ALU.add, ALU.min, less[:, t:t + 1])
                        else:
                            ins = dve.tensor_reduce(less, b, AXX, ALU.max, negate=True)
                        ins.then_inc(s_max, 1)
                    if 1 <= step <= n:
                        job, j = jobs[step - 1], j0 + step - 1
                        dve.wait_ge(s_exp, j + 1)
                        link(dve.reciprocal(att[:, 2, j % 4, :], att[:, 1, j % 4, :]))
                        for t in range(T):
                            r, p = att[:, 2, j % 4, t:t + 1], Pb[:, j % 3, t, 0:seen(use, t)]
                            if job["gate"] is None:
                                ins = dve.tensor_scalar(p, p, r, None, ALU.mult)
                            else:
                                ins = dve.tensor_scalar(p, p, r, job["gate"](t), ALU.mult, ALU.mult)
                        ins.then_inc(s_prob, 1)
                    if (use, step) == ("ab", 2):
                        compressed_softmax()
                    if step >= 4 and jobs[step - 4]["last"]:
                        job, j = jobs[step - 4], j0 + step - 4
                        dve.wait_ge(y_full, j + 1)
                        for d, dest in enumerate(job["dest"]):
                            ins = parts(dest[:, 0, :], dest[:, 1, :], bank(job["y"])[:, d * S:(d + 1) * S])
                        ins.then_inc(bank_freed["d"], 1)

            dve.wait_ge(in_small, 16)
            norm_scale("norm1", X1, H1)
            split_to(3)
            norm_out("norm1", HT)
            dve.wait_ge(in_more, 16)
            hg = smalls[:, HG1].rearrange("p (n d) -> p n d", n=5)
            kinds = [[(8, hg[:, 0, :])], [(8, hg[:, 1, :])], [(8, hg[:, 2, :])], [(2, hg[:, 3, :]), (2, hg[:, 4, :])]]
            for n in range(N_WIN):
                full(("win", n, 0))
                for dst, cols in win_parts(n, 0):
                    ins = dve.tensor_copy(dst, bank(("win", n, 0))[:, cols])
                ins.then_inc(bank_freed["d"], 1)
                if n < 4:
                    head_norm(n, *head_block1(n), kinds[n], rope_first, units_to(("win", n, 0)))
            dve.memset(qkT[HD:P, 8:20:2, :], 0.0)
            dve.memset(qkT[0:HD, 9:20:2, :], 0.0).then_inc(pads, 1)
            dve.wait_ge(in_layer1, 16)
            for kv in range(2):
                full(("win2", kv))
                for g in range(KV_HEADS):
                    for kh in range(2):
                        src = bank(("win2", kv))[:, g * P + 8 * kh:g * P + 8 * kh + 8 * N_CMP]
                        pos = cpos[:, kv, 8 * kh:8 * kh + 8].unsqueeze(2).to_broadcast([P, 8, N_CMP])
                        ins = dve.tensor_tensor(blocks[:, kv, 8 * kh:8 * kh + 8, g, :],
                                                src.rearrange("p (n k) -> p k n", k=8), pos, ALU.add)
                ins.then_inc(bank_freed["d"], 1)
                wait_freed(dve, ("win2", kv))
                parts(*(blocksT[:, part, kv, :, :, :].rearrange("p k g n -> p (k g n)") for part in range(2)),
                      blocks[:, kv, :, :, :].rearrange("p k g n -> p (k g n)")).then_inc(blocks_done, 1)
            for kv in range(2):
                full(("hid", kv))
                dve.tensor_tensor(hid[0:2 * N_CMP, kv, :], bank(("hid", kv))[0:2 * N_CMP, 0:CMP_HID],
                                  cb1[0:2 * N_CMP, kv, :], ALU.add).then_inc(bank_freed["d"], 1)
            split_to(units_to(("mg", 4)) + 3)
            for kv in range(2):
                copy_bank(("hidT", kv), hidT[:, kv, :, :],
                          bank(("hidT", kv))[:, 0:64].rearrange("p (k n) -> p k n", k=2)[:, :, 0:2 * N_CMP])
            split_to(units_to(("mg", 5)) + 3)
            for kv in range(2):
                full(("c2", kv))
                dve.tensor_tensor(kvc[w, kv, :, :], bank(("c2", kv))[w, 0:2 * HD].rearrange("p (g d) -> p g d", g=2),
                                  cb2[w, kv, :].unsqueeze(1).to_broadcast([N_CMP, 2, HD]), ALU.add).then_inc(bank_freed["d"], 1)
            wait_freed(dve, ("c2", 0))
            link(dve.tensor_tensor(ctmp[w, 0, :, :], kvc[w, 0, :, :], kvc[w, 0, :, :], ALU.mult))
            dve.tensor_reduce(cst[w, 0, :], ctmp[w, 0, :, :], AXX, ALU.add).then_inc(cmp_sum, 1)
            split_to(units_to(("mg", 6)) + 3)
            dve.wait_ge(cmp_root, 1)
            link(dve.reciprocal(cst[w, 2, :], cst[w, 1, :]))
            link(dve.tensor_tensor(kvc[w, 0, :, :], kvc[w, 0, :, :], cst[w, 2, :].unsqueeze(2).to_broadcast([N_CMP, 2, HD]),
                                   ALU.mult))
            dve.tensor_tensor(kvc[w, 0, :, :], kvc[w, 0, :, :], kcg[w].unsqueeze(1).to_broadcast([N_CMP, 2, HD]),
                              ALU.mult).then_inc(cmp_key, 1)
            copy_bank(("kcT",), kcT[:, 0:N_CMP], bank(("kcT",))[:, 0:N_CMP])
            split_to(units_to(("mg", 7)) + 3)
            sc4 = scmp[:, :, :].rearrange("p (h t) n -> p h t n", t=T)[:, :, :, w]
            for g in range(KV_HEADS):
                full(("scmp", g))
                src = bank(("scmp", g))[:, 0:4 * T * 16].rearrange("p (r t n) -> p r t n", r=4, t=T)[:, :, :, w]
                dve.tensor_tensor(sc4[:, 4 * g:4 * g + 4], src, cmask.unsqueeze(1).to_broadcast([P, 4, T, N_CMP]),
                                  ALU.add).then_inc(bank_freed["d"], 1)
            wait_freed(dve, ("scmp", 1))
            link(dve.tensor_reduce(cred[:, 0, :], sc3, AXX, ALU.max))
            dve.tensor_tensor(sc3, sc3, cred[:, 0, :].unsqueeze(2).to_broadcast([P, 16, N_CMP]), ALU.subtract)\
               .then_inc(cmp_less, 1)
            attention("ab")
            for f in range(KD):
                full(("up", f))
                tmp = uptmp[:, f % 2, :, :]
                dve.tensor_tensor(tmp, bank(("up", f))[:, :].rearrange("p (b n) -> p b n", b=2), mgate[:, f, :, :],
                                  ALU.mult).then_inc(bank_freed["d"], 1)
                wait_freed(dve, ("up", f))
                link(dve.tensor_tensor(tmp[:, 0, :], tmp[:, 0, :], tmp[:, 1, :], ALU.add))
                parts(merged[:, 0, f, :], merged[:, 1, f, :], tmp[:, 0, :]).then_inc(merged_done, 1)
            split_to(UNIT["out", 4])
            norm_scale("mem", memN, memN)
            wide_read("out", X1)

            norm_scale("norm2", X1, Hp)
            norm_out("norm2", HT)

            def pick_tables():
                link(dve.tensor_scalar(tab[:, 0, :, :], ti[:, :, :], 4, None, ALU.logical_shift_right))
                link(dve.tensor_scalar(tab[:, 1, :, :], ti[:, :, :], 15, None, ALU.bitwise_and))
                link(dve.tensor_copy(tabf[:, :, :, :], tab[:, :, :, :]))
                link(dve.tensor_copy(i16f[:, :, :, :, :], i16[:, :, :, :, :]))

            def pick(t, s):
                link(dve.tensor_tensor(onehot16[:, s, :, :], tabf[:, s, t, :].unsqueeze(2).to_broadcast([P, P, TOPK]),
                                       iota[:, 0:TOPK].unsqueeze(1).to_broadcast([P, P, TOPK]), ALU.is_equal))
                o4 = onehot16[:, s].rearrange("p (h k) j -> p h k j", h=PEER_HEADS)
                link(dve.tensor_tensor(o4, o4, i16f[:, t, :, s, :].unsqueeze(2).to_broadcast([P, PEER_HEADS, TOPK, TOPK]),
                                       ALU.mult))
                link(dve.tensor_reduce(ex[:, 1 - s, t, :], onehot16[:, s, :, :], AXX, ALU.add))

            def top16(values, spare, v, ix):
                link(dve.max(v[:, 0:8], values))
                dve.max_index(ix[:, 0:8], v[:, 0:8], values)
                link(dve.match_replace(spare, v[:, 0:8], values, LOW))
                link(dve.max(v[:, 8:16], spare))
                return dve.max_index(ix[:, 8:16], v[:, 8:16], spare)

            split_to(CHOICE)
            for m in range(8):
                wait_freed(dve, ("sc", m))
                t = m % 2
                for h in range(2 * (m // 2), 2 * (m // 2) + 2):
                    for s in range(2):
                        ins = top16(sc[:, t, h, s, :], srep[:, s, :], v16[:, t, h, s, :], i16[:, t, h, s, :])
                    link(ins)
                    link(dve.tensor_tensor(cand[:, 0, :, :], v16[:, t, h, 0, :].unsqueeze(2).to_broadcast([P, TOPK, TOPK]),
                                           v16[:, t, h, 1, :].unsqueeze(1).to_broadcast([P, TOPK, TOPK]), ALU.add))
                    link(top16(cand[:, 0, :, :].rearrange("p a b -> p (a b)"), cand[:, 1, :, :].rearrange("p a b -> p (a b)"),
                               tv[:, t, h, :], ti[:, t, h * TOPK:(h + 1) * TOPK]))
                    if (m, h % 2) == (3, 0):
                        norm_out("mem0", memT)
                    if (m, h % 2) == (6, 1):
                        norm_out("mem1", memT)
            link(dve.tensor_copy(gsum[:, 0, :, :], tv[:, :, :, 0]))
            dve.tensor_tensor(tv[:, :, :, :], tv[:, :, :, :], gsum[:, 0, :, :].unsqueeze(3).to_broadcast([P, T, 8, TOPK]),
                              ALU.subtract).then_inc(gate_less, 1)
            pick_tables()
            for t in range(T):
                for s in range(2):
                    pick(t, s)
            dve.wait_ge(gate_exp, 1)
            link(dve.tensor_reduce(gsum[:, 0, :, :], tv[:, :, :, :], AXX, ALU.add))
            link(dve.reciprocal(gsum[:, 1, :, :], gsum[:, 0, :, :]))
            dve.tensor_tensor(tv[:, :, :, :], tv[:, :, :, :], gsum[:, 1, :, :].unsqueeze(3).to_broadcast([P, T, 8, TOPK]),
                              ALU.mult).then_inc(ex_done, 1)
            wait_first_units_used(dve)
            wait_freed(dve, ("et", 2))
            with dve.Fori(0, S // 16) as i:
                for four in range(4):
                    dve.wait_ge(hot_full, i * 4 + (four - 1 + BEGIN))
                    dve.tensor_tensor(hots[:, four % 2, 0, :, :], iota.unsqueeze(1).to_broadcast([P, 4, NKEYS]),
                                      eT[:, 0, bass.ds(i * 16 + 4 * four, 4)].unsqueeze(2).to_broadcast([P, 4, NKEYS]),
                                      ALU.is_equal)
                    for j in range(4):
                        if j not in POOL_TOKENS[four % 2]:
                            n = i * 16 + (4 * four + j)
                            ins = dve.tensor_scalar(hots[:, four % 2, 1, j, :], iota, eT[:, 1, bass.ds(n, 1)],
                                                    eT[:, 2, bass.ds(n, 1)], ALU.is_equal, ALU.mult)
                    ins.then_inc(hot_by_d, 1)
            dve.memset(act_e[:, 0, :], 0.0).then_inc(a_w, BEGIN)

            def v_second_part(e, s):
                dve.wait_ge(v_hi, e + 1)
                dve.tensor_tensor(wsplit[:, 2 + s, 1, :], raw0[:, 2 + s, :], f32(wsplit[:, 2 + s, 0, :]),
                                  ALU.subtract).then_inc(v_lo, 1)

            def weigh(e, s):
                dve.wait_ge(a_gelu, e + 1)
                dve.wait_ge(a_v, e + (BEGIN - 1))
                g = gates[:, bass.ds(e, 1), :] if not isinstance(e, int) else gates[:, e:e + 1, :]
                dve.tensor_tensor(act_e[:, s, :].unsqueeze(1), act_e[:, s, :].unsqueeze(1), g, ALU.mult).then_inc(a_mul, 1)
                dve.wait_ge(a_mul, e + 1)
                dve.tensor_copy(wexp[:, s, 0, :], act_e[:, s, :]).then_inc(a_hi, 1)
                dve.wait_ge(a_hi, e + 1)
                dve.tensor_tensor(wexp[:, s, 1, :], act_e[:, s, :], f32(wexp[:, s, 0, :]), ALU.subtract).then_inc(a_w, 1)

            v_second_part(0, 0)
            with dve.Fori(0, NKEYS // 2 - 1) as i:
                for s in range(2):
                    weigh(i * 2 + s, s)
                    v_second_part(i * 2 + (s + 1), 1 - s)
            weigh(NKEYS - 2, 0)
            v_second_part(NKEYS - 1, 1)
            weigh(NKEYS - 1, 1)
            dve.wait_ge(in_x2, 16)
            for t in range(T):
                wait_wide_done(dve, "peer", t)
                for h in range(2):
                    o = X2[:, t, h * 512:(h + 1) * 512]
                    dve.tensor_tensor(o, o, PS[4 + 2 * t + h][:, :], ALU.add).then_inc(wide_out, 1)

            split[0], limit[0] = FIRST2, len(UNITS)
            wait_wide(dve, "peer")
            norm_scale("attn", X2, H2)
            split_to(FIRST2 + 3)
            norm_out("attn", HT)
            hg = smalls[:, HG2].rearrange("p (n d) -> p n d", n=2)
            for n in range(3):
                copy_bank(("qkv", n, 0), qkv[:, 0, 512 * n:512 * (n + 1)], bank(("qkv", n, 0))[:, :])
                head_norm(4 + n, *head_block2(n), [(8, hg[:, 0, :])] if n < 2 else [(N_KV, hg[:, 1, :])], rope_axial,
                          units_to(("qkv", n, 0)) - (2 if n == 2 else 0))
            dve.memset(qkT2[HD:P, 8:12:2, :], 0.0)
            dve.memset(qkT2[0:HD, 9:12:2, :], 0.0).then_inc(pads, 1)
            attention("self")
            wide_read("wo", X2)
            wait_wide(dve, "wo")
            for i in range(DEPTH2):
                if i:
                    norm_scale("pool", X2, H2)
                    for g in range(4):
                        dve.wait_ge(pool_hi, g + 1)
                        for c in range(2):
                            ct = 2 * g + c
                            ins = dve.scalar_tensor_tensor(
                                out=oT[:, 1, ct, :], in0=bank(("pm", g))[:, c * S:(c + 1) * S],
                                scalar=gains[:, GAINS_OF.index("pool"), ct:ct + 1], in1=f32(oT[:, 0, ct, :]),
                                op0=ALU.mult, op1=ALU.subtract).then_inc(pool_lo, 1)
                        dve.wait_ge(pool_lo, 2 * g + 2)
                        dve.sem_inc(bank_freed["d"], 1)
                    dve.wait_ge(in_wide, 16)
                    for t in range(T):
                        for g2 in range(2):
                            full(("py", t, g2))
                            cols = slice(g2 * 512, (g2 + 1) * 512)
                            tmp = ptmp[:, g2, :]
                            dve.tensor_tensor(tmp, bank(("py", t, g2))[:, :], wideg[:, 0, cols],
                                              ALU.mult).then_inc(bank_freed["d"], 1)
                            wait_freed(dve, ("py", t, g2))
                            dve.tensor_tensor(X2[:, t, cols], X2[:, t, cols], tmp, ALU.add).then_inc(pool_done, 1)
                norm_scale(f"x{i}", X2, H2)
                norm_out(f"x{i}", HT)
                split_to(units_to(("xq", i, 3)) + 3)
                attention(f"x{i}")
                wide_read(f"xo{i}", X2)
                norm_scale(f"ffn{i}", X2, H2)
                norm_out(f"ffn{i}", HT)
                for f in range(NF + 1):
                    if f < NF:
                        split_to(units_to(("ffu", i, f)) + 3)
                        dve.wait_ge(conv_a, NF * i + f + 1)
                        b = bank(("ffu", i, f))
                        for tap in (0, 2):
                            for c in range(2):
                                w = conv[:, i, c * NF + f, tap:tap + 1]
                                u = b[:, c * S:(c + 1) * S]
                                o, v = (slice(1, S), slice(0, S - 1)) if tap == 0 else (slice(0, S - 1), slice(1, S))
                                y = cv[:, f % 2, c, o]
                                ins = dve.scalar_tensor_tensor(out=y, in0=u[:, v], scalar=w, in1=y, op0=ALU.mult, op1=ALU.add)
                            if tap == 0:
                                link(ins)
                            else:
                                ins.then_inc(conv_d, 1)
                        dve.wait_ge(conv_d, NF * i + f + 1)
                        dve.sem_inc(bank_freed["d"], 1)
                    if f:
                        dve.wait_ge(conv_s, NF * i + f)
                        g = (f - 1) % 2
                        link(dve.tensor_tensor(cv[:, g, 0, :], cv[:, g, 0, :], cv[:, g, 1, :], ALU.mult))
                        parts(ff[:, 0, f - 1, :], ff[:, 1, f - 1, :], cv[:, g, 0, :]).then_inc(conv_m, 1)
                wide_read(f"ffd{i}", X2)
            dve.wait_ge(in_wide, 16)
            for t in range(T):
                dve.wait_ge(norm_root, T * NORMS.index("final") + t + 1)
                link(dve.reciprocal(stat[:, 4 + t:5 + t], stat[:, 2 + t:3 + t]))
                for h in range(2):
                    cols = slice(h * 512, (h + 1) * 512)
                    dve.scalar_tensor_tensor(out=H2[:, t, cols], in0=X2[:, t, cols], scalar=stat[:, 4 + t:5 + t],
                                             in1=wideg[:, 1, cols], op0=ALU.mult, op1=ALU.mult).then_inc(final_h, 1)


def pairs(w, axis, heads, kv):
    w = np.moveaxis(w, axis, 0)
    group = heads // kv
    w = w.reshape(kv // 2, 2, group, HD, -1).transpose(0, 2, 1, 3, 4).reshape(heads * HD, -1)
    return np.moveaxis(w, 0, axis)


def features(w):
    k, n = w.shape[0] // P, w.shape[1] // P
    return w.reshape(k, P, n, P).transpose(2, 1, 0, 3).reshape(n, P, k * P)


def rows(w, n, k):
    full = np.zeros((w.shape[0], n), np.float32)
    full[:, :w.shape[1]] = w
    return full.reshape(-1, k, P, n).transpose(0, 2, 1, 3).reshape(-1, P, k * n)


def weight_arrays(a):
    w_in = a["w_in"][0]
    at = np.cumsum([0, 512, 512, 512, 512, 128, 128, 128, 128, 128, 128, 24])
    aq, ak, av, bq, kc, vc, ks, vs, kw, vw, bg = (w_in[:, at[i]:at[i + 1]] for i in range(11))
    first = np.concatenate([aq, pairs(bq, 1, 8, 2), ak, ks, kw, av, vs, vw, kc, vc, bg], axis=1)
    out = {}

    def put(kind, units):
        for n, unit in enumerate(units):
            out[kind + (n,)] = unit

    for n in range(N_WIN):
        put(("win", n), rows(first[:, 512 * n:512 * n + 512], 512, 2))
    put(("mg",), features(w_in[:, at[11]:]))
    put(("wq",), features(a["peer_wq"][0]))
    for n, w in enumerate((a["cmp_k_w1"][0], a["cmp_v_w1"][0])):
        put(("cmp", n), rows(w, CMP_HID, 4))
    put(("up",), features(np.concatenate([a["w_up_a"][0], pairs(a["w_up_b"][0], 0, 8, 2)], axis=0)))
    put(("out",), rows(a["w_out"][0], D, 1))
    w = a["attn_w_qkv_2"][0]
    w = np.concatenate([pairs(w[:, :N_HEADS * HD], 1, N_HEADS, N_KV), w[:, N_HEADS * HD:]], axis=1)
    for n in range(3):
        put(("qkv", n), rows(w[:, 512 * n:512 * n + 512], 512, 2))
    put(("wo",), rows(pairs(a["attn_w_o_2"][0], 0, N_HEADS, N_KV), D, 1))
    put(("pool",), a["pool_w_2"][0].reshape(2, 4, P, S).transpose(0, 2, 1, 3).reshape(2, P, UNIT_COLS))
    for i in range(DEPTH2):
        put(("xk", i), features(a["xattn_w_kv_2"][i][:, :D]))
        put(("xv", i), rows(a["xattn_w_kv_2"][i][:, D:], D, 1))
        put(("xq", i), features(a["xattn_w_q_2"][i]))
        put(("xo", i), rows(a["xattn_w_o_2"][i], D, 1))
        put(("ffu", i), features(a["ffn_w_up_2"][i].reshape(D, 2, NF, P).transpose(0, 2, 1, 3).reshape(D, 2 * D_FF)))
        put(("ffd", i), rows(a["ffn_w_down_2"][i], D, 1))
    return out


def by_partition(v):
    return v.reshape(-1, P).T


def on_all(v):
    return np.broadcast_to(v.reshape(1, -1), (P, v.size))


def tables():
    pos = np.arange(S, dtype=np.float32)
    inv = np.float32(500000.0) ** (-np.arange(0, 16, 2, dtype=np.float32) / np.float32(16))
    ang = pos[:, None] * inv[None, :]
    rope1 = np.stack([np.cos(ang), np.sin(ang)]).reshape(2, T, P, 8).transpose(2, 0, 1, 3)
    inv = np.float32(10000.0) ** (-np.arange(16, dtype=np.float32) / np.float32(16))
    row, col = np.floor(pos / GRID_W).astype(np.float32), (pos % GRID_W).astype(np.float32)
    ang = np.stack([row[:, None] * inv, col[:, None] * inv], axis=1)
    rope2 = np.stack([np.cos(ang), np.sin(ang)]).reshape(2, T, P, 2, 16).transpose(2, 0, 1, 3, 4)
    tokens = np.arange(S)
    causal = np.where(tokens[None, :] <= tokens[:, None], 0.0, NEG).reshape(T, P, S).transpose(1, 0, 2)
    ends = np.arange(N_CMP) * CMP_STRIDE + CMP_LEN - 1
    seen = ends[None, :] <= tokens[:, None]
    cmask = np.where(seen, 0.0, NEG).reshape(T, P, N_CMP).transpose(1, 0, 2)
    some = seen.any(axis=1).astype(np.float32).reshape(T, P).T
    band = np.zeros((4, S, S), np.float32)
    for g, w in enumerate(POOL_WINDOWS):
        for t in range(S):
            lo, hi = max(t - w // 2, 0), min(t + w - w // 2, S)
            band[g, lo:hi, t] = 1.0 / (hi - lo)
            band[g, t, t] -= 1.0
    band = band.reshape(4, T, P, S).transpose(2, 0, 1, 3).reshape(P, 8, S)
    flat = lambda v: np.asarray(v, np.float32).reshape(P, -1)
    return flat(rope1), flat(rope2), flat(causal), flat(cmask), flat(some), np.ascontiguousarray(band)


def lay_out(a):
    rope1, rope2, causal, cmask, some, band = tables()
    units = weight_arrays(a)
    gain_of = {"norm1": a["norm1_g"][0], "norm2": a["norm2_g"][0], "attn": a["attn_norm_2"][0], "pool": a["pool_norm_2"][0]}
    for i in range(DEPTH2):
        gain_of.update({f"mem{i}": a["mem_norm_2"][i], f"x{i}": a["xattn_norm_2"][i], f"ffn{i}": a["ffn_norm_2"][i]})
    gains = [gain_of[n] for n in GAINS_OF]
    conv = np.stack([np.concatenate([a["ffn_conv_w_2"][i], a["ffn_conv_b_2"][i][None]]) for i in range(DEPTH2)])
    conv = conv.reshape(DEPTH2, 4, 2 * NF, P).transpose(3, 0, 2, 1).reshape(P, -1)
    small = np.concatenate(
        [np.eye(P, dtype=np.float32), np.full((P, 1), EPS, np.float32)] + [by_partition(g) for g in gains]
        + [on_all(np.arange(NKEYS, dtype=np.float32)), conv, by_partition(a["b_merge"][0].reshape(-1)), a["peer_k1"][0].T, a["peer_k2"][0].T,
           rope1, rope2]
        + [on_all(a[n][0]) for n in ("a_q_g", "b_q_g", "a_k_g", "b_ks_g", "b_kw_g", "attn_q_gain_2", "attn_k_gain_2")], axis=1)
    layer1 = np.concatenate(
        [causal, cmask, some] + [a[n][0].reshape(16, P).T for n in ("cmp_pos_k", "cmp_pos_v")]
        + [on_all(a[n][0]) for n in ("cmp_k_b1", "cmp_v_b1", "cmp_k_b2", "cmp_v_b2")]
        + [a[n][0].reshape(2, P, HD).transpose(1, 0, 2).reshape(P, -1) for n in ("cmp_k_w2", "cmp_v_w2")]
        + [on_all(a["b_kc_g"][0])], axis=1)
    assert small.shape[1] == SM.at and layer1.shape[1] == L1.at
    return {
        "x": a["x"], "mem": a["mem_2"],
        "weights": np.stack([units[name] for name in UNITS]),
        "expert_u": a["peer_u"][0].reshape(NKEYS, NKEYS, KD, P).transpose(0, 3, 2, 1).reshape(NKEYS, P, KD * NKEYS),
        "expert_v": a["peer_v"][0].reshape(NKEYS, NKEYS, D),
        "small": small, "layer1": layer1, "band": band,
        "wide_gains": np.broadcast_to(np.stack([a["pool_scale_2"][0], a["final_norm_2"]])[None], (P, 2, D)),
    }


def kernel(**inputs):
    import concourse.bacc as bacc
    from concourse.bass_utils import run_bass_kernel_spmd

    nc = bacc.Bacc("TRN2", target_bir_lowering=False, num_devices=1)
    arrays, args = {}, []
    for name, v in lay_out({k: np.asarray(v) for k, v in inputs.items()}).items():
        arrays[name] = np.ascontiguousarray(v)
        args.append(nc.dram_tensor(name, v.shape, F32, kind="ExternalInput").ap())
    args.append(nc.dram_tensor("result", (1, S, D), F32, kind="ExternalOutput").ap())
    block_stack(nc, *args)
    r = run_bass_kernel_spmd(nc, [arrays], core_ids=[0])
    return r.results[0]["result"]
```
